# Optimizing a Trainium2 kernel written in Bass

```python
import jax, jax.numpy as jnp
from jax import lax
import numpy as np
import math

D_MODEL = 1024
BATCH = 1
SEQ = 256
DEPTH = 2

HEAD_DIM = 64
ROT_DIM = HEAD_DIM // 4
ROPE_THETA = 500000.0
NORM_EPS = 1e-6
NEG_INF = -1e30

MOBA_HEADS = 8
MOBA_BLOCK = 256
MOBA_TOPK = 3
MOBA_Q_CHUNK = 32

NSA_HEADS = 8
NSA_KV_HEADS = 2
NSA_GROUP = NSA_HEADS // NSA_KV_HEADS
NSA_CMP_LEN = 32
NSA_CMP_STRIDE = 16
NSA_CMP_HIDDEN = 256
NSA_SEL_BLOCK = 64
NSA_SEL_TOPK = 16
NSA_WINDOW = 512
NSA_Q_CHUNK = 32
NSA_FORCE = 1e4

DIFF_HEADS = 8
DIFF_QK_DIM = HEAD_DIM
DIFF_V_DIM = 2 * HEAD_DIM
DIFF_Q_CHUNK = 128

FFN_HIDDEN = -(-8 * D_MODEL // (3 * 256)) * 256

MOBA_W = MOBA_HEADS * HEAD_DIM
NSA_Q_W = NSA_HEADS * HEAD_DIM
NSA_KV_W = 3 * 2 * NSA_KV_HEADS * HEAD_DIM
NSA_GATE_W = 3 * NSA_HEADS
SPARSE_IN = 3 * MOBA_W + NSA_Q_W + NSA_KV_W + NSA_GATE_W
SPARSE_SPLITS = [MOBA_W, 2 * MOBA_W, 3 * MOBA_W, 3 * MOBA_W + NSA_Q_W, 3 * MOBA_W + NSA_Q_W + NSA_KV_W]
SPARSE_OUT = MOBA_W + NSA_Q_W
DIFF_IN = 2 * DIFF_HEADS * 2 * DIFF_QK_DIM + DIFF_HEADS * DIFF_V_DIM
DIFF_OUT = DIFF_HEADS * DIFF_V_DIM


def rms_norm(t, gain):
    tf = t.astype(jnp.float32)
    y = tf * lax.rsqrt(jnp.mean(tf * tf, axis=-1, keepdims=True) + NORM_EPS)
    return (y * gain.astype(jnp.float32)).astype(t.dtype)

def rope_tables(positions):
    inv_freq = 1.0 / (ROPE_THETA ** (jnp.arange(0, ROT_DIM, 2, dtype=jnp.float32) / ROT_DIM))
    ang = positions.astype(jnp.float32)[:, None, :, None] * inv_freq
    return jnp.cos(ang), jnp.sin(ang)

def partial_rope(t, cos, sin):
    half = ROT_DIM // 2
    cos = cos.astype(t.dtype)
    sin = sin.astype(t.dtype)
    t1, t2, rest = t[..., :half], t[..., half:ROT_DIM], t[..., ROT_DIM:]
    return jnp.concatenate([t1 * cos - t2 * sin, t2 * cos + t1 * sin, rest], axis=-1)

def masked_softmax(s, valid):
    s = jnp.where(valid, s.astype(jnp.float32), NEG_INF)
    return jax.nn.softmax(s, axis=-1) * valid

def moba_attention(q, k, v):
    B, H, S, dh = q.shape
    Qc = MOBA_Q_CHUNK
    nb = -(-S // MOBA_BLOCK)
    pad = nb * MOBA_BLOCK - S
    kb = jnp.pad(k, ((0, 0), (0, 0), (0, pad), (0, 0))).reshape(B, H, nb, MOBA_BLOCK, dh)
    vb = jnp.pad(v, ((0, 0), (0, 0), (0, pad), (0, 0))).reshape(B, H, nb, MOBA_BLOCK, dh)
    kmean = jnp.mean(kb.astype(jnp.float32), axis=3)
    topk = min(MOBA_TOPK, nb)
    scale = dh ** -0.5
    bi = jnp.arange(B)[:, None, None, None]
    hi = jnp.arange(H)[None, :, None, None]
    blk = jnp.arange(nb)
    off = jnp.arange(MOBA_BLOCK)

    def one_chunk(ci):
        t0 = ci * Qc
        pos = t0 + jnp.arange(Qc)
        own = t0 // MOBA_BLOCK
        qc = lax.dynamic_slice_in_dim(q, t0, Qc, axis=2)
        gate = jnp.einsum('bhqd,bhnd->bhqn', qc.astype(jnp.float32), kmean)
        gate = jnp.where(blk < own, gate, NEG_INF)
        gval, idx = lax.top_k(gate, topk)
        sel_ok = gval > 0.5 * NEG_INF
        k_sel = kb[bi, hi, idx]
        v_sel = vb[bi, hi, idx]
        k_own = lax.dynamic_index_in_dim(kb, own, axis=2, keepdims=False)
        v_own = lax.dynamic_index_in_dim(vb, own, axis=2, keepdims=False)
        s_sel = jnp.einsum('bhqd,bhqnjd->bhqnj', qc, k_sel).reshape(B, H, Qc, topk * MOBA_BLOCK)
        s_own = jnp.einsum('bhqd,bhjd->bhqj', qc, k_own)
        ok_sel = jnp.broadcast_to(sel_ok[..., None], (B, H, Qc, topk, MOBA_BLOCK)).reshape(B, H, Qc, topk * MOBA_BLOCK)
        ok_own = jnp.broadcast_to((own * MOBA_BLOCK + off)[None, :] <= pos[:, None], (B, H, Qc, MOBA_BLOCK))
        p = masked_softmax(jnp.concatenate([s_sel, s_own], axis=-1) * scale,
                           jnp.concatenate([ok_sel, ok_own], axis=-1)).astype(v.dtype)
        p_sel = p[..., :topk * MOBA_BLOCK].reshape(B, H, Qc, topk, MOBA_BLOCK)
        p_own = p[..., topk * MOBA_BLOCK:]
        return (jnp.einsum('bhqnj,bhqnjd->bhqd', p_sel, v_sel)
                + jnp.einsum('bhqj,bhjd->bhqd', p_own, v_own))

    out = lax.map(one_chunk, jnp.arange(S // Qc))
    return out.transpose(1, 2, 0, 3, 4).reshape(B, H, S, dh)

def nsa_compress(t, pos_emb, w1, w2):
    S = t.shape[2]
    ncmp = (S - NSA_CMP_LEN) // NSA_CMP_STRIDE + 1
    idx = np.arange(ncmp)[:, None] * NSA_CMP_STRIDE + np.arange(NSA_CMP_LEN)[None, :]
    blocks = t[:, :, idx] + pos_emb
    hid = jax.nn.silu(jnp.einsum('bgnld,lde->bgne', blocks, w1))
    return jnp.einsum('bgne,ed->bgnd', hid, w2)

def nsa_overlap(ncmp, nsel):
    cs = np.arange(ncmp) * NSA_CMP_STRIDE
    ss = np.arange(nsel) * NSA_SEL_BLOCK
    ov = np.minimum(cs[:, None] + NSA_CMP_LEN, ss[None, :] + NSA_SEL_BLOCK) - np.maximum(cs[:, None], ss[None, :])
    return jnp.asarray(np.clip(ov, 0, None) / NSA_CMP_LEN, dtype=jnp.float32)

def nsa_attention(q, kc, vc, ks, vs, kw, vw, gates):
    B, H, S, dh = q.shape
    G, R, Qc, SB, W = NSA_KV_HEADS, NSA_GROUP, NSA_Q_CHUNK, NSA_SEL_BLOCK, NSA_WINDOW
    ncmp = kc.shape[2]
    nsel = S // SB
    topk = min(NSA_SEL_TOPK, nsel)
    scale = dh ** -0.5
    cmp_end = jnp.arange(ncmp) * NSA_CMP_STRIDE + NSA_CMP_LEN - 1
    overlap = nsa_overlap(ncmp, nsel)
    ksb = ks.reshape(B, G, nsel, SB, dh)
    vsb = vs.reshape(B, G, nsel, SB, dh)
    kwp = jnp.pad(kw, ((0, 0), (0, 0), (W, 0), (0, 0)))
    vwp = jnp.pad(vw, ((0, 0), (0, 0), (W, 0), (0, 0)))
    bi = jnp.arange(B)[:, None, None, None]
    gi = jnp.arange(G)[None, :, None, None]
    sel_blk = jnp.arange(nsel)
    sel_off = jnp.arange(SB)
    win_off = jnp.arange(W + Qc)

    def one_chunk(ci):
        t0 = ci * Qc
        pos = t0 + jnp.arange(Qc)
        qg = lax.dynamic_slice_in_dim(q, t0, Qc, axis=2).reshape(B, G, R, Qc, dh)
        g = lax.dynamic_slice_in_dim(gates, t0, Qc, axis=2).reshape(B, G, R, Qc, 3)
        ok_c = cmp_end[None, :] <= pos[:, None]
        p_c = masked_softmax(jnp.einsum('bgrqd,bgnd->bgrqn', qg, kc) * scale, ok_c)
        o_c = jnp.einsum('bgrqn,bgnd->bgrqd', p_c.astype(vc.dtype), vc)
        imp = jnp.einsum('bgqn,nm->bgqm', p_c.sum(axis=2), overlap)
        cur = pos // SB
        ok_blk = sel_blk[None, :] <= cur[:, None]
        forced = ok_blk & ((sel_blk[None, :] == 0) | (sel_blk[None, :] >= cur[:, None] - 1))
        score = jnp.where(ok_blk, jnp.where(forced, NSA_FORCE, imp), NEG_INF)
        sval, idx = lax.top_k(score, topk)
        sel_ok = sval > 0.5 * NEG_INF
        k_sel = ksb[bi, gi, idx]
        v_sel = vsb[bi, gi, idx]
        tok = idx[..., None] * SB + sel_off
        ok_s = (sel_ok[..., None] & (tok <= pos[None, None, :, None, None])).reshape(B, G, 1, Qc, topk * SB)
        s_s = jnp.einsum('bgrqd,bgqnjd->bgrqnj', qg, k_sel).reshape(B, G, R, Qc, topk * SB) * scale
        p_s = masked_softmax(s_s, ok_s).astype(vs.dtype).reshape(B, G, R, Qc, topk, SB)
        o_s = jnp.einsum('bgrqnj,bgqnjd->bgrqd', p_s, v_sel)
        k_w = lax.dynamic_slice_in_dim(kwp, t0, W + Qc, axis=2)
        v_w = lax.dynamic_slice_in_dim(vwp, t0, W + Qc, axis=2)
        kpos = t0 - W + win_off
        ok_w = (kpos[None, :] <= pos[:, None]) & (kpos[None, :] > pos[:, None] - W) & (kpos[None, :] >= 0)
        p_w = masked_softmax(jnp.einsum('bgrqd,bgkd->bgrqk', qg, k_w) * scale, ok_w)
        o_w = jnp.einsum('bgrqk,bgkd->bgrqd', p_w.astype(vw.dtype), v_w)
        o = g[..., 0:1] * o_c + g[..., 1:2] * o_s + g[..., 2:3] * o_w
        return o.reshape(B, H, Qc, dh)

    out = lax.map(one_chunk, jnp.arange(S // Qc))
    return out.transpose(1, 2, 0, 3, 4).reshape(B, H, S, dh)

def to_heads(t, n_heads):
    B, S, _ = t.shape
    return t.reshape(B, S, n_heads, HEAD_DIM).transpose(0, 2, 1, 3)

def qk_prep(t, gain, cos, sin):
    return partial_rope(rms_norm(t, gain), cos, sin)

def sparse_mixer(h, cos, sin, w_in, w_out, moba_qn, moba_kn, nsa_qn, nsa_kn, cmp_pos, cmp_w1, cmp_w2):
    B, S, _ = h.shape
    mq, mk, mv, nq, nkv, ng = jnp.split(h @ w_in, SPARSE_SPLITS, axis=-1)
    o_moba = moba_attention(qk_prep(to_heads(mq, MOBA_HEADS), moba_qn, cos, sin),
                            qk_prep(to_heads(mk, MOBA_HEADS), moba_kn, cos, sin),
                            to_heads(mv, MOBA_HEADS))
    kv = nkv.reshape(B, S, 3, 2, NSA_KV_HEADS, HEAD_DIM).transpose(2, 3, 0, 4, 1, 5)
    kc = nsa_compress(qk_prep(kv[0, 0], nsa_kn[0], cos, sin), cmp_pos[0], cmp_w1[0], cmp_w2[0])
    vc = nsa_compress(kv[0, 1], cmp_pos[1], cmp_w1[1], cmp_w2[1])
    gates = jax.nn.sigmoid(ng).reshape(B, S, 3, NSA_HEADS).transpose(0, 3, 1, 2)
    o_nsa = nsa_attention(qk_prep(to_heads(nq, NSA_HEADS), nsa_qn, cos, sin), kc, vc,
                          qk_prep(kv[1, 0], nsa_kn[1], cos, sin), kv[1, 1],
                          qk_prep(kv[2, 0], nsa_kn[2], cos, sin), kv[2, 1], gates)
    o = jnp.concatenate([o_moba, o_nsa], axis=1).transpose(0, 2, 1, 3).reshape(B, S, SPARSE_OUT)
    return o @ w_out

def diff_mixer(h, cos, sin, w_in, w_out, q_norm, k_norm, lam_params, out_norm, lam_init):
    B, S, _ = h.shape
    H, Qc = DIFF_HEADS, DIFF_Q_CHUNK
    qk_w = H * 2 * DIFF_QK_DIM
    q, k, v = jnp.split(h @ w_in, [qk_w, 2 * qk_w], axis=-1)
    cos5, sin5 = cos[:, :, None], sin[:, :, None]
    q = partial_rope(rms_norm(q.reshape(B, S, H, 2, DIFF_QK_DIM).transpose(0, 2, 3, 1, 4), q_norm), cos5, sin5)
    k = partial_rope(rms_norm(k.reshape(B, S, H, 2, DIFF_QK_DIM).transpose(0, 2, 3, 1, 4), k_norm), cos5, sin5)
    v = v.reshape(B, S, H, DIFF_V_DIM).transpose(0, 2, 1, 3)
    lp = lam_params.astype(jnp.float32)
    lam = jnp.exp(jnp.sum(lp[0] * lp[1])) - jnp.exp(jnp.sum(lp[2] * lp[3])) + lam_init
    scale = DIFF_QK_DIM ** -0.5
    key_idx = jnp.arange(S)

    def one_chunk(ci):
        t0 = ci * Qc
        pos = t0 + jnp.arange(Qc)
        qc = lax.dynamic_slice_in_dim(q, t0, Qc, axis=3)
        s = jnp.einsum('bhcqd,bhckd->bhcqk', qc, k) * scale
        p = masked_softmax(s, key_idx[None, :] <= pos[:, None])
        a = p[:, :, 0] - lam * p[:, :, 1]
        return jnp.einsum('bhqk,bhkd->bhqd', a.astype(v.dtype), v)

    o = lax.map(one_chunk, jnp.arange(S // Qc)).transpose(1, 2, 0, 3, 4).reshape(B, H, S, DIFF_V_DIM)
    o = rms_norm(o, out_norm) * (1.0 - lam_init)
    return o.transpose(0, 2, 1, 3).reshape(B, S, DIFF_OUT) @ w_out

def swiglu(h, w_gate, w_up, w_down):
    return (jax.nn.silu(h @ w_gate) * (h @ w_up)) @ w_down

def first_inputs(seed: int = 0) -> dict:
    key = jax.random.key(seed)
    keys = iter(jax.random.split(key, 40))
    n_even = (DEPTH + 1) // 2
    n_odd = DEPTH // 2

    def nrm(shape, scale):
        return jax.random.normal(next(keys), shape, jnp.float32) * scale

    def gain(shape):
        return 1.0 + nrm(shape, 0.05)

    offsets = jax.random.randint(next(keys), (BATCH, 1), 0, 1024, dtype=jnp.int32)
    positions = offsets + jnp.arange(SEQ, dtype=jnp.int32)[None, :]
    return {
        'x': nrm((BATCH, SEQ, D_MODEL), 1.0),
        'c': nrm((BATCH, D_MODEL), 1.0),
        'positions': positions,
        'ada_w': nrm((DEPTH, D_MODEL, 6 * D_MODEL), 0.5 * D_MODEL ** -0.5),
        'ada_b': nrm((DEPTH, 6 * D_MODEL), 0.02),
        'attn_norm': gain((DEPTH, D_MODEL)),
        'ffn_norm': gain((DEPTH, D_MODEL)),
        'ffn_w_gate': nrm((DEPTH, D_MODEL, FFN_HIDDEN), D_MODEL ** -0.5),
        'ffn_w_up': nrm((DEPTH, D_MODEL, FFN_HIDDEN), D_MODEL ** -0.5),
        'ffn_w_down': nrm((DEPTH, FFN_HIDDEN, D_MODEL), FFN_HIDDEN ** -0.5),
        'sp_w_in': nrm((n_even, D_MODEL, SPARSE_IN), D_MODEL ** -0.5),
        'sp_w_out': nrm((n_even, SPARSE_OUT, D_MODEL), SPARSE_OUT ** -0.5),
        'moba_q_norm': gain((n_even, HEAD_DIM)),
        'moba_k_norm': gain((n_even, HEAD_DIM)),
        'nsa_q_norm': gain((n_even, HEAD_DIM)),
        'nsa_k_norm': gain((n_even, 3, HEAD_DIM)),
        'nsa_cmp_pos': nrm((n_even, 2, NSA_CMP_LEN, HEAD_DIM), 0.1),
        'nsa_cmp_w1': nrm((n_even, 2, NSA_CMP_LEN, HEAD_DIM, NSA_CMP_HIDDEN), (NSA_CMP_LEN * HEAD_DIM) ** -0.5),
        'nsa_cmp_w2': nrm((n_even, 2, NSA_CMP_HIDDEN, HEAD_DIM), NSA_CMP_HIDDEN ** -0.5),
        'diff_w_in': nrm((n_odd, D_MODEL, DIFF_IN), D_MODEL ** -0.5),
        'diff_w_out': nrm((n_odd, DIFF_OUT, D_MODEL), DIFF_OUT ** -0.5),
        'diff_q_norm': gain((n_odd, DIFF_QK_DIM)),
        'diff_k_norm': gain((n_odd, DIFF_QK_DIM)),
        'diff_lambda': nrm((n_odd, 4, DIFF_QK_DIM), 0.1),
        'diff_out_norm': gain((n_odd, DIFF_V_DIM)),
    }

def first_block(x, c, positions, ada_w, ada_b, attn_norm, ffn_norm, ffn_w_gate, ffn_w_up, ffn_w_down,
              sp_w_in, sp_w_out, moba_q_norm, moba_k_norm, nsa_q_norm, nsa_k_norm, nsa_cmp_pos,
              nsa_cmp_w1, nsa_cmp_w2, diff_w_in, diff_w_out, diff_q_norm, diff_k_norm, diff_lambda,
              diff_out_norm):
    cos, sin = rope_tables(positions)
    for i in range(DEPTH):
        mod = jax.nn.silu(c) @ ada_w[i] + ada_b[i]
        sh_a, sc_a, g_a, sh_f, sc_f, g_f = jnp.split(mod[:, None, :], 6, axis=-1)
        h = rms_norm(x, attn_norm[i]) * (1.0 + sc_a) + sh_a
        j = i // 2
        if i % 2 == 0:
            y = sparse_mixer(h, cos, sin, sp_w_in[j], sp_w_out[j], moba_q_norm[j], moba_k_norm[j],
                             nsa_q_norm[j], nsa_k_norm[j], nsa_cmp_pos[j], nsa_cmp_w1[j], nsa_cmp_w2[j])
        else:
            lam_init = 0.8 - 0.6 * float(np.exp(-0.3 * i))
            y = diff_mixer(h, cos, sin, diff_w_in[j], diff_w_out[j], diff_q_norm[j], diff_k_norm[j],
                           diff_lambda[j], diff_out_norm[j], lam_init)
        x = x + g_a * y
        h = rms_norm(x, ffn_norm[i]) * (1.0 + sc_f) + sh_f
        x = x + g_f * swiglu(h, ffn_w_gate[i], ffn_w_up[i], ffn_w_down[i])
    return x


GRID_W = 64
CTX_LEN = 256

MIX_W = D_MODEL
POOL_W = MIX_W // 2
POOL_GROUPS = 4
POOL_WINDOWS = (2, 4, 8, 16)
POOL_GC = POOL_W // POOL_GROUPS
MLA_HEADS = 8
QK_NOPE = 64
QK_ROPE = 32
V_HEAD = 64
Q_LORA = D_MODEL // 4
KV_LORA = D_MODEL // 4
IN_W = POOL_W + Q_LORA + KV_LORA + QK_ROPE
ROPE_AXIS = QK_ROPE // 2
ROPE_BASE = 10000.0
Q_BLOCK = 128
D_FF = 2816
N_EXPERTS = 8
TOP_K = 2
D_FF_EXPERT = 3584
HY_WIDTH = D_MODEL
HY_SHORT = 3
HY_BANDS = 16
HY_EMB = 1 + 2 * HY_BANDS
HY_FILTER_HIDDEN = 64
HY_FAST_DECAY = 0.3
HY_SLOW_DECAY = 1.5
HY_TARGET = 1e-2
HY_MIN_DECAY = math.log(HY_TARGET) / HY_SLOW_DECAY
HY_MAX_DECAY = math.log(HY_TARGET) / HY_FAST_DECAY
LN_EPS = 1e-5
RMS_EPS = 1e-6


def layer_norm(x, g, b):
    xf = x.astype(jnp.float32)
    mu = jnp.mean(xf, axis=-1, keepdims=True)
    var = jnp.mean(jnp.square(xf - mu), axis=-1, keepdims=True)
    return ((xf - mu) * lax.rsqrt(var + LN_EPS) * g.astype(jnp.float32) + b.astype(jnp.float32)).astype(x.dtype)

def rms_norm_2(x, g):
    xf = x.astype(jnp.float32)
    return (xf * lax.rsqrt(jnp.mean(jnp.square(xf), axis=-1, keepdims=True) + RMS_EPS) * g.astype(jnp.float32)).astype(x.dtype)

def ada_chunks(s, w, b, k):
    mod = s @ w[:, :k * D_MODEL] + b[:k * D_MODEL]
    return [m[:, None, :] for m in jnp.split(mod, k, axis=-1)]

def axial_angles(n):
    rows = n // GRID_W
    r = jnp.repeat(jnp.arange(rows, dtype=jnp.float32), GRID_W)
    col = jnp.tile(jnp.arange(GRID_W, dtype=jnp.float32), rows)
    inv = ROPE_BASE ** (-jnp.arange(0, ROPE_AXIS, 2, dtype=jnp.float32) / ROPE_AXIS)
    return r[:, None] * inv, col[:, None] * inv

def rotate_pairs(x, ang):
    half = x.shape[-1] // 2
    x1, x2 = x[..., :half], x[..., half:]
    cos = jnp.cos(ang).astype(x.dtype)
    sin = jnp.sin(ang).astype(x.dtype)
    return jnp.concatenate([x1 * cos - x2 * sin, x2 * cos + x1 * sin], axis=-1)

def axial_rope(x, ang_r, ang_c):
    return jnp.concatenate([rotate_pairs(x[..., :ROPE_AXIS], ang_r), rotate_pairs(x[..., ROPE_AXIS:], ang_c)], axis=-1)

def multiscale_pool(u, pool_w, pool_scale):
    b, n, _ = u.shape
    ug = u.reshape(b, n, POOL_GROUPS, POOL_GC)
    cs = jnp.cumsum(ug.astype(jnp.float32), axis=1)
    cs = jnp.concatenate([jnp.zeros((b, 1, POOL_GROUPS, POOL_GC), jnp.float32), cs], axis=1)
    t = jnp.arange(n)[:, None]
    half = jnp.array([w // 2 for w in POOL_WINDOWS], dtype=jnp.int32)[None, :]
    lo = jnp.clip(t - half, 0, n)
    hi = jnp.clip(t + half, 0, n)
    grp = jnp.arange(POOL_GROUPS)[None, :]
    win_sum = cs[:, hi, grp] - cs[:, lo, grp]
    mean = win_sum / (hi - lo).astype(jnp.float32)[None, :, :, None]
    d = (mean - ug.astype(jnp.float32)).astype(u.dtype)
    y = jnp.einsum('bngc,gcd->bngd', d, pool_w)
    return y.reshape(b, n, POOL_W) * pool_scale

def mla_queries(q_lat, q_norm, q_up, ang):
    b, n, _ = q_lat.shape
    q = (rms_norm_2(q_lat, q_norm) @ q_up).reshape(b, n, MLA_HEADS, QK_NOPE + QK_ROPE)
    q_nope, q_rope = q[..., :QK_NOPE], q[..., QK_NOPE:]
    if ang is not None:
        q_rope = axial_rope(q_rope, ang[0][:, None, :], ang[1][:, None, :])
    return jnp.concatenate([q_nope, q_rope], axis=-1) * (QK_NOPE + QK_ROPE) ** -0.5

def mla_keys_values(kv_in, kv_norm, kv_up, ang):
    b, n, _ = kv_in.shape
    kv_lat, k_rope = kv_in[..., :KV_LORA], kv_in[..., KV_LORA:]
    kv = (rms_norm_2(kv_lat, kv_norm) @ kv_up).reshape(b, n, MLA_HEADS, QK_NOPE + V_HEAD)
    k_nope, v = kv[..., :QK_NOPE], kv[..., QK_NOPE:]
    if ang is not None:
        k_rope = axial_rope(k_rope, ang[0], ang[1])
    k = jnp.concatenate([k_nope, jnp.broadcast_to(k_rope[:, :, None, :], (b, n, MLA_HEADS, QK_ROPE))], axis=-1)
    return k, v

def attend(q, k, v):
    s = jnp.einsum('bqhd,bkhd->bhqk', q, k).astype(jnp.float32)
    p = jax.nn.softmax(s, axis=-1).astype(v.dtype)
    return jnp.einsum('bhqk,bkhd->bqhd', p, v)

def blocked_attend(q, k, v):
    b, n, h, d = q.shape
    qb = q.reshape(b, n // Q_BLOCK, Q_BLOCK, h, d).transpose(1, 0, 2, 3, 4)
    o = lax.map(lambda qq: attend(qq, k, v), qb)
    return o.transpose(1, 0, 2, 3, 4).reshape(b, n, h, V_HEAD)

def pool_mla_mixer(u, u_ctx, ctx_out, ang, in_w, pool_w, pool_scale, q_norm, q_up, kv_norm, kv_up, out_w):
    b, n, _ = u.shape
    kv0 = POOL_W + Q_LORA
    proj = u @ in_w
    if ctx_out:
        proj_c = u_ctx @ in_w
        kv_c_in = proj_c[..., kv0:]
    else:
        kv_c_in = u_ctx @ in_w[:, kv0:]
    k_c, v_c = mla_keys_values(kv_c_in, kv_norm, kv_up, None)
    k_l, v_l = mla_keys_values(proj[..., kv0:], kv_norm, kv_up, ang)
    q_l = mla_queries(proj[..., POOL_W:kv0], q_norm, q_up, ang)
    o_l = blocked_attend(q_l, jnp.concatenate([k_c, k_l], axis=1), jnp.concatenate([v_c, v_l], axis=1))
    y_l = jnp.concatenate([multiscale_pool(proj[..., :POOL_W], pool_w, pool_scale), o_l.reshape(b, n, MLA_HEADS * V_HEAD)], axis=-1) @ out_w
    y_c = None
    if ctx_out:
        m = u_ctx.shape[1]
        q_c = mla_queries(proj_c[..., POOL_W:kv0], q_norm, q_up, None)
        o_c = attend(q_c, k_c, v_c)
        y_c = jnp.concatenate([multiscale_pool(proj_c[..., :POOL_W], pool_w, pool_scale), o_c.reshape(b, m, MLA_HEADS * V_HEAD)], axis=-1) @ out_w
    return y_l, y_c

def short_conv(z, w, bias):
    y = lax.conv_general_dilated(z, w[:, None, :], window_strides=(1,), padding=[(HY_SHORT // 2, HY_SHORT // 2)],
                                 dimension_numbers=('NWC', 'WIO', 'NWC'), feature_group_count=z.shape[-1])
    return y + bias

def hyena_filters(n, fw1, fb1, fw2, fb2, fw3, fb3, fout, freq):
    t = jnp.linspace(0.0, 1.0, n, dtype=jnp.float32)[:, None]
    w_ang = (2.0 * math.pi / n) * jnp.arange(n, dtype=jnp.float32)[:, None]
    bands = jnp.linspace(1e-4, HY_BANDS - 1, HY_BANDS, dtype=jnp.float32)[None, :]
    z = jnp.concatenate([t, jnp.cos(bands * w_ang), -jnp.sin(bands * w_ang)], axis=-1)
    freq = freq.astype(jnp.float32)
    h = jnp.sin(freq * (z @ fw1.astype(jnp.float32) + fb1.astype(jnp.float32)))
    h = jnp.sin(freq * (h @ fw2.astype(jnp.float32) + fb2.astype(jnp.float32)))
    h = jnp.sin(freq * (h @ fw3.astype(jnp.float32) + fb3.astype(jnp.float32)))
    h = (h @ fout.astype(jnp.float32)).reshape(n, 2, HY_WIDTH)
    deltas = jnp.abs(jnp.linspace(HY_MIN_DECAY, HY_MAX_DECAY, HY_WIDTH, dtype=jnp.float32))
    h = h * jnp.exp(-t * deltas)[:, None, :]
    return h[:, 0], h[:, 1]

def bidir_long_conv(v, h_f, h_b, skip):
    b, n, ch = v.shape
    vf = v.astype(jnp.float32)
    k = jnp.concatenate([h_f, jnp.zeros((1, ch), jnp.float32), jnp.flip(h_b[1:], axis=0)], axis=0)
    spec = jnp.fft.rfft(vf, n=2 * n, axis=1) * jnp.fft.rfft(k, n=2 * n, axis=0)[None]
    y = jnp.fft.irfft(spec, n=2 * n, axis=1)[:, :n]
    return (y + vf * skip.astype(jnp.float32)).astype(v.dtype)

def hyena_mixer(u, in_w, conv_w, conv_b, fw1, fb1, fw2, fb2, fw3, fb3, fout, freq, skip, out_w):
    n = u.shape[1]
    z = short_conv(u @ in_w, conv_w, conv_b)
    x0, x1, v = jnp.split(z, 3, axis=-1)
    h_f, h_b = hyena_filters(n, fw1, fb1, fw2, fb2, fw3, fb3, fout, freq)
    y = x0 * bidir_long_conv(v * x1, h_f, h_b, skip)
    return y @ out_w

def swiglu_2(h, wg, wu, wd):
    return (jax.nn.silu(h @ wg) * (h @ wu)) @ wd

def moe_swiglu(h, router_w, wg, wu, wd):
    shp = h.shape
    t = h.reshape(-1, shp[-1])
    logits = (t @ router_w).astype(jnp.float32)
    top_v, top_i = lax.top_k(logits, TOP_K)
    gates = jax.nn.softmax(top_v, axis=-1)
    combine = jnp.sum(jax.nn.one_hot(top_i, N_EXPERTS, dtype=jnp.float32) * gates[..., None], axis=1).astype(h.dtype)
    out = jnp.zeros_like(t)
    for e in range(N_EXPERTS):
        out = out + combine[:, e:e + 1] * swiglu_2(t, wg[e], wu[e], wd[e])
    return out.reshape(shp)

def second_inputs(seed: int = 0) -> dict:
    key = jax.random.key(seed)
    keys = jax.random.split(key, 48)
    counter = [0]

    def nrm(shape, scale):
        k = keys[counter[0]]
        counter[0] += 1
        return jax.random.normal(k, shape, jnp.float32) * scale

    D = D_MODEL
    ne = (DEPTH + 1) // 2
    no = DEPTH // 2
    beta = (8.0 * DEPTH) ** -0.25
    fh = HY_FILTER_HIDDEN
    return {
        'x': nrm((BATCH, SEQ, D), 1.0),
        'c': nrm((BATCH, D), 1.0),
        'ctx': nrm((BATCH, CTX_LEN, D), 1.0),
        'c_ctx': nrm((D,), 1.0),
        'ada_w': nrm((DEPTH, D, 6 * D), 0.5 * D ** -0.5),
        'ada_b': nrm((DEPTH, 6 * D), 0.02),
        'ln_g': 1.0 + nrm((DEPTH, 2, D), 0.02),
        'ln_b': nrm((DEPTH, 2, D), 0.02),
        'mix_in_w': nrm((ne, D, IN_W), D ** -0.5),
        'pool_w': nrm((ne, POOL_GROUPS, POOL_GC, POOL_GC), POOL_GC ** -0.5),
        'pool_scale': 1.0 + nrm((ne, POOL_W), 0.02),
        'q_norm': 1.0 + nrm((ne, Q_LORA), 0.02),
        'q_up': nrm((ne, Q_LORA, MLA_HEADS * (QK_NOPE + QK_ROPE)), Q_LORA ** -0.5),
        'kv_norm': 1.0 + nrm((ne, KV_LORA), 0.02),
        'kv_up': nrm((ne, KV_LORA, MLA_HEADS * (QK_NOPE + V_HEAD)), KV_LORA ** -0.5),
        'mix_out_w': nrm((ne, MIX_W, D), beta * MIX_W ** -0.5),
        'ffn_gate': nrm((ne, D, D_FF), D ** -0.5),
        'ffn_up': nrm((ne, D, D_FF), D ** -0.5),
        'ffn_down': nrm((ne, D_FF, D), beta * D_FF ** -0.5),
        'hy_in_w': nrm((no, D, 3 * HY_WIDTH), D ** -0.5),
        'hy_conv_w': nrm((no, HY_SHORT, 3 * HY_WIDTH), HY_SHORT ** -0.5),
        'hy_conv_b': nrm((no, 3 * HY_WIDTH), 0.02),
        'hy_fw1': nrm((no, HY_EMB, fh), HY_EMB ** -0.5),
        'hy_fb1': nrm((no, fh), 0.1),
        'hy_fw2': nrm((no, fh, fh), fh ** -0.5),
        'hy_fb2': nrm((no, fh), 0.1),
        'hy_fw3': nrm((no, fh, fh), fh ** -0.5),
        'hy_fb3': nrm((no, fh), 0.1),
        'hy_fout': nrm((no, fh, 2 * HY_WIDTH), 0.1 * fh ** -0.5),
        'hy_freq': 1.0 + nrm((no, fh), 0.02),
        'hy_skip': nrm((no, HY_WIDTH), 1.0),
        'hy_out_w': nrm((no, HY_WIDTH, D), beta * HY_WIDTH ** -0.5),
        'router_w': nrm((no, D, N_EXPERTS), D ** -0.5),
        'moe_gate': nrm((no, N_EXPERTS, D, D_FF_EXPERT), D ** -0.5),
        'moe_up': nrm((no, N_EXPERTS, D, D_FF_EXPERT), D ** -0.5),
        'moe_down': nrm((no, N_EXPERTS, D_FF_EXPERT, D), beta * D_FF_EXPERT ** -0.5),
    }

def second_block(x, c, ctx, c_ctx, ada_w, ada_b, ln_g, ln_b, mix_in_w, pool_w, pool_scale, q_norm, q_up, kv_norm, kv_up,
              mix_out_w, ffn_gate, ffn_up, ffn_down, hy_in_w, hy_conv_w, hy_conv_b, hy_fw1, hy_fb1, hy_fw2, hy_fb2,
              hy_fw3, hy_fb3, hy_fout, hy_freq, hy_skip, hy_out_w, router_w, moe_gate, moe_up, moe_down):
    alpha = (2.0 * DEPTH) ** 0.25
    n = x.shape[1]
    ang = axial_angles(n)
    s_lat = jax.nn.silu(c)
    s_ctx = jax.nn.silu(c_ctx)[None, :]
    last_reader = (DEPTH - 1) - ((DEPTH - 1) % 2)
    h, hc = x, ctx
    for l in range(DEPTH):
        i = l // 2
        even = (l % 2 == 0)
        ctx_live = l <= last_reader
        ctx_out = l < last_reader
        sh1, sc1, g1, sh2, sc2, g2 = ada_chunks(s_lat, ada_w[l], ada_b[l], 6)
        u = h * (1 + sc1) + sh1
        uc, mc = None, None
        if ctx_live:
            mc = ada_chunks(s_ctx, ada_w[l], ada_b[l], 6 if ctx_out else 2)
            uc = hc * (1 + mc[1]) + mc[0]
        if even:
            y, yc = pool_mla_mixer(u, uc, ctx_out, ang, mix_in_w[i], pool_w[i], pool_scale[i], q_norm[i], q_up[i],
                                   kv_norm[i], kv_up[i], mix_out_w[i])
        else:
            hy_args = (hy_in_w[i], hy_conv_w[i], hy_conv_b[i], hy_fw1[i], hy_fb1[i], hy_fw2[i], hy_fb2[i],
                       hy_fw3[i], hy_fb3[i], hy_fout[i], hy_freq[i], hy_skip[i], hy_out_w[i])
            y = hyena_mixer(u, *hy_args)
            yc = hyena_mixer(uc, *hy_args) if ctx_out else None

        def channel_mix(z):
            if even:
                return swiglu_2(z, ffn_gate[i], ffn_up[i], ffn_down[i])
            return moe_swiglu(z, router_w[i], moe_gate[i], moe_up[i], moe_down[i])

        h = layer_norm(alpha * h + g1 * y, ln_g[l, 0], ln_b[l, 0])
        h = layer_norm(alpha * h + g2 * channel_mix(h * (1 + sc2) + sh2), ln_g[l, 1], ln_b[l, 1])
        if ctx_out:
            hc = layer_norm(alpha * hc + mc[2] * yc, ln_g[l, 0], ln_b[l, 0])
            hc = layer_norm(alpha * hc + mc[5] * channel_mix(hc * (1 + mc[4]) + mc[3]), ln_g[l, 1], ln_b[l, 1])
    return h


def setup_inputs(seed=0):
    out = dict(first_inputs(seed))
    for name, value in second_inputs(seed + 1).items():
        if name != "x":
            out[name + "_2"] = value
    return out


def reference(
    x, c, positions, ada_w, ada_b, attn_norm, ffn_norm, ffn_w_gate, ffn_w_up, ffn_w_down,
    sp_w_in, sp_w_out, moba_q_norm, moba_k_norm, nsa_q_norm, nsa_k_norm, nsa_cmp_pos,
    nsa_cmp_w1, nsa_cmp_w2, diff_w_in, diff_w_out, diff_q_norm, diff_k_norm, diff_lambda,
    diff_out_norm, c_2, ctx_2, c_ctx_2, ada_w_2, ada_b_2, ln_g_2, ln_b_2, mix_in_w_2, pool_w_2,
    pool_scale_2, q_norm_2, q_up_2, kv_norm_2, kv_up_2, mix_out_w_2, ffn_gate_2, ffn_up_2,
    ffn_down_2, hy_in_w_2, hy_conv_w_2, hy_conv_b_2, hy_fw1_2, hy_fb1_2, hy_fw2_2, hy_fb2_2,
    hy_fw3_2, hy_fb3_2, hy_fout_2, hy_freq_2, hy_skip_2, hy_out_w_2, router_w_2, moe_gate_2,
    moe_up_2, moe_down_2,
):
    x = first_block(
        x, c, positions, ada_w, ada_b, attn_norm, ffn_norm, ffn_w_gate, ffn_w_up, ffn_w_down,
        sp_w_in, sp_w_out, moba_q_norm, moba_k_norm, nsa_q_norm, nsa_k_norm, nsa_cmp_pos,
        nsa_cmp_w1, nsa_cmp_w2, diff_w_in, diff_w_out, diff_q_norm, diff_k_norm, diff_lambda,
        diff_out_norm,
    )
    return second_block(
        x, c_2, ctx_2, c_ctx_2, ada_w_2, ada_b_2, ln_g_2, ln_b_2, mix_in_w_2, pool_w_2,
        pool_scale_2, q_norm_2, q_up_2, kv_norm_2, kv_up_2, mix_out_w_2, ffn_gate_2, ffn_up_2,
        ffn_down_2, hy_in_w_2, hy_conv_w_2, hy_conv_b_2, hy_fw1_2, hy_fb1_2, hy_fw2_2, hy_fb2_2,
        hy_fw3_2, hy_fb3_2, hy_fout_2, hy_freq_2, hy_skip_2, hy_out_w_2, router_w_2, moe_gate_2,
        moe_up_2, moe_down_2,
    )


_drawn_inputs = setup_inputs


def setup_inputs(seed=0):
    import zlib

    import numpy as np

    out = dict(_drawn_inputs(seed))
    spreads = {}
    factors = {'attn_norm': 3.907,
     'moba_q_norm': 8.0,
     'moba_k_norm': 8.0,
     'nsa_q_norm': 8.0,
     'nsa_k_norm': 8.0,
     'nsa_cmp_pos': 6.562,
     'diff_q_norm': 8.0,
     'diff_k_norm': 8.0,
     'diff_out_norm': 5.442,
     'ctx_2': 8.0,
     'c_ctx_2': 5.548,
     'ada_b_2': 3.6,
     'pool_scale_2': 54.38,
     'q_norm_2': 8.0,
     'q_up_2': 7.494,
     'kv_norm_2': 8.0,
     'kv_up_2': 3.055,
     'hy_conv_b_2': 8.0,
     'hy_fb1_2': 6.267,
     'hy_fb2_2': 6.974,
     'hy_fb3_2': 5.02,
     'hy_freq_2': 8.0}
    for name, (base, spread) in spreads.items():
        noise = np.random.default_rng([zlib.crc32(name.encode()), seed]).standard_normal(out[name].shape)
        drawn = base * np.exp(spread * noise) if base else spread * noise
        out[name] = __import__('jax').numpy.asarray(drawn.astype(out[name].dtype))
    for name, factor in factors.items():
        out[name] = (out[name] * factor).astype(out[name].dtype)
    return out
```

```python
from contextlib import ExitStack

import numpy as np

import concourse.bass as bass
from concourse import mybir
from concourse.alu_op_type import AluOpType as ALU

F32 = mybir.dt.float32
BF16 = mybir.dt.bfloat16
I32 = mybir.dt.int32
ACT = mybir.ActivationFunctionType
AX = mybir.AxisListType

P = 128
T = 256
D = 1024
KT = D // P
NEG = -1e30
HD = 64
ROT = HD // 4
FF = 2816
FE = 3584
NE = 8
SLOTS = 128
CH = 512
CHW = KT * CH
NC_LEN, NC_STRIDE = 32, 16
NCMP = (T - NC_LEN) // NC_STRIDE + 1
CTX = 256
LAM_INIT = 0.8 - 0.6 * float(np.exp(-0.3 * 1))
ALPHA = (2.0 * 2) ** 0.25
MLA_SCALE = (64 + 32) ** -0.5
TWO_PI = 2.0 * np.pi
MAGIC = 12582912.0
PI_A = 6.28125
PI_B = float(np.float32(np.float16(TWO_PI - PI_A)))
PI_C = float(np.float32(TWO_PI - PI_A - PI_B))
PI_CLAMP = 3.1415925

VEC = {}
_at = 0
for _name, _n in [("c", 8), ("c2", 8), ("cctx", 8), ("attn_norm", 16), ("ffn_norm", 16), ("ada_b", 96),
                  ("ada_b2", 96), ("ln_g", 32), ("ln_b", 32), ("pool_scale", 4), ("q_norm", 2), ("kv_norm", 2),
                  ("conv_w", 72), ("conv_b", 24), ("skip", 8), ("moba_q", 1), ("moba_k", 1), ("nsa_q", 1),
                  ("nsa_k", 3), ("diff_q", 1), ("diff_k", 1), ("out_norm", 1), ("lam", 4), ("fb", 3),
                  ("freq", 1), ("pos_k", 16), ("pos_v", 16)]:
    VEC[_name] = (_at, _n)
    _at += _n
NVEC = _at

CON = {}
_at = 0
for _name, _n in [("ident", 128), ("ones", 128), ("half", 64), ("whole", 64), ("rot", 128), ("mask", 384),
                  ("invf", 1), ("rms_eps", 1), ("ln_eps", 1), ("half_pi", 1), ("cmask", 2 * NCMP), ("cvalid", 2 * NCMP)]:
    CON[_name] = (_at, _n)
    _at += _n
NCON = _at
MLAC = {"pool": (0, 2048), "rot": (2048, 96), "cos": (2144, 256), "sin": (2400, 256), "pool_w": (2656, 512)}
NMLAC = 2656
HYC = {"fr": (0, 512), "fs": (512, 512), "fi": (1024, 512), "gr": (1536, 512), "gi": (2048, 512),
       "z": (2560, 256), "nyq": (2816, 1), "fw": (2817, 192),
       "before": (3009, 128), "slot": (3137, 128), "tie": (3265, 64)}
NHYC = 2817


def shape_constants():
    f32 = np.float32
    con = np.zeros((P, NCON), f32)

    def put(name, a):
        o, n = CON[name]
        a = np.asarray(a, f32)
        con[:a.shape[0], o:o + n] = a.reshape(a.shape[0], n)

    p = np.arange(P)
    put("ident", np.eye(P))
    put("ones", np.ones((P, P)))
    half = np.zeros((P, 64))
    half[:64, 32] = 1
    half[64:, 33] = 1
    put("half", half)
    whole = np.zeros((P, 64))
    whole[:, 32] = 1
    put("whole", whole)
    rot = np.zeros((P, P))
    for base in (0, 64):
        for i in range(ROT // 2):
            rot[base + i + ROT // 2, base + i] = -1
            rot[base + i, base + i + ROT // 2] = 1
    put("rot", rot)
    causal = np.where(p[None, :] <= p[:, None], 0.0, NEG)
    put("mask", np.concatenate([np.zeros((P, P)), causal, causal], 1))
    inv = (f32(1.0) / (f32(500000.0) ** (np.arange(0, ROT, 2, dtype=f32) / f32(ROT)))).astype(f32)
    invf = np.zeros((P, 1), f32)
    for base in (0, 64):
        invf[base:base + 8, 0] = inv
        invf[base + 8:base + 16, 0] = inv
    put("invf", invf)
    put("rms_eps", np.full((P, 1), 1e-6))
    put("ln_eps", np.full((P, 1), 1e-5))
    put("half_pi", np.full((P, 1), np.pi / 2))
    e = np.arange(NE)
    routing = np.concatenate([(p[:, None] < p[None, :]), np.tile(p[None, :], (P, 1)),
                              np.tile((e[None, :] < e[:, None]).reshape(1, 64), (P, 1))], 1).astype(f32)
    end = np.arange(NCMP) * NC_STRIDE + NC_LEN - 1
    ok = end[None, None, :] <= (p[:, None, None] + np.array([0, P])[None, :, None])
    put("cmask", np.where(ok, 0.0, NEG))
    put("cvalid", ok)

    mla = np.zeros((P, NMLAC), f32)
    t = np.arange(T)
    pool = np.zeros((4, T, T))
    for g, w in enumerate((2, 4, 8, 16)):
        lo, hi = np.clip(t - w // 2, 0, T), np.clip(t + w // 2, 0, T)
        inside = (t[:, None] >= lo[None, :]) & (t[:, None] < hi[None, :])
        pool[g] = inside / (hi - lo)[None, :] - np.eye(T)
    mla[:, 0:2048] = pool.reshape(4, 2, P, T).transpose(2, 1, 0, 3).reshape(P, 2048)
    rot = np.eye(96) * 0
    ang = np.zeros((96, T), f32)
    inv = (f32(10000.0) ** (-np.arange(0, 16, 2, dtype=f32) / f32(16))).astype(f32)
    for base, where in ((64, t // 64), (80, t % 64)):
        for i in range(8):
            rot[base + i + 8, base + i] = -1
            rot[base + i, base + i + 8] = 1
            ang[base + i] = ang[base + 8 + i] = where.astype(f32) * inv[i]
    mla[:96, 2048:2144] = rot
    mla[:96, 2144:2400] = np.cos(ang)
    mla[:96, 2400:2656] = np.sin(ang)

    hyc = np.zeros((P, NHYC), f32)
    th = 2 * np.pi / 512 * ((t[:, None] * t[None, :]) % 512)
    alt = (-1.0) ** t
    fr, fs = np.cos(th), -np.sin(th)
    fi = fs.copy()
    fi[:, 0] = alt
    gr, gi = 2 * fr.T / 512, 2 * fs.T / 512
    gr[0] = 1.0 / 512
    gi[0] = alt / 512
    for n, a in (("fr", fr), ("fs", fs), ("fi", fi), ("gr", gr), ("gi", gi)):
        hyc[:, HYC[n][0]:HYC[n][0] + 512] = a.reshape(2, P, T).transpose(1, 0, 2).reshape(P, 512)
    tt = np.linspace(0.0, 1.0, T, dtype=f32)[:, None]
    wa = (f32(2.0 * np.pi / T) * np.arange(T, dtype=f32))[:, None]
    bands = np.linspace(1e-4, 15, 16, dtype=f32)[None, :]
    z = np.concatenate([tt, np.cos(bands * wa), -np.sin(bands * wa)], 1)
    hyc[:33, 2560:2816] = z.T
    hyc[:, 2816] = (-1.0) ** p
    lo, hi = np.log(1e-2) / 1.5, np.log(1e-2) / 0.3
    deltas = np.abs(np.linspace(lo, hi, D, dtype=f32))
    dec = np.exp(-tt * deltas).astype(f32)
    decb = dec.copy()
    decb[0] = 0
    decay = np.stack([dec, decb]).reshape(2, 2, P, D).transpose(2, 0, 1, 3).reshape(P, 4 * D)
    spread = np.zeros((32, 16, 2, 64), f32)
    for t_ in range(16):
        for h_ in range(2):
            spread[2 * t_ + h_, t_, h_] = 1
    return con, mla, hyc, routing, spread.reshape(32, 2048), np.ascontiguousarray(decay)


class Bank:

    def __init__(self, sem, name, credit=0):
        self.full, self.free = sem(name + "_full"), sem(name + "_free")
        self.credit, self.uses = credit, 0


class Job:

    def __init__(self, banks, b, use=None, stride=0):
        self.b, self.bank, self.stride = b, banks[b], stride
        if use is None:
            use = self.bank.uses
            self.bank.uses += 1
        self.use = use

    def at(self, i):
        return self.use if i is None or self.stride == 0 else self.use + i * self.stride

    def open(self, eng, i=None):
        if i is None and self.use + self.bank.credit == 0:
            return
        eng.wait_ge(self.bank.free, self.at(i) + self.bank.credit)

    def filled(self, eng, i=None):
        eng.wait_ge(self.bank.full, self.at(i) + 1)

    def emptied(self, eng, i=None):
        eng.wait_ge(self.bank.free, self.at(i) + 1 + self.bank.credit)

    def when_full(self):
        return self.bank.full, self.use + 1, self.stride


def loop_jobs(banks, order, passes):
    per = {b: order.count(b) for b in order}
    jobs = [Job(banks, b, banks[b].uses + order[:n].count(b), per[b]) for n, b in enumerate(order)]
    for b in per:
        banks[b].uses += per[b] * passes
    return jobs


class Ring:

    def __init__(self, sem, name, slots):
        self.sems = [sem(f"{name}_loaded{s}") for s in range(slots)]
        self.slots, self.n = slots, 0
        self.last, self.loads = [None] * slots, [0] * slots


class Chunk:

    def __init__(self, ring, dmas=1, slot=None):
        self.ring, self.freed_by, self.before, self.stride, self.wrap = ring, None, None, 0, False
        self.slot = ring.n % ring.slots
        ring.n += 1
        self.before = ring.last[self.slot]
        ring.last[self.slot] = self
        ring.loads[self.slot] += 16 * dmas
        self.value = ring.loads[self.slot]

    @property
    def sem(self):
        return self.ring.sems[self.slot]

    def room(self, eng, i=None):
        if self.wrap and i is not None:
            sem, value, stride = self.wrap.freed_by
            eng.wait_ge(sem, value - stride + i * stride)
        elif self.before is not None:
            sem, value, stride = self.before.freed_by
            eng.wait_ge(sem, value if i is None or stride == 0 else value + i * stride)

    def loaded(self, eng, i=None):
        eng.wait_ge(self.sem, self.value if i is None or self.stride == 0 else self.value + i * self.stride)


class LoopEnd:

    def __init__(self, chunk, passes):
        self.chunk, self.passes = chunk, passes

    @property
    def freed_by(self):
        sem, value, stride = self.chunk.freed_by
        return sem, value + (self.passes - 1) * stride, 0


def loop_chunks(ring, count, passes):
    assert count % ring.slots == 0
    chunks = [Chunk(ring) for _ in range(count)]
    turns = count // ring.slots
    for n, c in enumerate(chunks):
        c.stride = 16 * turns
        if n < ring.slots:
            c.wrap = chunks[count - ring.slots + n]
    for c in chunks[count - ring.slots:]:
        ring.last[c.slot] = LoopEnd(c, passes)
        ring.loads[c.slot] += 16 * turns * (passes - 1)
    return chunks


class Steps:

    def __init__(self, eng, sem):
        self.eng, self.sem, self.n = eng, sem, 0

    def __call__(self, ins):
        ins.then_inc(self.sem, 1)
        self.n += 1
        self.eng.wait_ge(self.sem, self.n)


def moe_sequence():
    out = [("gu", 0)]
    for g in range(14):
        if g + 1 < 14:
            out.append(("gu", g + 1))
        out.append(("t", g))
        if g >= 1:
            out.append(("d", g - 1))
        if 9 <= g < 13:
            out.append(("s", 0, g - 9))
    out.append(("d", 13))
    return out + [("s", 1, q) for q in range(4)]


def build(nc, a, out):
    with ExitStack() as ctx:
        def sb(name, shape, dt=F32):
            return ctx.enter_context(nc.sbuf_tensor(name, shape, dt))

        def sem(name):
            return ctx.enter_context(nc.semaphore(name))

        wring = sb("wring", [P, 6, CHW])
        aring = sb("aring", [P, 2, CHW])
        X = sb("X", [P, KT, T])
        H = sb("H", [P, KT, T])
        F = sb("F", [P, 24, T])
        V = sb("V", [P, 2048])
        OT = sb("OT", [P, KT, T])
        work = sb("work", [P, 3072])
        con = sb("con", [P, NCON])
        vec = sb("vec", [P, NVEC])
        mod = sb("mod", [P, 4, 48])
        modc = sb("modc", [P, 16])
        cs = sb("cs", [P, 24])
        gsc = sb("gsc", [P, KT])
        tables = sb("tables", [P, 2, T])
        cosT, sinT = tables[:, 0, :], tables[:, 1, :]
        posi = work[:, 2048:2304].bitcast(I32)
        rstd = sb("rstd", [P, T])
        rheads = rstd[0:32, :]
        gates = sb("gates", [P, 2, 24])
        zero = sb("zero", [P, P], BF16)
        nmax, ssum, fac = sb("nmax", [P, 2, 2]), sb("ssum", [P, 2, 2]), sb("fac", [P, 2, 2])
        cst = sb("cst", [P, 2, 16])
        lamt = sb("lamt", [P, 4])
        ogain = sb("ogain", [P, 1])
        rw = sb("rw", [P, KT, NE])
        lg, ch8, pw, posm = (sb(n, [P, 2, NE]) for n in ("lg", "ch8", "pw", "posm"))
        mx8, psum8 = sb("mx8", [P, 2, 8]), sb("psum8", [P, 2])
        over = sb("over", [P, 1])
        flag = sb("flag", [P, 1], I32)
        PS = [ctx.enter_context(nc.psum_tensor(f"ps{b}", [P, 512], F32)) for b in range(8)]

        Fl = F[:].rearrange("p a t -> p (a t)")
        Hl = H[:].rearrange("p a t -> p (a t)")
        OTl = OT[:].rearrange("p a t -> p (a t)")
        Xl = X[:].rearrange("p a t -> p (a t)")
        cw2 = OTl[:, 0:384]
        cmp8 = work[:, 0:128].rearrange("p (a n) -> p a n", a=2)
        scr = aring[:, 1, :]

        def C(name, rows=P):
            o, n = CON[name]
            return con[0:rows, o:o + n]

        def R(name):
            o, n = HYC[name]
            return aring[:, 0, o:o + n]

        def vc(name, k=0, rows=P, n=1):
            o = VEC[name][0] + k
            return vec[0:rows, o:o + n]

        def w3(c, n=CH, k=KT):
            return wring[:, c.slot, 0:k * n].rearrange("p (k n) -> p k n", n=n)

        def bank3(b, n, rows=P):
            return PS[b][0:rows, :].rearrange("p (a n) -> p a n", n=n)

        banks = [Bank(sem, f"bank{b}") for b in range(8)]
        ring, mring = Ring(sem, "w", 6), Ring(sem, "m", 2)
        small_loaded = sem("small_loaded")
        ctx_loaded = sem("ctx_loaded")
        out_stored = sem("out_stored")
        dve_step = sem("dve_step")
        cs_ready, zero_ready = sem("cs_ready"), sem("zero_ready")
        ada_step, ada_used = sem("ada_step"), sem("ada_used")
        sq_ready, sd_ready, h_ready, x_ready = (
            sem("sq_ready"), sem("sd_ready"), sem("h_ready"), sem("x_ready"))
        x_ready_raw = sem("x_ready_raw")
        sin_arg, sin_done = sem("sin_arg"), sem("sin_done")
        proj_copied, stat_summed = sem("proj_copied"), sem("stat_summed")
        rh_sd, rh_ready, rope_done = sem("rh_sd"), sem("rh_ready"), sem("rope_done")
        nmax_ready, exp_done, p_ready, pv_done = sem("nmax_ready"), sem("exp_done"), sem("p_ready"), sem("pv_done")
        gate_raw, gates_ready = sem("gate_raw"), sem("gates_ready")
        windows_ready, blocks_ready, hidrep_ready = sem("windows_ready"), sem("blocks_ready"), sem("hidrep_ready")
        cshift, cexp, cp_ready = sem("cshift"), sem("cexp"), sem("cp_ready")
        ksw_ready, rows_done, vrows_ready = sem("ksw_ready"), sem("rows_done"), sem("vrows_ready")
        lam_prod = sem("lam_prod")
        down_used, silu_done, hid_done = sem("down_used"), sem("silu_done"), sem("hid_done")
        lat_ready = sem("lat_ready")
        zconv = sem("zconv")
        hy_ready, spec_ready = sem("hy_ready"), sem("spec_ready")
        rt_exp, rt_ready, route_ready, flag_ready = sem("rt_exp"), sem("rt_ready"), sem("route_ready"), sem("flag_ready")
        over_done = sem("over_done")

        def J(b):
            return Job(banks, b)

        ada0 = loop_chunks(mring, 2, 6)
        for n, c in enumerate(ada0):
            c.freed_by = (ada_used, n + 1, 2)
        adas = 12
        mod_job = [J(7)]
        norm_job = []

        def plan_norm(mean):
            norm_job.append(([J(6)] if mean else []) + [J(6)])

        def plan_proj(pairs, per_chunk):
            return [J(j % 4) for j in range(pairs)]

        def plan_rope(pairs):
            return J(7), [J(j % 2) for j in range(pairs)], [J(2 + j % 2) for j in range(pairs)]

        def plan_units(groups):
            s, t, o = [], [], []
            n = 0
            for g in groups:
                o.append(J(4 + len(o) % 2))
                for _ in range(g):
                    s.append(J(n % 2))
                    t.append(J(2 + n % 2))
                    n += 1
            return s, t, o

        def plan_out():
            cs2 = [Chunk(ring), Chunk(ring)]
            jobs = [J(j) for j in range(4)]
            cs2[0].freed_by, cs2[1].freed_by = jobs[1].when_full(), jobs[3].when_full()
            return cs2, jobs

        def plan_ffn(f, adas):
            L = {}
            L["c"] = loop_chunks(ring, 6, 2)
            L["j"] = loop_jobs(banks, [0, 1, 2, 3] * 2, 2)
            for n in range(2):
                L["c"][2 * n].freed_by = L["j"][4 * n + 2].when_full()
                L["c"][2 * n + 1].freed_by = L["j"][4 * n + 3].when_full()
                L["c"][4 + n].freed_by = (down_used, 5 * f + n + 1, 2)
            L["a"] = loop_chunks(mring, 4, 2)
            for n, c in enumerate(L["a"]):
                c.freed_by = (ada_used, adas + n + 1, 4)
            L["tc"] = [Chunk(ring) for _ in range(6)]
            L["tj"] = [J(b) for b in (0, 1, 2, 3, 0, 1)]
            for n, j in ((0, 2), (1, 3), (2, 4), (3, 5)):
                L["tc"][n].freed_by = L["tj"][j].when_full()
            L["ta"] = [Chunk(mring) for _ in range(4)]
            for n, c in enumerate(L["ta"]):
                c.freed_by = (ada_used, adas + 8 + n + 1, 0)
            L["y"] = [J(b) for b in (4, 5, 6, 7)]
            L["tc"][4].freed_by = (down_used, 5 * f + 5, 0)
            L["tc"][5].freed_by = L["y"][3].when_full()
            return L

        plan_norm(False)
        sp_w = [Chunk(ring) for _ in range(6)]
        sp_pair = plan_proj(8, 2)
        sp_tok = [J(0), J(1)]
        sp_v = [J(2), J(3)]
        for n in range(3):
            sp_w[n].freed_by = sp_pair[2 * n + 1].when_full()
        sp_w[3].freed_by = sp_w[4].freed_by = sp_tok[1].when_full()
        sp_w[5].freed_by = sp_v[1].when_full()
        sp_rope = plan_rope(8)
        sp_const, sp_scr = Chunk(mring), Chunk(mring, dmas=0)
        sp_const.freed_by = sp_scr.freed_by = sp_rope[1][7].when_full()
        cmp_w = [Chunk(ring), Chunk(ring)]
        hid_job, kvc_job, cs_job, ct_job = J(0), J(1), J(2), J(3)
        cmp_w[0].freed_by = cmp_w[1].freed_by = hid_job.when_full()
        sp_units = plan_units([1] * 8 + [2] * 8)
        sp_out, sp_y = plan_out()
        plan_norm(False)
        ffn = [plan_ffn(0, adas)]
        adas += 12
        mod_job.append(J(3))
        plan_norm(False)
        df_w = [Chunk(ring) for _ in range(6)]
        df_pair = plan_proj(8, 2)
        df_v = [J(b) for b in range(4)]
        for n in range(4):
            df_w[n].freed_by = df_pair[2 * n + 1].when_full()
        df_w[4].freed_by, df_w[5].freed_by = df_v[1].when_full(), df_v[3].when_full()
        df_rope = plan_rope(8)
        df_const, df_scr = Chunk(mring), Chunk(mring, dmas=0)
        df_const.freed_by = df_scr.freed_by = df_rope[1][7].when_full()
        lam_job = J(7)
        df_units = plan_units([2] * 8)
        on_stat, on_bc = J(7), [J(j) for j in range(4)]
        df_out, df_y = plan_out()
        plan_norm(False)
        ffn.append(plan_ffn(1, adas))
        adas += 12
        mod_job.append(J(3))
        ml_const, ml_scr = Chunk(mring, dmas=2), Chunk(mring, dmas=0)
        ml_w = [Chunk(ring) for _ in range(3)] + [Chunk(ring, dmas=2)]
        ml_pool = [J(0), J(1)]
        ml_lat = [J(2), J(3), J(0)]
        ml_kr = J(1)
        ml_stat = [J(2), J(3)]
        ml_d = [J(0), J(1)]
        ml_py = [J(2), J(3)]
        ml_q, ml_qr = [J(j % 2) for j in range(4)], [J(2 + j % 2) for j in range(4)]
        ml_krr = J(0)
        ml_k = [J(1 + h % 3) for h in range(8)]
        ml_v = [J(j) for j in range(4)]
        ml_w[0].freed_by, ml_w[1].freed_by = ml_pool[1].when_full(), ml_lat[2].when_full()
        ml_w[2].freed_by, ml_w[3].freed_by = ml_kr.when_full(), ml_v[3].when_full()
        ml_const.freed_by = (rope_done, 16 + 5, 0)
        ml_units = plan_units([2] * 8)
        ml_scr.freed_by = ml_units[0][0].when_full()
        ml_out, ml_y = plan_out()
        plan_norm(True)
        ffn.append(plan_ffn(2, adas))
        adas += 12
        mod_job.append(J(3))
        plan_norm(True)
        hy_const, hy_scr = Chunk(mring, dmas=5), Chunk(mring, dmas=0)
        hy_f = [Chunk(ring), Chunk(ring)]
        hy_w = [Chunk(ring) for _ in range(6)]
        hy_sin = [J(0), J(1), J(2)]
        hy_taps = [(J(2 * (n % 2)), J(2 * (n % 2) + 1)) for n in range(4)]
        hy_f[0].freed_by = (hy_ready, 1, 0)
        hy_f[1].freed_by = hy_taps[3][1].when_full()
        hy_k = [J(n % 4) for n in range(8)]
        hy_n = [J(0), J(1)]
        hy_pair = [J(n % 4) for n in range(12)]
        for n in range(6):
            hy_w[n].freed_by = hy_pair[2 * n + 1].when_full()
        hy_t = [J(n) for n in range(4)]
        hy_vs = [[J(n) for n in range(4)] for _ in range(2)]
        hy_y = [[J(4), J(5)] for _ in range(2)]
        hy_out, hy_yo = plan_out()
        plan_norm(True)
        rt_job, zt_job, pos_job = J(7), [J(n) for n in range(4)], J(7)

        def plan_moe(banks, ring, used):
            M = {"used": used}
            order, names = [], []

            def j(name, b):
                order.append(b)
                names.append(name)

            for e in range(2):
                j(("gather", e, 0), 7), j(("gather", e, 1), 7), j(("st", e), 7)
            for name in moe_sequence():
                kind, g = name[0], name[1]
                if kind == "gu":
                    j(("g", g), g % 2), j(("u", g), 2 + g % 2)
                elif kind == "t":
                    j(("t", g), 4)
                elif kind == "d" and g % 7 == 0:
                    j(("y", g // 7, 0), 5), j(("y", g // 7, 1), 6)
                elif kind == "s":
                    j(("s", g, name[2]), 7)
            M["j"] = dict(zip(names, loop_jobs(banks, order, NE // 2)))
            cks = loop_chunks(ring, 42, NE // 2)
            M["c"] = {}
            at = 0
            for name in moe_sequence():
                if name[0] == "gu":
                    M["c"]["g", name[1]], M["c"]["u", name[1]] = cks[at], cks[at + 1]
                    cks[at].freed_by = M["j"]["g", name[1]].when_full()
                    cks[at + 1].freed_by = M["j"]["u", name[1]].when_full()
                    at += 2
                elif name[0] == "d":
                    g = name[1]
                    M["c"]["d", g] = cks[at]
                    last = g % 7 == 6
                    cks[at].freed_by = (M["j"]["y", g // 7, 1].when_full() if last
                                        else (used, g + 1 - g // 7, 12))
                    at += 1
            return M

        moe = plan_moe(banks, ring, sem("expert_down_used"))
        banks2 = [Bank(sem, f"again{b}", credit=1) for b in range(8)]
        ring2 = Ring(sem, "again_w", 6)
        moe2 = plan_moe(banks2, ring2, sem("again_down_used"))
        for M, tag in ((moe, "moe"), (moe2, "again")):
            for name in ("sel", "wsel", "xg", "st", "silu", "hid", "ht", "ye", "acc"):
                M[name] = sem(f"{tag}_{name}")
        plan_norm(True)

        SMALL = 8 * 16

        CAUSAL_TURN = [(256, 0), (0, 128), (128, 256)]

        def causal(q, k, v0, v1, out, first, last, factor, extra=None):
            if first and last:
                values = [(v0, 0, 128, 0, True, True), (v0, 128, 256, 128, True, False), (v1, 256, 384, 128, False, True)]
            elif first:
                values = [(v0, 0, 256, 0, extra is None, False), (v1, 256, 384, 128, False, False)]
            else:
                values = [(v1, 256, 384, 128, False, False), (v0, 0, 256, 0, False, True)]
            return {"scores": [(0, q[:, P:T], k), (256, q[:, 0:P], k[:, 0:P])],
                    "turn": CAUSAL_TURN, "values": values,
                    "rows": [(0, 256, 1), (256, 384, 0)], "width": 384, "out": out, "first": first, "last": last,
                    "factor": factor, "cmp": extra, "scale": HD ** -0.5, "mask": C("mask")}

        Vt = V[:].rearrange("p (t n) -> p t n", t=2)

        def sparse_specs():
            out = []
            for h in range(8):
                p0 = (h % 2) * HD
                out.append(causal(F[p0:p0 + HD, h // 2, :], F[p0:p0 + HD, 4 + h // 2, :],
                                  Vt[:, 0, h * HD:(h + 1) * HD], Vt[:, 1, h * HD:(h + 1) * HD], h, True, True, None))
            for h in range(8):
                g, p0 = h // 4, (h % 2) * HD
                q = F[p0:p0 + HD, 8 + h // 2, :]
                for b in range(2):
                    k = F[p0:p0 + HD, 13 + b, :] if g == h % 2 else Hl[p0:p0 + HD, b * T:(b + 1) * T]
                    v = [Vt[:, t, 512 + b * P + g * HD:512 + b * P + (g + 1) * HD] for t in range(2)]
                    o = 1024 + h * HD
                    extra = (Hl[:, o:o + HD], Hl[:, 512 + g * T:512 + (g + 1) * T]) if b == 0 else None
                    out.append(causal(q, k, v[0], v[1], 8 + h, b == 0, b == 1,
                                      gates[:, :, (1 + b) * 8 + h], extra))
            return out

        def diff_specs():
            out = []
            for h in range(8):
                for c in range(2):
                    p0 = c * HD
                    out.append(causal(F[p0:p0 + HD, h, :], F[p0:p0 + HD, 8 + h, :], Vt[:, 0, h * P:(h + 1) * P],
                                      Vt[:, 1, h * P:(h + 1) * P], h, c == 0, c == 1,
                                      None if c == 0 else lamt[:, 3:4].to_broadcast([P, 2])))
            return out

        def mla_specs():
            out = []
            K8 = Fl[0:96, 2048:6144].rearrange("p (h t) -> p h t", h=8)
            V4 = V[:].rearrange("p (t n) -> p t n", t=4)
            for h in range(8):
                for qt in range(2):
                    out.append({"scores": [(0, F[0:96, h, qt * P:(qt + 1) * P], K8[:, h, :])],
                                "turn": [(n * P, n * P) for n in range(4)],
                                "values": [(V4[:, n, h * HD:(h + 1) * HD], n * P, (n + 1) * P, qt * P, n == 0, n == 3)
                                           for n in range(4)],
                                "rows": [(0, 512, 0)], "width": 512, "out": h, "first": qt == 0, "last": qt == 1,
                                "factor": None, "scale": MLA_SCALE, "mask": None})
            return out

        def heads_to(h):
            return OT[(h % 2) * HD:(h % 2 + 1) * HD, h // 2, :]

        def spectrum(h):
            a_, o = (Fl, 2048) if h == 0 else (scr, 1024)
            return tuple(a_[:, o + n * 1024:o + (n + 1) * 1024].rearrange("p (k n) -> p k n", k=2) for n in range(2))

        def gathered(e):
            return Fl[:, e * 1024:(e + 1) * 1024].rearrange("p (k n) -> p k n", k=KT)

        yacc = F[:, 8:16, :]
        ye = Fl[:, 4096:5120]

        def sel(e):
            return Fl[:, 5120 + e * 256:5376 + e * 256].rearrange("p (t n) -> p t n", t=2)

        def wsel(e):
            return Fl[:, 5632 + e * 256:5888 + e * 256].rearrange("p (t n) -> p t n", t=2)

        spare = work[:, 2560:2816]

        def spread_sel(e):
            return tables[:, e, :]

        def window(par, g, half, v):
            src = F[g * HD:(g + 1) * HD, 15 if v else 12, :].rearrange("p (m s) -> p s m", s=16)
            dst = Hl[par * HD:(par + 1) * HD, 512 + 480 * v:992 + 480 * v].rearrange(
                "p (l g n) -> p l g n", l=16, g=2)
            return dst[:, 8 * half:8 * half + 8, g, :], src[:, par::2, half:half + NCMP]

        block = ctx.enter_context(nc.Block())

        @block.sync
        def _(sp):
            def load(c, src, i=None, dst=None):
                c.room(sp, i)
                src = src.rearrange("(k p) n -> p k n", p=P)
                k, n = src.shape[1], src.shape[2]
                dst = wring[:, c.slot, 0:k * n] if dst is None else dst
                sp.dma_start(dst.rearrange("p (k n) -> p k n", n=n), src).then_inc(c.sem, 16)

            def load_ada(c, w, col, i=None):
                load(c, w[:, bass.ds(col, CH)], i, aring[:, c.slot, :])

            def small(dst, src):
                sp.dma_start(dst, src).then_inc(small_loaded, 16)

            small(vec[:], a["vec"])
            small(con[:], a["con"])
            small(posi, a["positions"].to_broadcast([P, T]))
            small(X[:], a["x"])
            small(rw[:], a["router_w_2"][0].rearrange("(k p) e -> p k e", p=P))
            w2 = a["nsa_cmp_w2"][0].rearrange("v (k p) d -> v p k d", p=P)
            for dup in range(2):
                small(cw2[:, 0:256].rearrange("p (k u d) -> p k u d", k=2, u=2)[:, :, dup, :], w2[0])
            small(cw2[:, 256:384].rearrange("p (k d) -> p k d", k=2), w2[1])

            for n in range(2):
                load_ada(ada0[n], a["ada_w"][0], n * CH)
            with sp.Fori(1, 6) as i:
                for n in range(2):
                    load_ada(ada0[n], a["ada_w"][0], i * 2 * CH + n * CH, i)

            w = a["sp_w_in"][0]
            for c, lo, n in zip(sp_w, (0, 512, 1536, 2048, 2560, 1024), (512, 512, 512, 512, 280, 512)):
                load(c, w[:, lo:lo + n])
            sp_const.room(sp)
            sp.dma_start(aring[0:32, sp_const.slot, 0:2048], a["spread"]).then_inc(sp_const.sem, 16)
            for v in range(2):
                load(cmp_w[v], a["nsa_cmp_w1"][0, v].rearrange("l d e -> (l d) e"))
            for c, h in zip(sp_out, range(2)):
                load(c, a["sp_w_out"][0][:, h * CH:(h + 1) * CH])

            def ffn_loads(L, wg, wu, wd, ada_w):
                def body(i, at):
                    for n in range(2):
                        load(L["c"][2 * n], wg[:, bass.ds(at * 2 * CH + n * CH, CH)], i)
                        load(L["c"][2 * n + 1], wu[:, bass.ds(at * 2 * CH + n * CH, CH)], i)
                        load_ada(L["a"][n], ada_w, 4 * CH + at * 4 * CH + n * CH, i)
                    for n in range(2):
                        load(L["c"][4 + n], wd[bass.ds(at * 2 * CH + n * CH, CH), :], i)
                        load_ada(L["a"][2 + n], ada_w, 6 * CH + at * 4 * CH + n * CH, i)

                body(None, 0)
                with sp.Fori(1, 2) as i:
                    body(i, i)
                tc = L["tc"]
                load(tc[0], wg[:, 4 * CH:5 * CH])
                load(tc[1], wu[:, 4 * CH:5 * CH])
                load_ada(L["ta"][0], ada_w, 0)
                load(tc[2], wg[:, 5 * CH:FF])
                load(tc[3], wu[:, 5 * CH:FF])
                load_ada(L["ta"][1], ada_w, CH)
                load(tc[4], wd[4 * CH:5 * CH, :])
                load_ada(L["ta"][2], ada_w, 2 * CH)
                load(tc[5], wd[5 * CH:FF, :])
                load_ada(L["ta"][3], ada_w, 3 * CH)

            ffn_loads(ffn[0], a["ffn_w_gate"][0], a["ffn_w_up"][0], a["ffn_w_down"][0], a["ada_w"][1])

            for n, c in enumerate(df_w):
                load(c, a["diff_w_in"][0][:, n * CH:(n + 1) * CH])
            df_const.room(sp)
            sp.dma_start(aring[0:32, df_const.slot, 0:2048], a["spread"]).then_inc(df_const.sem, 16)
            for c, h in zip(df_out, range(2)):
                load(c, a["diff_w_out"][0][:, h * CH:(h + 1) * CH])
            ffn_loads(ffn[1], a["ffn_w_gate"][1], a["ffn_w_up"][1], a["ffn_w_down"][1], a["ada_w_2"][0])

            ml_const.room(sp)
            sp.dma_start(aring[:, ml_const.slot, 0:NMLAC], a["mlac"]).then_inc(ml_const.sem, 16)
            sp.dma_start(aring[:, ml_const.slot, NMLAC:NMLAC + 512].rearrange("p (g d) -> p g d", g=4),
                         a["pool_w_2"][0].rearrange("g c d -> c g d")).then_inc(ml_const.sem, 16)
            mod_job[2].emptied(sp)
            sp.dma_start(F[:, 16:24, :], a["ctx_2"]).then_inc(ctx_loaded, 16)
            w = a["mix_in_w_2"][0]
            load(ml_w[0], w[:, 0:512])
            load(ml_w[1], w[:, 512:1024])
            load(ml_w[2], w[:, 960:1056])
            load(ml_w[3], a["q_up_2"][0])
            src = a["kv_up_2"][0].rearrange("(k p) n -> p k n", p=P)
            sp.dma_start(wring[:, ml_w[3].slot, 1536:3584].rearrange("p (k n) -> p k n", k=2),
                         src).then_inc(ml_w[3].sem, 16)
            for c, h in zip(ml_out, range(2)):
                load(c, a["mix_out_w_2"][0][:, h * CH:(h + 1) * CH])
            ffn_loads(ffn[2], a["ffn_gate_2"][0], a["ffn_up_2"][0], a["ffn_down_2"][0], a["ada_w_2"][1])

            hy_const.room(sp)
            hc = aring[:, hy_const.slot, :]
            sp.dma_start(hc[:, 0:NHYC], a["hyc"]).then_inc(hy_const.sem, 16)
            o = HYC["before"][0]
            sp.dma_start(hc[:, o:o + 320], a["routing"]).then_inc(hy_const.sem, 16)
            o = HYC["fw"][0]
            sp.dma_start(hc[0:33, o:o + 64], a["hy_fw1_2"][0]).then_inc(hy_const.sem, 16)
            sp.dma_start(hc[0:64, o + 64:o + 128], a["hy_fw2_2"][0]).then_inc(hy_const.sem, 16)
            sp.dma_start(hc[0:64, o + 128:o + 192], a["hy_fw3_2"][0]).then_inc(hy_const.sem, 16)
            hy_f[0].room(sp)
            sp.dma_start(wring[:, hy_f[0].slot, :], a["decay"]).then_inc(hy_f[0].sem, 16)
            hy_f[1].room(sp)
            sp.dma_start(wring[0:64, hy_f[1].slot, 0:2 * D], a["hy_fout_2"][0]).then_inc(hy_f[1].sem, 16)
            for n, c in enumerate(hy_w):
                load(c, a["hy_in_w_2"][0][:, n * CH:(n + 1) * CH])
            for c, h in zip(hy_out, range(2)):
                load(c, a["hy_out_w_2"][0][:, h * CH:(h + 1) * CH])

            def moe_loads(M, dst_ring):
                gate = a["moe_gate_2"][0].rearrange("e (k p) n -> p k e n", p=P)
                up = a["moe_up_2"][0].rearrange("e (k p) n -> p k e n", p=P)
                down = a["moe_down_2"][0].rearrange("e (s k p) n -> p k (e s) n", k=4, p=P)

                def body(i, at):
                    for name in moe_sequence():
                        g = name[1]
                        e, s = g // 7, g % 7
                        if name[0] == "gu":
                            for kind, src in (("g", gate), ("u", up)):
                                c = M["c"][kind, g]
                                c.room(sp, i)
                                sp.dma_start(w3(c), src[:, :, bass.ds(2 * at + e, 1), s * CH:(s + 1) * CH]
                                             .rearrange("p k e n -> p k (e n)")).then_inc(c.sem, 16)
                        elif name[0] == "d":
                            c = M["c"]["d", g]
                            c.room(sp, i)
                            sp.dma_start(w3(c, D, 4), down[:, :, bass.ds(14 * at + g, 1), :]
                                         .rearrange("p k e n -> p k (e n)")).then_inc(c.sem, 16)

                body(None, 0)
                with sp.Fori(1, NE // 2) as i:
                    body(i, i)

            moe_loads(moe, ring)
            sp.wait_ge(flag_ready, 1)
            with sp.If(sp.value_load(flag[0:1, 0:1], min_val=0, max_val=1) > 0):
                moe["j"]["y", 1, 1].filled(sp, NE // 2 - 1)
                moe_loads(moe2, ring2)
            sp.wait_ge(x_ready, 4)
            sp.dma_start(out, X[:]).then_inc(out_stored, 16)
            sp.wait_ge(out_stored, 16)

        @block.tensor
        def _(pe):
            def mm(dst, lhsT, rhs, start=True, stop=True, **kw):
                return pe.matmul(dst, lhsT, rhs, start=start, stop=stop, **kw)

            def fill(job, ins, i=None):
                ins.then_inc(job.bank.full, 1)

            def reduce_mod(layer):
                job = mod_job[layer]
                job.open(pe)
                pe.wait_ge(ada_used, 12 * (layer + 1))
                for t in range(48):
                    last = mm(PS[job.b][:, t:t + 1], Fl[:, t * P:(t + 1) * P], C("ones")[:, 0:1])
                if layer == 2:
                    for t in range(16):
                        last = mm(PS[job.b][:, 64 + t:65 + t], OTl[:, t * P:(t + 1) * P], C("ones")[:, 0:1])
                fill(job, last)

            def sum_features(job, src, need, count):
                job.open(pe)
                pe.wait_ge(need, count)
                for k in range(KT):
                    last = mm(PS[job.b][:, 0:T], C("ones"), src[:, k, :], k == 0, k == KT - 1)
                fill(job, last)

            def norm(n, sq_count):
                jobs = norm_job[n]
                if len(jobs) == 2:
                    sum_features(jobs[0], X, x_ready_raw, n - 3)
                sum_features(jobs[-1], H, sq_ready, sq_count)

            def tile(dst, w, lo, rhs):
                rows = dst.shape[0]
                for k in range(KT):
                    last = mm(dst, w[:, k, lo:lo + rows], rhs[:, k, :], k == 0, k == KT - 1)
                return last

            def by_token(dst, w, lo, n, src, qt):
                for k in range(w.shape[1]):
                    last = mm(dst, src[:, k, qt * P:(qt + 1) * P], w[:, k, lo:lo + n], k == 0, k == w.shape[1] - 1)
                return last

            def head_sums(job, j, copied, tiles, total, full):
                pe.wait_ge(proj_copied, copied)
                for m, t in enumerate(tiles):
                    last = mm(PS[job.b][0:32, 0:T], C("half")[:, 32 - 2 * t:64 - 2 * t],
                              work[:, (j % 2) * 512 + m * T:(j % 2) * 512 + (m + 1) * T], t == 0, t == total - 1)
                if full:
                    fill(job, last)
                else:
                    last.then_inc(stat_summed, 1)

            def rope(rp, base, tiles, table):
                _, bc, ro = rp
                pe.wait_ge(rh_ready, base // 8 + 1)
                table.loaded(pe)
                for j in range(9):
                    if j < 8:
                        bc[j].open(pe)
                        for m in range(2):
                            if 2 * j + m < tiles:
                                t = 2 * j + m
                                last = mm(PS[bc[j].b][:, m * T:(m + 1) * T],
                                          aring[0:32, table.slot, t * P:(t + 1) * P], rheads)
                        fill(bc[j], last)
                    if j >= 1:
                        n = min(2, tiles - 2 * (j - 1)) * T
                        ro[j - 1].open(pe)
                        bc[j - 1].emptied(pe)
                        fill(ro[j - 1], mm(PS[ro[j - 1].b][:, 0:n], C("rot"), Fl[:, (j - 1) * 512:(j - 1) * 512 + n]))

            def units(plan, specs, base):
                s, t, o = plan
                for i in range(len(specs) + 2):
                    if i < len(specs):
                        s[i].open(pe)
                        for dst, q, k in specs[i]["scores"]:
                            last = mm(PS[s[i].b][:, dst:dst + k.shape[-1]], q, k)
                        fill(s[i], last)
                    if 0 <= i - 1 < len(specs):
                        u = i - 1
                        t[u].open(pe)
                        pe.wait_ge(p_ready, base + u + 1)
                        pr = work[:, 1024 + (u % 2) * 512:1024 + (u % 2 + 1) * 512]
                        for src, dst in specs[u]["turn"]:
                            last = pe.transpose(PS[t[u].b][:, dst:dst + P], pr[:, src:src + P], C("ident"))
                        fill(t[u], last)
                    if i >= 2:
                        u = i - 2
                        sp_ = specs[u]
                        job = o[sp_["out"]]
                        if sp_["first"]:
                            job.open(pe)
                            if sp_.get("cmp") is not None:
                                mm(PS[job.b][0:HD, 0:T], *sp_["cmp"], True, False)
                        t[u].emptied(pe)
                        pt = work[:, 2048 + (u % 2) * 512:2048 + (u % 2 + 1) * 512]
                        for v, lo, hi, dst, start, stop in sp_["values"]:
                            last = mm(PS[job.b][0:v.shape[-1], dst:dst + hi - lo], v, pt[:, lo:hi], start, stop)
                        if sp_["last"]:
                            fill(job, last)
                        else:
                            last.then_inc(pv_done, 1)

            def project_out(cks, jobs, src):
                for j in range(4):
                    if j % 2 == 0:
                        cks[j // 2].loaded(pe)
                    jobs[j].open(pe)
                    for m in range(2):
                        last = tile(PS[jobs[j].b][:, m * T:(m + 1) * T], w3(cks[j // 2]), (j % 2) * T + m * P, src)
                    fill(jobs[j], last)

            def hidden_pair(jg, ju, cg, cu, lo, width, i=None):
                for job, c in ((jg, cg), (ju, cu)):
                    c.loaded(pe, i)
                    job.open(pe, i)
                    for m in range(2):
                        last = tile(PS[job.b][:, m * T:(m + 1) * T], w3(c, width), lo + m * P, H)
                    fill(job, last)

            def down(c, buf, tiles, i=None, full=None):
                c.loaded(pe, i)
                for kt in range(tiles):
                    for o in range(KT):
                        last = mm(PS[4 + o // 2][:, (o % 2) * T:(o % 2 + 1) * T],
                                  w3(c, D, tiles)[:, kt, o * P:(o + 1) * P],
                                  work[:, buf * 1024 + kt * T:buf * 1024 + (kt + 1) * T],
                                  False, full is not None and kt == tiles - 1 and o % 2 == 1)
                        if full is not None and kt == tiles - 1 and o % 2 == 1:
                            fill(full[o // 2], last)
                if full is None:
                    last.then_inc(down_used, 1)

            def feed_forward(f, L):
                for job in L["y"]:
                    job.open(pe)
                    mm(PS[job.b][:, :], zero[:], con[:, 0:2 * P].bitcast(BF16), True, False)
                pe.wait_ge(h_ready, [2, 4, 6][f])
                with pe.Fori(0, 2) as i:
                    for n in range(2):
                        for h in range(2):
                            hidden_pair(L["j"][4 * n + 2 * h], L["j"][4 * n + 2 * h + 1], L["c"][2 * n],
                                        L["c"][2 * n + 1], h * T, CH, i)
                    for n in range(2):
                        pe.wait_ge(hid_done, 2 + 11 * f + 2 * (n + 1) + i * 4)
                        down(L["c"][4 + n], n, 4, i)
                tj, tc = L["tj"], L["tc"]
                hidden_pair(tj[0], tj[1], tc[0], tc[1], 0, CH)
                hidden_pair(tj[2], tj[3], tc[0], tc[1], T, CH)
                hidden_pair(tj[4], tj[5], tc[2], tc[3], 0, CH // 2)
                pe.wait_ge(hid_done, 2 + 11 * f + 10)
                down(tc[4], 0, 4)
                pe.wait_ge(hid_done, 2 + 11 * f + 11)
                down(tc[5], 1, 2, full=L["y"])

            pe.wait_ge(small_loaded, SMALL)
            pe.wait_ge(zero_ready, 1)
            reduce_mod(0)
            norm(0, 1)
            pe.wait_ge(h_ready, 1)
            at = {12: (3, 0), 13: (3, 256), 14: (4, 0), 15: (3, 128)}
            for j in range(9):
                if j < 8:
                    sp_pair[j].open(pe)
                    for m in range(2):
                        t = 2 * j + m
                        c, lo = at.get(t, (t // 4, (t % 4) * P))
                        sp_w[c].loaded(pe)
                        last = tile(PS[sp_pair[j].b][:, m * T:(m + 1) * T], w3(sp_w[c], 280 if c == 4 else CH), lo, H)
                    fill(sp_pair[j], last)
                if j >= 1:
                    if j == 1:
                        sp_rope[0].open(pe)
                    head_sums(sp_rope[0], j - 1, j, [t for t in (2 * j - 2, 2 * j - 1) if t < 15], 15, j == 8)
            for qt in range(2):
                sp_tok[qt].open(pe)
                b = PS[sp_tok[qt].b]
                by_token(b[:, 0:P], w3(sp_w[3]), 384, P, H, qt)
                fill(sp_tok[qt], by_token(b[:, P:P + 152], w3(sp_w[4], 280), P, 152, H, qt))
            sp_w[5].loaded(pe)
            for qt in range(2):
                sp_v[qt].open(pe)
                fill(sp_v[qt], by_token(PS[sp_v[qt].b][:, :], w3(sp_w[5]), 0, CH, H, qt))
            rope(sp_rope, 0, 15, sp_const)

            pe.wait_ge(blocks_ready, 2)
            hid_job.open(pe)
            for v in range(2):
                cmp_w[v].loaded(pe)
                blk = Hl[:, 512 + 480 * v:992 + 480 * v].rearrange("p (l n) -> p l n", l=16)
                wv = wring[:, cmp_w[v].slot, :].rearrange("p (l e) -> p l e", l=16)
                for et in range(2):
                    for l2 in range(16):
                        o = v * 60 + et * 30
                        last = mm(PS[hid_job.b][:, o:o + 30], wv[:, l2, et * P:(et + 1) * P], blk[:, l2, :],
                                  l2 == 0, l2 == 15)
            fill(hid_job, last)
            hid_job.emptied(pe)
            kvc_job.open(pe)
            hid = Hl[:, 1792:1912].rearrange("p (v e n) -> p v e n", v=2, e=2)
            for et in range(2):
                mm(PS[kvc_job.b][:, 0:30], cw2[:, et * P:(et + 1) * P], hid[:, 0, et, :], et == 0, et == 1)
            pe.wait_ge(hidrep_ready, 1)
            rep = Hl[:, 512:1024].rearrange("p (e g m) -> p e g m", e=2, g=2)
            for g in range(2):
                for et in range(2):
                    last = mm(PS[kvc_job.b][:, 64 + 64 * g:128 + 64 * g], rep[:, et, g, :],
                              cw2[:, 256 + 64 * et:320 + 64 * et], et == 0, et == 1)
            fill(kvc_job, last)
            kvc_job.emptied(pe)
            pe.wait_ge(rope_done, 8)
            cs_job.open(pe)
            for par in range(2):
                for h, qt in ((h, qt) for h in range(par, 8, 2) for qt in range(2)):
                        g, jj = h // 4, h % 4
                        p0 = par * HD
                        o = ((g * 2 + qt) * 4 + jj) * 32
                        last = mm(PS[cs_job.b][:, o:o + NCMP], F[p0:p0 + HD, 8 + h // 2, qt * P:(qt + 1) * P],
                                  Hl[p0:p0 + HD, 1600 + g * NCMP:1600 + (g + 1) * NCMP])
                if par == 0:
                    last.then_inc(rows_done, 1)
                    pe.wait_ge(rows_done, 1)
            fill(cs_job, last)
            pe.wait_ge(cp_ready, 1)
            ct_job.open(pe)
            for g in range(2):
                for qt in range(2):
                    o = (g * 2 + qt) * P
                    last = pe.transpose(PS[ct_job.b][:, o:o + P], Hl[:, 1024 + o:1024 + o + P], C("ident"))
            fill(ct_job, last)
            ct_job.emptied(pe)
            pe.wait_ge(ksw_ready, 1)
            pe.wait_ge(vrows_ready, 1)
            sp_v[1].emptied(pe)
            units(sp_units, sparse_specs(), 0)
            sp_units[2][-1].emptied(pe)
            project_out(sp_out, sp_y, OT)
            norm(1, 2)
            feed_forward(0, ffn[0])
            reduce_mod(1)

            norm(2, 3)
            pe.wait_ge(h_ready, 3)
            for j in range(9):
                if j < 8:
                    if j % 2 == 0:
                        df_w[j // 2].loaded(pe)
                    df_pair[j].open(pe)
                    for m in range(2):
                        last = tile(PS[df_pair[j].b][:, m * T:(m + 1) * T], w3(df_w[j // 2]), (j % 2) * T + m * P, H)
                    fill(df_pair[j], last)
                if j >= 1:
                    if j == 1:
                        df_rope[0].open(pe)
                    head_sums(df_rope[0], j - 1, 8 + j, (2 * j - 2, 2 * j - 1), 16, j == 8)
            for n in range(4):
                df_w[4 + n // 2].loaded(pe)
                df_v[n].open(pe)
                fill(df_v[n], by_token(PS[df_v[n].b][:, :], w3(df_w[4 + n // 2]), 0, CH, H, n % 2))
            rope(df_rope, 8, 16, df_const)
            pe.wait_ge(lam_prod, 1)
            lam_job.open(pe)
            fill(lam_job, mm(PS[lam_job.b][:, 0:2], C("ones")[0:HD, :], lamt[0:HD, 0:2]))
            pe.wait_ge(rope_done, 16)
            df_v[3].emptied(pe)
            units(df_units, diff_specs(), 24)
            pe.wait_ge(sq_ready, 4)
            on_stat.open(pe)
            for t in range(KT):
                last = mm(PS[on_stat.b][0:32, 0:T], C("whole")[:, 32 - t:64 - t], H[:, t, :], t == 0, t == KT - 1)
            fill(on_stat, last)
            pe.wait_ge(rh_ready, 3)
            for j in range(4):
                on_bc[j].open(pe)
                for m in range(2):
                    t = 2 * j + m
                    last = mm(PS[on_bc[j].b][:, m * T:(m + 1) * T],
                              C("ident")[0:32, t:t + 1].to_broadcast([32, P]), rheads)
                fill(on_bc[j], last)
            on_bc[3].emptied(pe)
            project_out(df_out, df_y, OT)
            norm(3, 5)
            feed_forward(1, ffn[1])
            reduce_mod(2)

            pe.wait_ge(h_ready, 5)
            for qt in range(2):
                ml_w[0].loaded(pe)
                ml_pool[qt].open(pe)
                fill(ml_pool[qt], by_token(PS[ml_pool[qt].b][:, :], w3(ml_w[0]), 0, CH, H, qt))
            ml_w[1].loaded(pe)
            ml_lat[0].open(pe)
            for m in range(2):
                last = tile(PS[ml_lat[0].b][:, m * T:(m + 1) * T], w3(ml_w[1]), m * P, H)
            fill(ml_lat[0], last)
            pe.wait_ge(lat_ready, 1)
            UC = F[:, 8:16, :]
            for m in range(2):
                ml_lat[1 + m].open(pe)
                tile(PS[ml_lat[1 + m].b][:, 0:T], w3(ml_w[1]), (2 + m) * P, UC)
                fill(ml_lat[1 + m], tile(PS[ml_lat[1 + m].b][:, T:2 * T], w3(ml_w[1]), (2 + m) * P, H))
            ml_w[2].loaded(pe)
            ml_kr.open(pe)
            tile(PS[ml_kr.b][0:96, 0:T], w3(ml_w[2], 96), 0, UC)
            fill(ml_kr, tile(PS[ml_kr.b][0:96, T:2 * T], w3(ml_w[2], 96), 0, H))
            pe.wait_ge(proj_copied, 17)
            ml_stat[0].open(pe)
            for m in range(2):
                last = mm(PS[ml_stat[0].b][:, 0:T], C("ones"), work[:, m * T:(m + 1) * T], m == 0, m == 1)
            fill(ml_stat[0], last)
            pe.wait_ge(proj_copied, 19)
            ml_stat[1].open(pe)
            for m in range(2):
                last = mm(PS[ml_stat[1].b][:, :], C("ones"), work[:, 512 + m * 512:1024 + m * 512], m == 0, m == 1)
            fill(ml_stat[1], last)
            ml_const.loaded(pe)
            mc = aring[:, ml_const.slot, :]
            ml_pool[1].emptied(pe)
            pm = mc[:, 0:2048].rearrange("p (s g t) -> p s g t", s=2, g=4)
            for n in range(2):
                ml_d[n].open(pe)
                for m in range(2):
                    g = 2 * n + m
                    for s in range(2):
                        last = mm(PS[ml_d[n].b][:, m * T:(m + 1) * T],
                                  scr[:, 2048 + s * 512 + g * P:2048 + s * 512 + (g + 1) * P], pm[:, s, g, :],
                                  s == 0, s == 1)
                fill(ml_d[n], last)
            for n in range(2):
                ml_d[n].emptied(pe)
                ml_py[n].open(pe)
                for m in range(2):
                    g = 2 * n + m
                    last = mm(PS[ml_py[n].b][:, m * T:(m + 1) * T], mc[:, NMLAC + g * P:NMLAC + (g + 1) * P],
                              scr[:, 3072 + g * T:3072 + (g + 1) * T])
                fill(ml_py[n], last)
            pe.wait_ge(lat_ready, 2)
            ml_w[3].loaded(pe)
            qu = wring[:, ml_w[3].slot, 0:1536].rearrange("p (k n) -> p k n", k=2)
            ku = wring[:, ml_w[3].slot, 1536:3584].rearrange("p (k h n) -> p k h n", k=2, h=8)
            QL = scr[:, 0:512].rearrange("p (k t) -> p k t", k=2)
            KV = scr[:, 512:1536].rearrange("p (k t) -> p k t", k=2)
            for j in range(5):
                if j < 4:
                    ml_q[j].open(pe)
                    for m in range(2):
                        h = 2 * j + m
                        for k in range(2):
                            last = mm(PS[ml_q[j].b][0:96, m * T:(m + 1) * T], qu[:, k, h * 96:(h + 1) * 96],
                                      QL[:, k, :], k == 0, k == 1)
                    fill(ml_q[j], last)
                if j >= 1:
                    ml_qr[j - 1].open(pe)
                    ml_q[j - 1].emptied(pe)
                    fill(ml_qr[j - 1], mm(PS[ml_qr[j - 1].b][0:96, :], mc[0:96, 2048:2144],
                                          Fl[0:96, (j - 1) * 512:j * 512]))
            ml_krr.open(pe)
            ml_kr.emptied(pe)
            fill(ml_krr, mm(PS[ml_krr.b][0:96, 0:T], mc[0:96, 2048:2144], scr[0:96, 1792:2048]))
            for h in range(8):
                ml_k[h].open(pe)
                for k in range(2):
                    last = mm(PS[ml_k[h].b][0:HD, :], ku[:, k, h, 0:HD], KV[:, k, :], k == 0, k == 1)
                fill(ml_k[h], last)
            for n in range(4):
                ml_v[n].open(pe)
                for k in range(2):
                    last = mm(PS[ml_v[n].b][:, :], KV[:, k, n * P:(n + 1) * P], ku[:, k, :, HD:P], k == 0, k == 1)
                fill(ml_v[n], last)
            pe.wait_ge(rope_done, 16 + 6)
            ml_k[7].emptied(pe)
            ml_v[3].emptied(pe)
            units(ml_units, mla_specs(), 40)
            ml_units[2][-1].emptied(pe)
            ml_py[1].emptied(pe)
            project_out(ml_out, ml_y, OT)
            norm(4, 6)
            feed_forward(2, ffn[2])
            reduce_mod(3)
            norm(5, 7)

            hy_const.loaded(pe)
            hc = aring[:, hy_const.slot, :]
            o = HYC["fw"][0]
            for n in range(3):
                if n:
                    pe.wait_ge(sin_done, 2 + n)
                rows = 33 if n == 0 else 64
                src = hc[0:33, 2560:2816] if n == 0 else work[0:64, 0:T]
                hy_sin[n].open(pe)
                fill(hy_sin[n], mm(PS[hy_sin[n].b][0:64, 0:T], hc[0:rows, o + 64 * n:o + 64 * (n + 1)], src))
            pe.wait_ge(sin_done, 5)
            hy_f[1].loaded(pe)
            fo = wring[0:64, hy_f[1].slot, 0:2 * D]
            for n in range(4):
                for d in range(2):
                    hy_taps[n][d].open(pe)
                    fill(hy_taps[n][d], mm(PS[hy_taps[n][d].b][:, :], work[0:64, (n // 2) * P:(n // 2 + 1) * P],
                                           fo[:, d * D + (n % 2) * 512:d * D + (n % 2 + 1) * 512]))

            def table(name):
                return hc[:, HYC[name][0]:HYC[name][0] + 512].rearrange("p (k n) -> p k n", k=2)

            taps = [Fl[:, 0:2048].rearrange("p (k n) -> p k n", k=2), Fl[:, 2048:4096].rearrange("p (k n) -> p k n", k=2)]
            pe.wait_ge(hy_ready, 1)
            for n in range(8):
                f, h, im = n // 4, n // 2 % 2, n % 2
                hy_k[n].open(pe)
                for k in range(2):
                    last = mm(PS[hy_k[n].b][:, :], table("fs" if im else "fr")[:, k, f * P:(f + 1) * P],
                              taps[im][:, k, h * 512:(h + 1) * 512], k == 0, k == 1)
                fill(hy_k[n], last)
            for h in range(2):
                hy_n[h].open(pe)
                for k in range(2):
                    last = mm(PS[hy_n[h].b][0:1, :], hc[:, 2816:2817], taps[0][:, k, h * 512:(h + 1) * 512], k == 0, k == 1)
                fill(hy_n[h], last)
            pe.wait_ge(h_ready, 7)
            for j in range(12):
                if j % 2 == 0:
                    hy_w[j // 2].loaded(pe)
                hy_pair[j].open(pe)
                for m in range(2):
                    last = tile(PS[hy_pair[j].b][:, m * T:(m + 1) * T], w3(hy_w[j // 2]), (j % 2) * T + m * P, H)
                fill(hy_pair[j], last)
            pe.wait_ge(hy_ready, 2)
            for n in range(4):
                hy_t[n].open(pe)
                for m in range(4):
                    ct = (n % 2) * 4 + m
                    last = pe.transpose(PS[hy_t[n].b][:, m * P:(m + 1) * P],
                                        F[:, 16 + ct, (n // 2) * P:(n // 2 + 1) * P], C("ident"))
                fill(hy_t[n], last)
            hy_t[3].emptied(pe)
            vt = Hl.rearrange("p (k n) -> p k n", k=2)
            for h in range(2):
                for n in range(4):
                    f, im = n // 2, n % 2
                    job = hy_vs[h][n]
                    job.open(pe)
                    for k in range(2):
                        last = mm(PS[job.b][:, :], table("fi" if im else "fr")[:, k, f * P:(f + 1) * P],
                                  vt[:, k, h * 512:(h + 1) * 512], k == 0, k == 1)
                    fill(job, last)
            for h in range(2):
                pe.wait_ge(spec_ready, h + 1)
                re, im = spectrum(h)
                for n in range(2):
                    job = hy_y[h][n]
                    job.open(pe)
                    for m in range(2):
                        lo = (2 * n + m) * P
                        parts = [(s, g, f) for f in range(2) for s, g in ((re, "gr"), (im, "gi"))]
                        for q, (s, g, f) in enumerate(parts):
                            last = mm(PS[job.b][:, m * T:(m + 1) * T], s[:, f, lo:lo + P], table(g)[:, f, :], q == 0, q == 3)
                    fill(job, last)
            pe.wait_ge(hy_ready, 3)
            project_out(hy_out, hy_yo, F)
            norm(6, 8)

            pe.wait_ge(h_ready, 8)
            rt_job.open(pe)
            for qt in range(2):
                for k in range(KT):
                    last = mm(PS[7][:, qt * 8:qt * 8 + 8], H[:, k, qt * P:(qt + 1) * P], rw[:, k, :], k == 0, k == KT - 1)
            fill(rt_job, last)
            for n in range(4):
                zt_job[n].open(pe)
                for m in range(4):
                    k = (n % 2) * 4 + m
                    last = pe.transpose(PS[zt_job[n].b][:, m * P:(m + 1) * P], H[:, k, (n // 2) * P:(n // 2 + 1) * P], C("ident"))
                fill(zt_job[n], last)
            pe.wait_ge(route_ready, 1)
            pos_job.open(pe)
            mm(PS[7][:, 0:8], R("before"), ch8[:, 0, :])
            for o, lhs in ((8, R("before")), (16, C("ones"))):
                mm(PS[7][:, o:o + 8], C("ones"), ch8[:, 0, :], True, False)
                last = mm(PS[7][:, o:o + 8], lhs, ch8[:, 1, :], False, True)
            fill(pos_job, last)
            zt_job[3].emptied(pe)

            def experts(M):
                J_, K_ = M["j"], M["c"]
                ztok = V[:].rearrange("p (t n) -> p t n", t=2)
                with pe.Fori(0, NE // 2) as i:
                    for e in range(2):
                        pe.wait_ge(M["sel"], 2 * i + e + 1)
                        for q in range(2):
                            job = J_["gather", e, q]
                            job.open(pe, i)
                            for m in range(4):
                                for t in range(2):
                                    last = mm(PS[7][:, m * P:(m + 1) * P], ztok[:, t, (4 * q + m) * P:(4 * q + m + 1) * P],
                                              sel(e)[:, t, :], t == 0, t == 1)
                            fill(job, last)
                        job = J_["st", e]
                        job.open(pe, i)
                        pe.wait_ge(M["wsel"], 2 * i + e + 1)
                        for t in range(2):
                            last = pe.transpose(PS[7][:, t * P:(t + 1) * P], wsel(e)[:, t, :], C("ident"))
                        fill(job, last)
                    for name in moe_sequence():
                        kind, g = name[0], name[1]
                        if kind == "gu":
                            if g % 7 == 0:
                                J_["gather", g // 7, 1].emptied(pe, i)
                            for w in ("g", "u"):
                                K_[w, g].loaded(pe, i)
                                J_[w, g].open(pe, i)
                                for k in range(KT):
                                    last = mm(PS[J_[w, g].b][:, :], gathered(g // 7)[:, k, :], w3(K_[w, g])[:, k, :],
                                              k == 0, k == KT - 1)
                                fill(J_[w, g], last)
                        elif kind == "t":
                            J_["t", g].open(pe, i)
                            pe.wait_ge(M["hid"], 14 * i + g + 1)
                            for m in range(4):
                                last = pe.transpose(PS[4][:, m * P:(m + 1) * P],
                                                    work[:, (g % 2) * 512 + m * P:(g % 2) * 512 + (m + 1) * P], C("ident"))
                            fill(J_["t", g], last)
                        elif kind == "d":
                            e = g // 7
                            y = J_["y", e, 0], J_["y", e, 1]
                            if g % 7 == 0:
                                y[0].open(pe, i)
                                y[1].open(pe, i)
                            K_["d", g].loaded(pe, i)
                            J_["t", g].emptied(pe, i)
                            ht = work[:, 1024 + (g % 2) * 512:1536 + (g % 2) * 512].rearrange("p (k n) -> p k n", k=4)
                            for k in range(4):
                                for h in range(2):
                                    last = mm(PS[5 + h][:, :], ht[:, k, :], w3(K_["d", g], D, 4)[:, k, h * 512:(h + 1) * 512],
                                              g % 7 == 0 and k == 0, g % 7 == 6 and k == 3)
                                    if g % 7 == 6 and k == 3:
                                        fill(y[h], last)
                            if g % 7 != 6:
                                last.then_inc(M["used"], 1)
                        else:
                            e, q = name[1], name[2]
                            job = J_["s", e, q]
                            job.open(pe, i)
                            if q == 0:
                                J_["y", e, 1].emptied(pe, i)
                                J_["st", e].emptied(pe, i)
                            for m in range(2):
                                k = 2 * q + m
                                last = mm(PS[7][:, m * T:(m + 1) * T], ye[:, k * P:(k + 1) * P], spread_sel(e))
                            fill(job, last)

            experts(moe)
            pe.wait_ge(flag_ready, 1)
            with pe.If(pe.value_load(flag[0:1, 0:1], min_val=0, max_val=1) > 0):
                for job in (moe["j"]["s", 1, 3], moe["j"]["y", 1, 1], moe["j"]["t", 13], moe["j"]["u", 13], moe["j"]["u", 12]):
                    job.emptied(pe, NE // 2 - 1)
                experts(moe2)
            norm(7, 9)

        @block.scalar
        def _(act):
            def copy(dst, src, **kw):
                return act.activation(dst, src, ACT.Copy, **kw)

            def root(dst, src, n, eps):
                return act.activation(dst, src, ACT.Sqrt, bias=eps, scale=1.0 / n)

            def norm(n, eps="rms_eps"):
                norm_job[n][-1].filled(act)
                root(rstd[:], PS[6][:, 0:T], D, C(eps)).then_inc(norm_job[n][-1].bank.free, 1)

            def project(jobs, base, tiles):
                for j, job in enumerate(jobs):
                    job.filled(act)
                    if j >= 2:
                        act.wait_ge(stat_summed, (7 if base else 0) + j - 1)
                    n = min(2, tiles - 2 * j) * T
                    sq = act.activation(work[:, (j % 2) * 512:(j % 2) * 512 + n], PS[job.b][:, 0:n], ACT.Square)
                    sq.then_inc(proj_copied, 1)
                    copy(Fl[:, j * 512:(j + 1) * 512], PS[job.b][:, :]).then_inc(job.bank.free, 1)

            def head_root(job, n, rows=32):
                job.filled(act)
                root(rheads[0:rows, :], PS[job.b][0:rows, 0:T], n, C("rms_eps", rows)).then_inc(job.bank.free, 1)

            def units(plan, specs, base, place, pv_base):
                s, t, o = plan
                pv = pv_base
                for i in range(len(specs) + 2):
                    if i < len(specs):
                        sp_ = specs[i]
                        b = i % 2
                        act.wait_ge(nmax_ready, base + i + 1)
                        for n, (lo, hi, r) in enumerate(sp_["rows"]):
                            last = act.activation(work[:, 1024 + b * 512 + lo:1024 + b * 512 + hi],
                                                  work[:, b * 512 + lo:b * 512 + hi], ACT.Exp,
                                                  bias=nmax[:, b, r:r + 1], accum_out=ssum[:, b, r:r + 1])
                        last.then_inc(exp_done, 1)
                    if 0 <= i - 1 < len(specs):
                        u = i - 1
                        t[u].filled(act)
                        if u >= 2:
                            sp_ = specs[u - 2]
                            if sp_["last"]:
                                o[sp_["out"]].filled(act)
                            else:
                                pv += 1
                                act.wait_ge(pv_done, pv)
                        w = specs[u]["width"]
                        copy(work[:, 2048 + (u % 2) * 512:2048 + (u % 2) * 512 + w],
                             PS[t[u].b][:, 0:w]).then_inc(t[u].bank.free, 1)
                    if i >= 2 and specs[i - 2]["last"]:
                        h = specs[i - 2]["out"]
                        o[h].filled(act)
                        dst = place(h)
                        copy(dst, PS[o[h].b][0:dst.shape[0], 0:T]).then_inc(o[h].bank.free, 1)

            def feed_forward(f, L):
                def silu(job, n, i=None):
                    job.filled(act, i)
                    act.wait_ge(hid_done, 11 * f + n + 1 if i is None else i * 4 + (11 * f + n + 1))
                    act.activation(work[:, 2048 + (n % 2) * 512:2560 + (n % 2) * 512], PS[job.b][:, :],
                                   ACT.Silu).then_inc(job.bank.free, 1)

                with act.Fori(0, 2) as i:
                    for n in range(4):
                        silu(L["j"][2 * n], n, i)
                for n in range(3):
                    silu(L["tj"][2 * n], 8 + n)

            act.wait_ge(small_loaded, SMALL)
            act.activation(cs[:], vec[:, 0:24], ACT.Silu).then_inc(cs_ready, 1)
            for n in range(2):
                act.wait_ge(sin_arg, n + 1)
                if n == 0:
                    act.activation(sinT, work[:, 0:T], ACT.Sin).then_inc(sin_done, 1)
                else:
                    act.activation(cosT, work[:, T:2 * T], ACT.Sin, bias=C("half_pi"), scale=-1.0).then_inc(sin_done, 1)
            norm(0)
            project(sp_pair, 0, 15)
            head_root(sp_rope[0], HD)
            act.wait_ge(gate_raw, 2)
            act.activation(gates[:], gates[:], ACT.Sigmoid).then_inc(gates_ready, 1)
            sp_v[1].filled(act)
            sp_pair[7].emptied(act)
            for par in range(2):
                for g in range(2):
                    for half in range(2):
                        last = copy(*window(par, g, half, 1))
            last.then_inc(windows_ready, 1)
            hid_job.filled(act)
            act.activation(Hl[:, 1792:1912], PS[hid_job.b][:, 0:120], ACT.Silu).then_inc(hid_job.bank.free, 1)
            kvc_job.filled(act)
            copy(Hl[:, 1600:1630], PS[kvc_job.b][:, 0:30])
            copy(Hl[:, 1632:1760], PS[kvc_job.b][:, 64:192]).then_inc(kvc_job.bank.free, 1)
            act.wait_ge(cshift, 1)
            cexp_view = Hl[:, 1024:1536].rearrange("p (a n) -> p a n", a=16)[:, :, 0:NCMP]
            act.activation(cexp_view, cexp_view, ACT.Exp).then_inc(cexp, 1)
            ct_job.filled(act)
            copy(Hl[:, 512:1024], PS[ct_job.b][:, :]).then_inc(ct_job.bank.free, 1)
            units(sp_units, sparse_specs(), 0, heads_to, 0)
            norm(1)
            feed_forward(0, ffn[0])

            norm(2)
            project(df_pair, 8, 16)
            head_root(df_rope[0], HD)
            lam_job.filled(act)
            act.activation(lamt[:, 0:2], PS[lam_job.b][:, 0:2], ACT.Exp).then_inc(lam_job.bank.free, 1)
            units(df_units, diff_specs(), 24, lambda h: OT[:, h, :], 8)
            head_root(on_stat, P)
            norm(3)
            feed_forward(1, ffn[1])

            for qt in range(2):
                ml_pool[qt].filled(act)
                copy(scr[:, 2048 + qt * 512:2560 + qt * 512], PS[ml_pool[qt].b][:, :]).then_inc(ml_pool[qt].bank.free, 1)
            for n, dst in ((0, 0), (1, 512), (2, 1024)):
                job = ml_lat[n]
                job.filled(act)
                act.activation(work[:, dst:dst + 512], PS[job.b][:, :], ACT.Square).then_inc(proj_copied, 1)
                copy(scr[:, dst:dst + 512], PS[job.b][:, :]).then_inc(job.bank.free, 1)
            ml_kr.filled(act)
            copy(scr[0:96, 1536:2048], PS[ml_kr.b][0:96, :]).then_inc(ml_kr.bank.free, 1)
            for n, (lo, w) in enumerate(((1536, T), (1792, 512))):
                ml_stat[n].filled(act)
                root(work[:, lo:lo + w], PS[ml_stat[n].b][:, 0:w], 256, C("rms_eps")).then_inc(ml_stat[n].bank.free, 1)
            for n in range(2):
                ml_d[n].filled(act)
                copy(scr[:, 3072 + n * 512:3584 + n * 512], PS[ml_d[n].b][:, :]).then_inc(ml_d[n].bank.free, 1)
            for j in range(4):
                ml_q[j].filled(act)
                copy(Fl[0:96, j * 512:(j + 1) * 512], PS[ml_q[j].b][0:96, :]).then_inc(ml_q[j].bank.free, 1)
            for h in range(8):
                ml_k[h].filled(act)
                copy(Fl[0:HD, 2048 + h * 512:2560 + h * 512], PS[ml_k[h].b][0:HD, :]).then_inc(ml_k[h].bank.free, 1)
            for n in range(4):
                ml_v[n].filled(act)
                copy(V[:, n * 512:(n + 1) * 512], PS[ml_v[n].b][:, :]).then_inc(ml_v[n].bank.free, 1)
            units(ml_units, mla_specs(), 40, lambda h: heads_to(8 + h), 16)
            norm(4, "ln_eps")
            feed_forward(2, ffn[2])
            norm(5, "ln_eps")

            for n in range(3):
                act.wait_ge(sin_arg, 3 + n)
                act.activation(work[0:64, 0:T], work[0:64, T:2 * T], ACT.Sin).then_inc(sin_done, 1)
            for n in range(8):
                hy_k[n].filled(act)
                f, h, im = n // 4, n // 2 % 2, n % 2
                dst = (V if im else OTl)[:, f * 1024 + h * 512:f * 1024 + (h + 1) * 512]
                copy(dst, PS[hy_k[n].b][:, :]).then_inc(hy_k[n].bank.free, 1)
            for h in range(2):
                hy_n[h].filled(act)
                copy(scr[0:1, h * 512:(h + 1) * 512], PS[hy_n[h].b][0:1, :]).then_inc(hy_n[h].bank.free, 1)
            for j in range(12):
                hy_pair[j].filled(act)
                for m in range(2):
                    t = 2 * j + m
                    last = act.activation(F[:, t, :], PS[hy_pair[j].b][:, m * T:(m + 1) * T], ACT.Identity,
                                          bias=vc("conv_b", t), scale=vc("conv_w", 24 + t))
                last.then_inc(zconv, 1)
            for n in range(4):
                hy_t[n].filled(act)
                copy(Hl[:, n * 512:(n + 1) * 512], PS[hy_t[n].b][:, :]).then_inc(hy_t[n].bank.free, 1)
            for h in range(2):
                for n in range(4):
                    hy_vs[h][n].filled(act)
                    copy(spectrum(h)[n % 2][:, n // 2, :], PS[hy_vs[h][n].b][:, :]).then_inc(hy_vs[h][n].bank.free, 1)
            norm(6, "ln_eps")

            act.wait_ge(rt_ready, 1)
            act.activation(pw[:], pw[:], ACT.Exp).then_inc(rt_exp, 1)
            for n in range(4):
                zt_job[n].filled(act)
                copy(V[:, n * 512:(n + 1) * 512], PS[zt_job[n].b][:, :]).then_inc(zt_job[n].bank.free, 1)

            def experts(M):
                J_ = M["j"]
                with act.Fori(0, NE // 2) as i:
                    for e in range(2):
                        for q in range(2):
                            job = J_["gather", e, q]
                            job.filled(act, i)
                            copy(gathered(e)[:, 4 * q:4 * q + 4, :].rearrange("p k n -> p (k n)"),
                                 PS[7][:, :]).then_inc(job.bank.free, 1)
                        job = J_["st", e]
                        job.filled(act, i)
                        copy(spread_sel(e), PS[7][:, 0:T]).then_inc(job.bank.free, 1)
                    for g in range(15):
                        if g < 14:
                            J_["g", g].filled(act, i)
                            act.wait_ge(M["hid"], 14 * i + g - 1) if g >= 2 else None
                            act.activation(work[:, 2048 + (g % 2) * 512:2560 + (g % 2) * 512], PS[g % 2][:, :],
                                           ACT.Silu).then_inc(J_["g", g].bank.free, 1)
                        if g >= 1:
                            J_["t", g - 1].filled(act, i)
                            copy(work[:, 1024 + ((g - 1) % 2) * 512:1536 + ((g - 1) % 2) * 512],
                                 PS[4][:, :]).then_inc(J_["t", g - 1].bank.free, 1)
                        if g in (8, 14):
                            e = 0 if g == 8 else 1
                            for h in range(2):
                                J_["y", e, h].filled(act, i)
                                copy(ye[:, h * 512:(h + 1) * 512], PS[5 + h][:, :]).then_inc(J_["y", e, h].bank.free, 1)

            experts(moe)
            act.wait_ge(flag_ready, 1)
            with act.If(act.value_load(flag[0:1, 0:1], min_val=0, max_val=1) > 0):
                experts(moe2)
            norm(7, "ln_eps")

        @block.vector
        def _(ve):
            turned = [0]
            step = Steps(ve, dve_step)

            def tt(dst, x, y, op):
                return ve.tensor_tensor(dst, x, y, op)

            def ts(dst, x, s1, op0, s2=None, op1=None):
                return ve.tensor_scalar(dst, x, s1, s2, op0, op1) if op1 is not None else ve.tensor_scalar(
                    dst, x, s1, None, op0)

            def stt(dst, x, s, y, op0, op1):
                return ve.scalar_tensor_tensor(out=dst, in0=x, scalar=s, in1=y, op0=op0, op1=op1)

            def reduced(dst, src, out, rows=P):
                step(ts(dst, src, 1.0 / TWO_PI, ALU.mult, MAGIC, ALU.add))
                step(ts(dst, dst, -MAGIC, ALU.add))
                turns = spare[0:rows, :]
                step(ve.tensor_copy(turns, dst))
                step(stt(dst, turns, -PI_A, src, ALU.mult, ALU.add))
                step(stt(dst, turns, -PI_B, dst, ALU.mult, ALU.add))
                step(stt(dst, turns, -PI_C, dst, ALU.mult, ALU.add))
                ts(dst, dst, PI_CLAMP, ALU.min, -PI_CLAMP, ALU.max).then_inc(out, 1)

            def add_chunk(slot, dst, cvec, counts, final, i=None):
                w = aring[:, slot, :].rearrange("p (k n) -> p k n", k=KT)
                at, stride = counts
                for k in range(KT):
                    if k:
                        ve.wait_ge(ada_step, at + k if i is None else i * stride + (at + k))
                    ins = (ts(dst, w[:, k, :], cvec[:, k:k + 1], ALU.mult) if k == 0 else
                           stt(dst, w[:, k, :], cvec[:, k:k + 1], dst, ALU.mult, ALU.add))
                    ins.then_inc(ada_step if k < KT - 1 else final, 1)

            def take_mod(layer):
                job = mod_job[layer]
                job.filled(ve)
                b = vec[:, VEC["ada_b"][0] + 48 * layer:VEC["ada_b"][0] + 48 * (layer + 1)]
                if layer == 2:
                    step(tt(modc[:], PS[job.b][:, 64:80], b[:, 0:16], ALU.add))
                tt(mod[:, layer, :], PS[job.b][:, 0:48], b, ALU.add).then_inc(job.bank.free, 1)
                job.emptied(ve)

            def scale_of(layer, sc, gain):
                step(stt(gsc[:], mod[:, layer, sc:sc + 8], 1.0, gain, ALU.add, ALU.mult))

            def rms(n, layer, sc, gain, sh, sq):
                tt(H[:], X[:], X[:], ALU.mult).then_inc(sq_ready, 1)
                scale_of(layer, sc, gain)
                norm_job[n][-1].emptied(ve)
                ve.wait_ge(sq_ready, sq)
                step(ve.reciprocal(rstd[:], rstd[:]))
                step(tt(H[:], X[:], rstd[:].unsqueeze(1).to_broadcast([P, KT, T]), ALU.mult))
                for k in range(KT):
                    last = ts(H[:, k, :], H[:, k, :], gsc[:, k:k + 1], ALU.mult, mod[:, layer, sh + k:sh + k + 1], ALU.add)
                last.then_inc(h_ready, 1)

            def layer_norm(n, ln, sq):
                mean, var = norm_job[n]
                mean.filled(ve)
                stt(X[:], PS[mean.b][:, 0:T].unsqueeze(1).to_broadcast([P, KT, T]), -1.0 / D, X[:],
                    ALU.mult, ALU.add).then_inc(mean.bank.free, 1)
                mean.emptied(ve)
                tt(H[:], X[:], X[:], ALU.mult).then_inc(sq_ready, 1)
                var.emptied(ve)
                step(ve.reciprocal(rstd[:], rstd[:]))
                step(tt(X[:], X[:], rstd[:].unsqueeze(1).to_broadcast([P, KT, T]), ALU.mult))
                for k in range(KT):
                    o = ln * 8 + k
                    last = ts(X[:, k, :], X[:, k, :], vc("ln_g", o), ALU.mult, vc("ln_b", o), ALU.add)
                last.then_inc(x_ready, 1)

            def modulate(dst, src, m, sc, sh, signal, count):
                step(ts(gsc[:], m[:, sc:sc + 8], 1.0, ALU.add))
                for k in range(KT):
                    last = ts(dst[:, k, :], src[:, k, :], gsc[:, k:k + 1], ALU.mult, m[:, sh + k:sh + k + 1], ALU.add)
                last.then_inc(signal, 1)
                ve.wait_ge(signal, count)

            def residual(jobs, layer, g, signal):
                for j, job in enumerate(jobs):
                    job.filled(ve)
                    for m in range(2):
                        k = 2 * j + m
                        last = stt(X[:, k, :], PS[job.b][:, m * T:(m + 1) * T], mod[:, layer, g + k:g + k + 1],
                                   X[:, k, :], ALU.mult, ALU.add)
                    last.then_inc(job.bank.free, 1)
                jobs[-1].emptied(ve)
                if signal is not None:
                    ve.tensor_copy(mx8[:, 0, 0:1], mx8[:, 0, 0:1]).then_inc(signal, 1)

            def rope(rp, pairs, gains, base, tiles):
                stat, bc, ro = rp
                stat.emptied(ve)
                step(ve.reciprocal(rheads, rheads))
                ve.tensor_copy(mx8[:, 0, 0:1], mx8[:, 0, 0:1]).then_inc(rh_ready, 1)
                pairs[-1].emptied(ve)
                for j in range(9):
                    if j < 8:
                        bc[j].filled(ve)
                        for m in range(2):
                            t = 2 * j + m
                            if t < tiles:
                                last = stt(F[:, t, :], F[:, t, :], gains(t), PS[bc[j].b][:, m * T:(m + 1) * T],
                                           ALU.mult, ALU.mult)
                        last.then_inc(bc[j].bank.free, 1)
                    if j >= 1:
                        n = min(2, tiles - 2 * (j - 1))
                        turn(F[:, 2 * j - 2:2 * j - 2 + n, :], ro[j - 1], cosT, sinT, n, P)

            def turn(x, job, cos, sin, n, rows):
                t1 = work[0:rows, 2048:2048 + n * T].rearrange("p (a t) -> p a t", a=n)
                t2 = work[0:rows, 2560:2560 + n * T].rearrange("p (a t) -> p a t", a=n)
                job.filled(ve)
                if turned[0]:
                    ve.wait_ge(rope_done, turned[0])
                turned[0] += 1
                tt(t1, x, cos.unsqueeze(1).to_broadcast([rows, n, T]), ALU.mult)
                ps = PS[job.b][0:rows, 0:n * T].rearrange("p (a t) -> p a t", a=n)
                tt(t2, ps, sin.unsqueeze(1).to_broadcast([rows, n, T]), ALU.mult).then_inc(job.bank.free, 1)
                job.emptied(ve)
                tt(x, t1, t2, ALU.add).then_inc(rope_done, 1)

            def units(plan, specs, base):
                s, _, _ = plan
                for i in range(len(specs) + 1):
                    if i < len(specs):
                        sp_, b = specs[i], i % 2
                        w = sp_["width"]
                        dst = work[:, b * 512:b * 512 + w]
                        s[i].filled(ve)
                        if sp_["mask"] is not None:
                            stt(dst, PS[s[i].b][:, 0:w], sp_["scale"], sp_["mask"], ALU.mult, ALU.add).then_inc(s[i].bank.free, 1)
                        else:
                            ts(dst, PS[s[i].b][:, 0:w], sp_["scale"], ALU.mult).then_inc(s[i].bank.free, 1)
                        s[i].emptied(ve)
                        for lo, hi, r in sp_["rows"]:
                            last = ve.tensor_reduce(nmax[:, b, r:r + 1], work[:, b * 512 + lo:b * 512 + hi], AX.X,
                                                    ALU.max, negate=True)
                        last.then_inc(nmax_ready, 1)
                    if i >= 1:
                        u = i - 1
                        sp_, b = specs[u], u % 2
                        ve.wait_ge(exp_done, base + u + 1)
                        n = len(sp_["rows"])
                        step(ve.reciprocal(fac[:, b, 0:n], ssum[:, b, 0:n]))
                        if sp_["factor"] is not None:
                            step(tt(fac[:, b, 0:n], fac[:, b, 0:n], sp_["factor"], ALU.mult))
                        for lo, hi, r in sp_["rows"]:
                            x = work[:, 1024 + b * 512 + lo:1024 + b * 512 + hi]
                            last = ts(x, x, fac[:, b, r:r + 1], ALU.mult)
                        last.then_inc(p_ready, 1)

            def feed_forward(f, L, layer):
                two = f == 1
                cvec = cs[:, 0:8] if f == 0 else cs[:, 8:16]
                s0 = 84 + f * 84 + (32 if f == 2 else 0)

                def product(n, job, dst, i=None):
                    job.filled(ve, i)
                    gate = L_gate[n]
                    gate.emptied(ve, i)
                    tt(work[:, dst:dst + 512], work[:, 2048 + (n % 2) * 512:2560 + (n % 2) * 512], PS[job.b][:, :],
                       ALU.mult).then_inc(job.bank.free, 1)
                    job.emptied(ve, i)
                    ve.tensor_copy(mx8[:, 0, 0:1], mx8[:, 0, 0:1]).then_inc(hid_done, 1)

                L_gate = {n: L["j"][2 * n] for n in range(4)} | {8 + n: L["tj"][2 * n] for n in range(3)}
                with ve.Fori(0, 2) as i:
                    for n in range(4):
                        product(n, L["j"][2 * n + 1], (n // 2) * 1024 + (n % 2) * 512, i)
                        c = L["a"][n]
                        c.loaded(ve, i)
                        add_chunk(c.slot, Fl[:, bass.ds(i * 4 * CH + (4 + n) * CH, CH)], cvec,
                                  (s0 + 7 * n, 28), ada_used, i)
                at = s0 + 56
                for n in range(4):
                    if n < 3:
                        product(8 + n, L["tj"][2 * n + 1], (n // 2) * 1024 + (n % 2) * 512)
                    c = L["ta"][n]
                    c.loaded(ve)
                    if two:
                        add_chunk(c.slot, OTl[:, n * CH:(n + 1) * CH], cs[:, 16:24], (at, 0), ada_step)
                        at += 8
                    add_chunk(c.slot, Fl[:, n * CH:(n + 1) * CH], cvec, (at, 0), ada_used)
                    at += 7

            ve.memset(zero[:], 0.0).then_inc(zero_ready, 1)
            ve.memset(mx8[:], 0.0)
            for _ in range(2):
                ve.sem_inc(hid_done, 1)
            for b in banks2:
                ve.sem_inc(b.free, 1)
            ve.wait_ge(small_loaded, SMALL)
            step(ve.tensor_copy(rstd[:], posi))
            step(ts(rstd[:], rstd[:], C("invf"), ALU.mult))
            reduced(work[:, 0:T], rstd[:], sin_arg)
            ve.wait_ge(sin_arg, 1)
            stt(work[:, T:2 * T], work[:, 0:T], -1.0, work[:, 0:T], ALU.mult, ALU.max).then_inc(sin_arg, 1)
            tt(lamt[0:HD, 0:1], vc("lam", 0, HD), vc("lam", 1, HD), ALU.mult)
            tt(lamt[0:HD, 1:2], vc("lam", 2, HD), vc("lam", 3, HD), ALU.mult).then_inc(lam_prod, 1)
            step(ts(ogain[:], vc("out_norm"), 1.0 - LAM_INIT, ALU.mult))
            ve.wait_ge(cs_ready, 1)
            with ve.Fori(0, 6) as i:
                for n in range(2):
                    ada0[n].loaded(ve, i)
                    add_chunk(ada0[n].slot, Fl[:, bass.ds(i * 2 * CH + n * CH, CH)], cs[:, 0:8], (7 * n, 14), ada_used, i)

            take_mod(0)
            rms(0, 0, 8, vec[:, VEC["attn_norm"][0]:VEC["attn_norm"][0] + 8], 0, 1)
            ve.wait_ge(sin_done, 2)
            for qt in range(2):
                sp_tok[qt].filled(ve)
                ve.tensor_copy(V[:, qt * 1024 + 512:qt * 1024 + 768], PS[sp_tok[qt].b][:, 0:256])
                ve.tensor_copy(gates[:, qt, :], PS[sp_tok[qt].b][:, 256:280]).then_inc(sp_tok[qt].bank.free, 1)
            sp_tok[1].emptied(ve)
            ve.tensor_copy(mx8[:, 0, 0:1], mx8[:, 0, 0:1]).then_inc(gate_raw, 2)
            for qt in range(2):
                sp_v[qt].filled(ve)
                ve.tensor_copy(V[:, qt * 1024:qt * 1024 + 512], PS[sp_v[qt].b][:, :]).then_inc(sp_v[qt].bank.free, 1)
            sp_gain = ["moba_q"] * 4 + ["moba_k"] * 4 + ["nsa_q"] * 4
            rope(sp_rope, sp_pair, lambda t: vc(sp_gain[t]) if t < 12 else vc("nsa_k", t - 12), 0, 15)
            ve.wait_ge(rope_done, 8)
            for par in range(2):
                for g in range(2):
                    for half in range(2):
                        last = ve.tensor_copy(*window(par, g, half, 0))
            step(last)
            ve.wait_ge(windows_ready, 1)
            for v in range(2):
                blk = Hl[:, 512 + 480 * v:992 + 480 * v].rearrange("p (l n) -> p l n", l=16)
                pos = vc("pos_v" if v else "pos_k", n=16).unsqueeze(2).to_broadcast([P, 16, 30])
                tt(blk, blk, pos, ALU.add).then_inc(blocks_ready, 1)
            for b in range(2):
                ve.tensor_copy(Hl[0:HD, b * T:(b + 1) * T], F[HD:P, 13 + b, :])
                last = ve.tensor_copy(Hl[HD:P, b * T:(b + 1) * T], F[0:HD, 13 + b, :])
            last.then_inc(ksw_ready, 1)
            hid_job.emptied(ve)
            rep = Hl[:, 512:1024].rearrange("p (e g j n) -> p e g j n", e=2, g=2, j=4)
            hid = Hl[:, 1792:1912].rearrange("p (v e g n) -> p v e g n", v=2, e=2, g=2)
            step(ve.memset(Hl[:, 512:1536], 0.0))
            for et in range(2):
                for g in range(2):
                    last = ve.tensor_copy(rep[:, et, g, :, 0:NCMP], hid[:, 1, et, g, :].unsqueeze(1).to_broadcast([P, 4, NCMP]))
            last.then_inc(hidrep_ready, 1)
            cs_job.filled(ve)
            pc5 = Hl[:, 1024:1536].rearrange("p (g t j n) -> p g t j n", g=2, t=2, j=4)
            ps5 = PS[cs_job.b][:, :].rearrange("p (g t j n) -> p g t j n", g=2, t=2, j=4)
            pc3 = Hl[:, 1024:1536].rearrange("p (a n) -> p a n", n=32)[:, :, 0:NCMP]

            def by_block(name, t):
                return C(name)[:, t * NCMP:(t + 1) * NCMP].unsqueeze(1).to_broadcast([P, 4, NCMP])

            for g in range(2):
                for t in range(2):
                    last = stt(pc5[:, g, t, :, 0:NCMP], ps5[:, g, t, :, 0:NCMP], HD ** -0.5, by_block("cmask", t), ALU.mult, ALU.add)
            last.then_inc(cs_job.bank.free, 1)
            cs_job.emptied(ve)
            step(ve.tensor_reduce(cst[:, 0, :], pc3, AX.X, ALU.max, negate=True))
            tt(pc3, pc3, cst[:, 0, :].unsqueeze(2).to_broadcast([P, 16, NCMP]), ALU.add).then_inc(cshift, 1)
            ve.wait_ge(cexp, 1)
            step(ve.tensor_reduce(cst[:, 0, :], pc3, AX.X, ALU.add))
            step(ve.reciprocal(cst[:, 0, :], cst[:, 0, :]))
            ve.wait_ge(gates_ready, 1)
            cst4 = cst[:, 0, :].rearrange("p (g t j) -> p g t j", g=2, t=2)
            gv = gates[:, :, 0:8].rearrange("p t (g j) -> p g t j", g=2)
            step(tt(cst4, cst4, gv, ALU.mult))
            step(tt(pc3, pc3, cst[:, 0, :].unsqueeze(2).to_broadcast([P, 16, NCMP]), ALU.mult))
            for g in range(2):
                for t in range(2):
                    last = tt(pc5[:, g, t, :, 0:NCMP], pc5[:, g, t, :, 0:NCMP], by_block("cvalid", t), ALU.mult)
            last.then_inc(cp_ready, 1)
            ct_job.filled(ve)
            step(ve.memset(Hl[:, 1024:1536], 0.0))
            vrows = Hl[:, 1024:1536].rearrange("p (g j d) -> p g j d", g=2, j=4)
            for jj in range(4):
                r = 32 * jj
                last = ve.tensor_copy(vrows[r:r + 32, :, jj, :],
                                      Hl[r:r + 32, 1632:1760].rearrange("p (g d) -> p g d", g=2))
            last.then_inc(vrows_ready, 1)
            units(sp_units, sparse_specs(), 0)
            residual(sp_y, 0, 16, None)
            rms(1, 0, 32, vec[:, VEC["ffn_norm"][0]:VEC["ffn_norm"][0] + 8], 24, 2)
            feed_forward(0, ffn[0], 0)
            residual(ffn[0]["y"], 0, 40, None)
            take_mod(1)

            rms(2, 1, 8, vec[:, VEC["attn_norm"][0] + 8:VEC["attn_norm"][0] + 16], 0, 3)
            for n in range(4):
                df_v[n].filled(ve)
                o = (n % 2) * 1024 + (n // 2) * 512
                ve.tensor_copy(V[:, o:o + 512], PS[df_v[n].b][:, :]).then_inc(df_v[n].bank.free, 1)
            rope(df_rope, df_pair, lambda t: vc("diff_q" if t < 8 else "diff_k"), 8, 16)
            lam_job.emptied(ve)
            step(tt(lamt[:, 2:3], lamt[:, 1:2], lamt[:, 0:1], ALU.subtract))
            step(ts(lamt[:, 3:4], lamt[:, 2:3], -LAM_INIT, ALU.add))
            units(df_units, diff_specs(), 24)
            df_units[2][-1].emptied(ve)
            tt(H[:], OT[:], OT[:], ALU.mult).then_inc(sq_ready, 1)
            on_stat.emptied(ve)
            step(ve.reciprocal(rheads, rheads))
            ve.tensor_copy(mx8[:, 0, 0:1], mx8[:, 0, 0:1]).then_inc(rh_ready, 1)
            for j in range(4):
                on_bc[j].filled(ve)
                for m in range(2):
                    t = 2 * j + m
                    last = stt(OT[:, t, :], OT[:, t, :], ogain[:], PS[on_bc[j].b][:, m * T:(m + 1) * T], ALU.mult, ALU.mult)
                last.then_inc(on_bc[j].bank.free, 1)
            residual(df_y, 1, 16, None)
            rms(3, 1, 32, vec[:, VEC["ffn_norm"][0] + 8:VEC["ffn_norm"][0] + 16], 24, 5)
            feed_forward(1, ffn[1], 1)
            residual(ffn[1]["y"], 1, 40, None)
            take_mod(2)

            modulate(H, X, mod[:, 2, :], 8, 0, h_ready, 5)
            ve.wait_ge(ctx_loaded, 16)
            modulate(F[:, 8:16, :], F[:, 16:24, :], modc[:], 8, 0, lat_ready, 1)
            step(ts(X[:], X[:], ALPHA, ALU.mult))
            ml_stat[1].emptied(ve)
            step(ve.reciprocal(work[:, 1536:2304], work[:, 1536:2304]))
            ml_lat[2].emptied(ve)
            for m in range(2):
                stt(scr[:, m * T:(m + 1) * T], scr[:, m * T:(m + 1) * T], vc("q_norm", m), work[:, 1536:1792], ALU.mult, ALU.mult)
                x = scr[:, 512 + m * 512:1024 + m * 512]
                last = stt(x, x, vc("kv_norm", m), work[:, 1792:2304], ALU.mult, ALU.mult)
            last.then_inc(lat_ready, 1)
            for n in range(2):
                ml_py[n].filled(ve)
                for m in range(2):
                    g = 2 * n + m
                    last = ts(OT[:, g, :], PS[ml_py[n].b][:, m * T:(m + 1) * T], vc("pool_scale", g), ALU.mult)
                last.then_inc(ml_py[n].bank.free, 1)
            mc = aring[:, ml_const.slot, :]
            ml_const.loaded(ve)
            for j in range(4):
                turn(F[0:96, 2 * j:2 * j + 2, :], ml_qr[j], mc[0:96, 2144:2400], mc[0:96, 2400:2656], 2, 96)
            turn(scr[0:96, 1792:2048].unsqueeze(1), ml_krr, mc[0:96, 2144:2400], mc[0:96, 2400:2656], 1, 96)
            ve.wait_ge(rope_done, 21)
            ve.tensor_copy(Fl[64:96, 2048:6144].rearrange("p (h t) -> p h t", h=8),
                           scr[64:96, 1536:2048].unsqueeze(1).to_broadcast([32, 8, 512])).then_inc(rope_done, 1)
            units(ml_units, mla_specs(), 40)
            residual(ml_y, 2, 16, x_ready_raw)
            layer_norm(4, 0, 6)
            ve.wait_ge(x_ready, 1)
            modulate(H, X, mod[:, 2, :], 32, 24, h_ready, 6)
            step(ts(X[:], X[:], ALPHA, ALU.mult))
            feed_forward(2, ffn[2], 2)
            residual(ffn[2]["y"], 2, 40, x_ready_raw)
            take_mod(3)
            layer_norm(5, 1, 7)
            ve.wait_ge(x_ready, 2)

            modulate(H, X, mod[:, 3, :], 8, 0, h_ready, 7)
            step(ts(X[:], X[:], ALPHA, ALU.mult))
            for n in range(3):
                hy_sin[n].filled(ve)
                x = work[0:64, 2 * T:3 * T]
                ts(x, PS[hy_sin[n].b][0:64, 0:T], vc("fb", n, HD), ALU.add, vc("freq", 0, HD), ALU.mult).then_inc(
                    hy_sin[n].bank.free, 1)
                hy_sin[n].emptied(ve)
                reduced(work[0:64, T:2 * T], x, sin_arg, 64)
            hy_f[0].loaded(ve)
            dec = wring[:, hy_f[0].slot, :].rearrange("p (d t n) -> p d t n", d=2, t=2)
            for n in range(4):
                t, h = n // 2, n % 2
                o = t * 1024 + h * 512
                fwd, bwd = work[:, 1024:1536], work[:, 1536:2048]
                for d, dst in ((0, fwd), (1, bwd)):
                    hy_taps[n][d].filled(ve)
                    tt(dst, PS[hy_taps[n][d].b][:, :], dec[:, d, t, h * 512:(h + 1) * 512], ALU.mult).then_inc(
                        hy_taps[n][d].bank.free, 1)
                hy_taps[n][1].emptied(ve)
                tt(Fl[:, o:o + 512], fwd, bwd, ALU.add)
                step(tt(Fl[:, 2048 + o:2560 + o], fwd, bwd, ALU.subtract))
            ve.tensor_copy(mx8[:, 0, 0:1], mx8[:, 0, 0:1]).then_inc(hy_ready, 1)
            for j in range(12):
                ve.wait_ge(zconv, j + 1)
                hy_pair[j].filled(ve)
                for m in range(2):
                    t = 2 * j + m
                    z = PS[hy_pair[j].b][:, m * T:(m + 1) * T]
                    step(stt(F[:, t, 1:T], z[:, 0:T - 1], vc("conv_w", t), F[:, t, 1:T], ALU.mult, ALU.add))
                    last = stt(F[:, t, 0:T - 1], z[:, 1:T], vc("conv_w", 48 + t), F[:, t, 0:T - 1], ALU.mult, ALU.add)
                last.then_inc(hy_pair[j].bank.free, 1)
            hy_pair[11].emptied(ve)
            tt(F[:, 16:24, :], F[:, 16:24, :], F[:, 8:16, :], ALU.mult).then_inc(hy_ready, 1)
            KR = OTl.rearrange("p (f n) -> p f n", f=2)
            KI = V[:].rearrange("p (f n) -> p f n", f=2)
            t1, t2, t3 = (work[:, q * 1024:(q + 1) * 1024].rearrange("p (f n) -> p f n", f=2) for q in range(3))
            hy_n[1].emptied(ve)
            for h in range(2):
                hy_vs[h][3].emptied(ve)
                re, im = spectrum(h)
                kr, ki = KR[:, :, h * 512:(h + 1) * 512], KI[:, :, h * 512:(h + 1) * 512]
                tt(t1, re, kr, ALU.mult)
                tt(t2, im, ki, ALU.mult)
                step(tt(t3, re, ki, ALU.mult))
                step(tt(re, t1, t2, ALU.subtract))
                step(tt(t1, im, kr, ALU.mult))
                step(tt(t1[0:1, 0, :], im[0:1, 0, :], scr[0:1, h * 512:(h + 1) * 512], ALU.mult))
                tt(im, t1, t3, ALU.add).then_inc(spec_ready, 1)
                ve.wait_ge(spec_ready, h + 1)
            for h in range(2):
                for n in range(2):
                    job = hy_y[h][n]
                    job.filled(ve)
                    for m in range(2):
                        ct = 4 * h + 2 * n + m
                        last = stt(F[:, 16 + ct, :], F[:, 16 + ct, :], vc("skip", ct), PS[job.b][:, m * T:(m + 1) * T],
                                   ALU.mult, ALU.add)
                    last.then_inc(job.bank.free, 1)
            hy_y[1][1].emptied(ve)
            tt(F[:, 0:8, :], F[:, 0:8, :], F[:, 16:24, :], ALU.mult).then_inc(hy_ready, 1)
            residual(hy_yo, 3, 16, x_ready_raw)
            layer_norm(6, 2, 8)
            ve.wait_ge(x_ready, 3)
            modulate(H, X, mod[:, 3, :], 32, 24, h_ready, 8)
            step(ts(X[:], X[:], ALPHA, ALU.mult))

            rt_job.filled(ve)
            ve.tensor_copy(lg[:], PS[7][:, 0:16].rearrange("p (t e) -> p t e", t=2)).then_inc(rt_job.bank.free, 1)
            rt_job.emptied(ve)
            for t in range(2):
                step(ve.max(out=mx8[:, t, :], in_=lg[:, t, :]))
                last = ts(pw[:, t, :], lg[:, t, :], mx8[:, t, 0:1], ALU.subtract)
            last.then_inc(rt_ready, 1)
            big = cmp8[:, 0, :].rearrange("p (e j) -> p e j", e=8)
            same = cmp8[:, 1, :].rearrange("p (e j) -> p e j", e=8)
            for t in range(2):
                mine = lg[:, t, :].unsqueeze(2).to_broadcast([P, 8, 8])
                other = lg[:, t, :].unsqueeze(1).to_broadcast([P, 8, 8])
                tt(big, other, mine, ALU.is_gt)
                step(tt(same, other, mine, ALU.is_equal))
                step(tt(same, same, R("tie").rearrange("p (e j) -> p e j", e=8), ALU.mult))
                step(tt(big, big, same, ALU.add))
                step(ve.tensor_reduce(ch8[:, t, :], big, AX.X, ALU.add))
            ts(ch8[:], ch8[:], 1.5, ALU.is_lt).then_inc(route_ready, 1)
            ve.wait_ge(route_ready, 1)
            ve.wait_ge(rt_exp, 1)
            step(tt(pw[:], pw[:], ch8[:], ALU.mult))
            step(ve.tensor_reduce(psum8[:], pw[:], AX.X, ALU.add))
            step(ve.reciprocal(psum8[:], psum8[:]))
            step(tt(pw[:], pw[:], psum8[:].unsqueeze(2).to_broadcast([P, 2, 8]), ALU.mult))
            pos_job.filled(ve)
            step(stt(posm[:], PS[7][:, 0:16].rearrange("p (t e) -> p t e", t=2), 1.0, ch8[:], ALU.add, ALU.mult))
            step(ts(posm[:], posm[:], -1.0, ALU.add))
            ve.tensor_reduce(over[:], PS[7][:, 16:24], AX.X, ALU.max).then_inc(pos_job.bank.free, 1)
            pos_job.emptied(ve)
            ts(flag[:], over[:], SLOTS + 0.5, ALU.is_gt).then_inc(flag_ready, 1)
            step(ve.memset(yacc, 0.0))

            def experts(M):
                J_ = M["j"]
                with ve.Fori(0, NE // 2) as i:
                    for e in range(2):
                        for t in range(2):
                            last = ts(sel(e)[:, t, :], R("slot"), posm[:, t, bass.ds(2 * i + e, 1)], ALU.is_equal)
                        last.then_inc(M["sel"], 1)
                        ve.wait_ge(M["sel"], 2 * i + e + 1)
                        for t in range(2):
                            last = ts(wsel(e)[:, t, :], sel(e)[:, t, :], pw[:, t, bass.ds(2 * i + e, 1)], ALU.mult)
                        last.then_inc(M["wsel"], 1)

                    def scatter(e, q):
                        job = J_["s", e, q]
                        job.filled(ve, i)
                        x = yacc[:, 2 * q:2 * q + 2, :]
                        tt(x, x, PS[7][:, :].rearrange("p (a t) -> p a t", a=2), ALU.add).then_inc(job.bank.free, 1)

                    for g in range(14):
                        J_["u", g].filled(ve, i)
                        J_["g", g].emptied(ve, i)
                        tt(work[:, (g % 2) * 512:(g % 2) * 512 + 512], work[:, 2048 + (g % 2) * 512:2560 + (g % 2) * 512],
                           PS[2 + g % 2][:, :], ALU.mult).then_inc(J_["u", g].bank.free, 1)
                        J_["u", g].emptied(ve, i)
                        ve.tensor_copy(mx8[:, 0, 0:1], mx8[:, 0, 0:1]).then_inc(M["hid"], 1)
                        if g >= 10:
                            scatter(0, g - 10)
                    for q in range(4):
                        scatter(1, q)
                    J_["s", 1, 3].emptied(ve, i)

            experts(moe)
            with ve.If(ve.value_load(flag[0:1, 0:1], min_val=0, max_val=1) > 0):
                ts(posm[:], posm[:], -float(SLOTS), ALU.add).then_inc(over_done, 1)
                ve.wait_ge(over_done, 1)
                experts(moe2)
            for k in range(KT):
                last = stt(X[:, k, :], yacc[:, k, :], mod[:, 3, 40 + k:41 + k], X[:, k, :], ALU.mult, ALU.add)
            last.then_inc(x_ready_raw, 1)
            layer_norm(7, 3, 9)


_WEIGHTS = ["ada_w", "ffn_w_gate", "ffn_w_up", "ffn_w_down", "sp_w_in", "sp_w_out", "nsa_cmp_w1", "nsa_cmp_w2",
            "diff_w_in", "diff_w_out", "ada_w_2", "mix_in_w_2", "pool_w_2", "q_up_2", "kv_up_2", "mix_out_w_2",
            "ffn_gate_2", "ffn_up_2", "ffn_down_2", "hy_in_w_2", "hy_fw1_2", "hy_fw2_2", "hy_fw3_2", "hy_fout_2",
            "hy_out_w_2", "router_w_2", "moe_gate_2", "moe_up_2", "moe_down_2"]


def kernel(**inputs):
    import concourse.bacc as bacc
    from concourse.bass_utils import run_bass_kernel_spmd as run

    x = {k: np.asarray(v) for k, v in inputs.items()}

    def columns(v):
        return np.ascontiguousarray(v).reshape(-1, P).T

    def twice(v):
        v = np.ascontiguousarray(v).reshape(-1, 64).T
        return np.concatenate([v, v], 0)

    def upper(v):
        v = np.ascontiguousarray(v).reshape(-1, 64).T
        return np.concatenate([v, np.zeros_like(v)], 0)

    def feature_major(v):
        return np.ascontiguousarray(v.reshape(T, KT, P).transpose(2, 1, 0))

    vec = np.concatenate([
        columns(x["c"]), columns(x["c_2"]), columns(x["c_ctx_2"]), columns(x["attn_norm"]), columns(x["ffn_norm"]),
        columns(x["ada_b"]), columns(x["ada_b_2"]), columns(x["ln_g_2"]), columns(x["ln_b_2"]),
        columns(x["pool_scale_2"]), columns(x["q_norm_2"]), columns(x["kv_norm_2"]), columns(x["hy_conv_w_2"]),
        columns(x["hy_conv_b_2"]), columns(x["hy_skip_2"]), twice(x["moba_q_norm"]), twice(x["moba_k_norm"]),
        twice(x["nsa_q_norm"]), twice(x["nsa_k_norm"]), twice(x["diff_q_norm"]), twice(x["diff_k_norm"]),
        columns(x["diff_out_norm"]), upper(x["diff_lambda"]), upper(x["hy_fb1_2"]), upper(x["hy_fb2_2"]),
        upper(x["hy_fb3_2"]), upper(x["hy_freq_2"]), columns(x["nsa_cmp_pos"])], 1)
    con, mlac, hyc, routing, spread, decay = shape_constants()
    arrays = {"vec": np.ascontiguousarray(vec), "con": con, "mlac": mlac, "hyc": hyc, "routing": routing, "spread": spread, "decay": decay,
              "positions": x["positions"], "x": feature_major(x["x"]), "ctx_2": feature_major(x["ctx_2"])}
    arrays |= {n: np.ascontiguousarray(x[n]) for n in _WEIGHTS}

    nc = bacc.Bacc("TRN2", target_bir_lowering=False, num_devices=1)
    args = {n: nc.dram_tensor(f"in_{n}", v.shape, mybir.dt.from_np(v.dtype), kind="ExternalInput").ap()
            for n, v in arrays.items()}
    out = nc.dram_tensor("out", (P, KT, T), F32, kind="ExternalOutput").ap()
    build(nc, args, out)
    got = run(nc, [{f"in_{n}": v for n, v in arrays.items()}], core_ids=[0]).results[0]["out"]
    return np.ascontiguousarray(got.transpose(2, 1, 0)).reshape(1, T, D)
```

```python
from contextlib import ExitStack

import numpy as np

import concourse.bass as bass
from concourse import mybir
from concourse.alu_op_type import AluOpType as ALU

F32 = mybir.dt.float32
F32R = mybir.dt.float32r
BF16 = mybir.dt.bfloat16
I32 = mybir.dt.int32
ACT = mybir.ActivationFunctionType
AX = mybir.AxisListType

P = 128
T = 256
D = 1024
KT = D // P
NEG = -1e30
HD = 64
ROT = HD // 4
FF = 2816
FE = 3584
NE = 8
SLOTS = 128
CH = 512
CHW = KT * CH
NC_LEN, NC_STRIDE = 32, 16
NCMP = (T - NC_LEN) // NC_STRIDE + 1
CTX = 256
LAM_INIT = 0.8 - 0.6 * float(np.exp(-0.3 * 1))
ALPHA = (2.0 * 2) ** 0.25
MLA_SCALE = (64 + 32) ** -0.5
TWO_PI = 2.0 * np.pi
MAGIC = 12582912.0
PI_A = 6.28125
PI_B = float(np.float32(np.float16(TWO_PI - PI_A)))
PI_C = float(np.float32(TWO_PI - PI_A - PI_B))
PI_CLAMP = 3.1415925

VEC = {}
_at = 0
for _name, _n in [("c", 8), ("c2", 8), ("cctx", 8), ("attn_norm", 16), ("ffn_norm", 16), ("ada_b", 96),
                  ("ada_b2", 96), ("ln_g", 32), ("ln_b", 32), ("pool_scale", 4), ("q_norm", 2), ("kv_norm", 2),
                  ("conv_w", 72), ("conv_b", 24), ("skip", 8), ("moba_q", 1), ("moba_k", 1), ("nsa_q", 1),
                  ("nsa_k", 3), ("diff_q", 1), ("diff_k", 1), ("out_norm", 1), ("lam", 4), ("fb", 3),
                  ("freq", 1), ("pos_k", 16), ("pos_v", 16)]:
    VEC[_name] = (_at, _n)
    _at += _n
NVEC = _at

CON = {}
_at = 0
for _name, _n in [("ident", 128), ("ones", 128), ("half", 64), ("whole", 64), ("rot", 128), ("mask", 384),
                  ("invf", 1), ("rms_eps", 1), ("ln_eps", 1), ("half_pi", 1), ("cmask", 2 * NCMP), ("cvalid", 2 * NCMP)]:
    CON[_name] = (_at, _n)
    _at += _n
NCON = _at
MLAC = {"pool": (0, 2048), "rot": (2048, 96), "cos": (2144, 256), "sin": (2400, 256), "pool_w": (2656, 512)}
NMLAC = 2656
HYC = {"fr": (0, 512), "fs": (512, 512), "fi": (1024, 512), "gr": (1536, 512), "gi": (2048, 512),
       "z": (2560, 256), "nyq": (2816, 1), "fw": (2817, 192),
       "before": (3009, 128), "slot": (3137, 128), "tie": (3265, 64)}
NHYC = 2817


def shape_constants():
    f32 = np.float32
    con = np.zeros((P, NCON), f32)

    def put(name, a):
        o, n = CON[name]
        a = np.asarray(a, f32)
        con[:a.shape[0], o:o + n] = a.reshape(a.shape[0], n)

    p = np.arange(P)
    put("ident", np.eye(P))
    put("ones", np.ones((P, P)))
    half = np.zeros((P, 64))
    half[:64, 32] = 1
    half[64:, 33] = 1
    put("half", half)
    whole = np.zeros((P, 64))
    whole[:, 32] = 1
    put("whole", whole)
    rot = np.zeros((P, P))
    for base in (0, 64):
        for i in range(ROT // 2):
            rot[base + i + ROT // 2, base + i] = -1
            rot[base + i, base + i + ROT // 2] = 1
    put("rot", rot)
    causal = np.where(p[None, :] <= p[:, None], 0.0, NEG)
    put("mask", np.concatenate([np.zeros((P, P)), causal, causal], 1))
    inv = (f32(1.0) / (f32(500000.0) ** (np.arange(0, ROT, 2, dtype=f32) / f32(ROT)))).astype(f32)
    invf = np.zeros((P, 1), f32)
    for base in (0, 64):
        invf[base:base + 8, 0] = inv
        invf[base + 8:base + 16, 0] = inv
    put("invf", invf)
    put("rms_eps", np.full((P, 1), 1e-6))
    put("ln_eps", np.full((P, 1), 1e-5))
    put("half_pi", np.full((P, 1), np.pi / 2))
    e = np.arange(NE)
    routing = np.concatenate([(p[:, None] < p[None, :]), np.tile(p[None, :], (P, 1)),
                              np.tile((e[None, :] < e[:, None]).reshape(1, 64), (P, 1))], 1).astype(f32)
    end = np.arange(NCMP) * NC_STRIDE + NC_LEN - 1
    ok = end[None, None, :] <= (p[:, None, None] + np.array([0, P])[None, :, None])
    put("cmask", np.where(ok, 0.0, NEG))
    put("cvalid", ok)

    mla = np.zeros((P, NMLAC), f32)
    t = np.arange(T)
    pool = np.zeros((4, T, T))
    for g, w in enumerate((2, 4, 8, 16)):
        lo, hi = np.clip(t - w // 2, 0, T), np.clip(t + w // 2, 0, T)
        inside = (t[:, None] >= lo[None, :]) & (t[:, None] < hi[None, :])
        pool[g] = inside / (hi - lo)[None, :] - np.eye(T)
    mla[:, 0:2048] = pool.reshape(4, 2, P, T).transpose(2, 1, 0, 3).reshape(P, 2048)
    rot = np.eye(96) * 0
    ang = np.zeros((96, T), f32)
    inv = (f32(10000.0) ** (-np.arange(0, 16, 2, dtype=f32) / f32(16))).astype(f32)
    for base, where in ((64, t // 64), (80, t % 64)):
        for i in range(8):
            rot[base + i + 8, base + i] = -1
            rot[base + i, base + i + 8] = 1
            ang[base + i] = ang[base + 8 + i] = where.astype(f32) * inv[i]
    mla[:96, 2048:2144] = rot
    mla[:96, 2144:2400] = np.cos(ang)
    mla[:96, 2400:2656] = np.sin(ang)

    hyc = np.zeros((P, NHYC), f32)
    th = 2 * np.pi / 512 * ((t[:, None] * t[None, :]) % 512)
    alt = (-1.0) ** t
    fr, fs = np.cos(th), -np.sin(th)
    fi = fs.copy()
    fi[:, 0] = alt
    gr, gi = 2 * fr.T / 512, 2 * fs.T / 512
    gr[0] = 1.0 / 512
    gi[0] = alt / 512
    for n, a in (("fr", fr), ("fs", fs), ("fi", fi), ("gr", gr), ("gi", gi)):
        hyc[:, HYC[n][0]:HYC[n][0] + 512] = a.reshape(2, P, T).transpose(1, 0, 2).reshape(P, 512)
    tt = np.linspace(0.0, 1.0, T, dtype=f32)[:, None]
    wa = (f32(2.0 * np.pi / T) * np.arange(T, dtype=f32))[:, None]
    bands = np.linspace(1e-4, 15, 16, dtype=f32)[None, :]
    z = np.concatenate([tt, np.cos(bands * wa), -np.sin(bands * wa)], 1)
    hyc[:33, 2560:2816] = z.T
    hyc[:, 2816] = (-1.0) ** p
    lo, hi = np.log(1e-2) / 1.5, np.log(1e-2) / 0.3
    deltas = np.abs(np.linspace(lo, hi, D, dtype=f32))
    dec = np.exp(-tt * deltas).astype(f32)
    decb = dec.copy()
    decb[0] = 0
    decay = np.stack([dec, decb]).reshape(2, 2, P, D).transpose(2, 0, 1, 3).reshape(P, 4 * D)
    spread = np.zeros((32, 16, 2, 64), f32)
    for t_ in range(16):
        for h_ in range(2):
            spread[2 * t_ + h_, t_, h_] = 1
    return con, mla, hyc, routing, spread.reshape(32, 2048), np.ascontiguousarray(decay)


class Bank:

    def __init__(self, sem, name, credit=0):
        self.full, self.free = sem(name + "_full"), sem(name + "_free")
        self.credit, self.uses = credit, 0


class Job:

    def __init__(self, banks, b, use=None, stride=0):
        self.b, self.bank, self.stride = b, banks[b], stride
        if use is None:
            use = self.bank.uses
            self.bank.uses += 1
        self.use = use

    def at(self, i):
        return self.use if i is None or self.stride == 0 else self.use + i * self.stride

    def open(self, eng, i=None):
        if i is None and self.use + self.bank.credit == 0:
            return
        eng.wait_ge(self.bank.free, self.at(i) + self.bank.credit)

    def filled(self, eng, i=None):
        eng.wait_ge(self.bank.full, self.at(i) + 1)

    def emptied(self, eng, i=None):
        eng.wait_ge(self.bank.free, self.at(i) + 1 + self.bank.credit)

    def when_full(self):
        return self.bank.full, self.use + 1, self.stride


def loop_jobs(banks, order, passes):
    per = {b: order.count(b) for b in order}
    jobs = [Job(banks, b, banks[b].uses + order[:n].count(b), per[b]) for n, b in enumerate(order)]
    for b in per:
        banks[b].uses += per[b] * passes
    return jobs


class Ring:

    def __init__(self, sem, name, slots):
        self.sems = [sem(f"{name}_loaded{s}") for s in range(slots)]
        self.slots, self.n = slots, 0
        self.last, self.loads = [None] * slots, [0] * slots


class Chunk:

    def __init__(self, ring, dmas=1, slot=None):
        self.ring, self.freed_by, self.before, self.stride, self.wrap = ring, None, None, 0, False
        self.slot = ring.n % ring.slots
        ring.n += 1
        self.before = ring.last[self.slot]
        ring.last[self.slot] = self
        ring.loads[self.slot] += 16 * dmas
        self.value = ring.loads[self.slot]

    @property
    def sem(self):
        return self.ring.sems[self.slot]

    def room(self, eng, i=None):
        if self.wrap and i is not None:
            sem, value, stride = self.wrap.freed_by
            eng.wait_ge(sem, value - stride + i * stride)
        elif self.before is not None:
            sem, value, stride = self.before.freed_by
            eng.wait_ge(sem, value if i is None or stride == 0 else value + i * stride)

    def loaded(self, eng, i=None):
        eng.wait_ge(self.sem, self.value if i is None or self.stride == 0 else self.value + i * self.stride)


class LoopEnd:

    def __init__(self, chunk, passes):
        self.chunk, self.passes = chunk, passes

    @property
    def freed_by(self):
        sem, value, stride = self.chunk.freed_by
        return sem, value + (self.passes - 1) * stride, 0


def loop_chunks(ring, count, passes):
    assert count % ring.slots == 0
    chunks = [Chunk(ring) for _ in range(count)]
    turns = count // ring.slots
    for n, c in enumerate(chunks):
        c.stride = 16 * turns
        if n < ring.slots:
            c.wrap = chunks[count - ring.slots + n]
    for c in chunks[count - ring.slots:]:
        ring.last[c.slot] = LoopEnd(c, passes)
        ring.loads[c.slot] += 16 * turns * (passes - 1)
    return chunks


class Steps:

    def __init__(self, eng, sem):
        self.eng, self.sem, self.n = eng, sem, 0

    def __call__(self, ins):
        ins.then_inc(self.sem, 1)
        self.n += 1
        self.eng.wait_ge(self.sem, self.n)


def _ada_body():
    shared = [(n * T, 4 * T, True) for n in range(4)]
    rest = [(8 * T + n * T, 6 * T, False) for n in range(6)]
    order = [(0, shared[0]), (1, rest[0]), (2, shared[1])] + [(3, p) for p in shared[2:] + rest[1:]]
    return [(pair, *p) for pair, p in order]


ADA_BODY = _ada_body()
ADA_TAIL = [(0, 20 * T), (1, 21 * T), (2, 22 * T), (2, 23 * T)]


def moe_sequence():
    out = [("gu", 0)]
    for g in range(14):
        if g + 1 < 14:
            out.append(("gu", g + 1))
        out.append(("t", g))
        if g >= 1:
            out.append(("d", g - 1))
        if 9 <= g < 13:
            out.append(("s", 0, g - 9))
    out.append(("d", 13))
    return out + [("s", 1, q) for q in range(4)]


def build(nc, a, out):
    with ExitStack() as ctx:
        def sb(name, shape, dt=F32):
            return ctx.enter_context(nc.sbuf_tensor(name, shape, dt))

        def sb2(name, shape):
            with nc.sbuf_tensor(name + "_rounded", shape, F32R) as rounded:
                pass
            return sb(name, shape), rounded

        def sem(name):
            return ctx.enter_context(nc.semaphore(name))

        wring, wringr = sb2("wring", [P, 6, CHW])
        with (nc.sbuf_tensor("aring_rounded", [P, CHW], F32R) as aring0r,
              nc.sbuf_tensor("scr_rounded", [P, CHW], F32R) as scrr):
            pass
        aring = sb("aring", [P, 2, CHW])
        X = sb("X", [P, KT, T])
        H, Hr = sb2("H", [P, KT, T])
        F, Fr = sb2("F", [P, 24, T])
        V, Vr = sb2("V", [P, 2048])
        OT, OTr = sb2("OT", [P, KT, T])
        work = sb("work", [P, 3072])
        con = sb("con", [P, NCON])
        vec = sb("vec", [P, NVEC])
        mod = sb("mod", [P, 4, 48])
        modc = sb("modc", [P, 16])
        cs = sb("cs", [P, 24])
        gsc = sb("gsc", [P, KT])
        tables = sb("tables", [P, 2, T])
        cosT, sinT = tables[:, 0, :], tables[:, 1, :]
        posi = work[:, 2048:2304].bitcast(I32)
        rstd = sb("rstd", [P, T])
        rheads = rstd[0:32, :]
        gates = sb("gates", [P, 2, 24])
        zero = sb("zero", [P, P], BF16)
        nmax, ssum, fac = sb("nmax", [P, 2, 2]), sb("ssum", [P, 2, 2]), sb("fac", [P, 2, 2])
        cst = sb("cst", [P, 2, 16])
        lamt = sb("lamt", [P, 4])
        ogain = sb("ogain", [P, 1])
        rw = sb("rw", [P, KT, NE])
        lg, ch8, pw, posm = (sb(n, [P, 2, NE]) for n in ("lg", "ch8", "pw", "posm"))
        mx8, psum8 = sb("mx8", [P, 2, 8]), sb("psum8", [P, 2])
        over = sb("over", [P, 1])
        flag = sb("flag", [P, 1], I32)
        PS = [ctx.enter_context(nc.psum_tensor(f"ps{b}", [P, 512], F32)) for b in range(8)]

        Fl = F[:].rearrange("p a t -> p (a t)")
        Hl = H[:].rearrange("p a t -> p (a t)")
        OTl = OT[:].rearrange("p a t -> p (a t)")
        Xl = X[:].rearrange("p a t -> p (a t)")
        cw2 = OTl[:, 0:384]
        cmp8 = work[:, 0:128].rearrange("p (a n) -> p a n", a=2)
        scr = aring[:, 1, :]

        def ada_half(c):
            return aring[:, 0, c.slot * 2048:(c.slot + 1) * 2048].rearrange("p (k n) -> p k n", k=KT)

        def w3r(c, n=CH, k=KT):
            return wringr[:, c.slot, 0:k * n].rearrange("p (k n) -> p k n", n=n)

        Vr, Hlr, OTlr, Flr = (t[:].rearrange("p a t -> p (a t)") if len(t.shape) == 3 else t[:]
                              for t in (Vr, Hr, OTr, Fr))

        def C(name, rows=P):
            o, n = CON[name]
            return con[0:rows, o:o + n]

        def R(name):
            o, n = HYC[name]
            return aring[:, 0, o:o + n]

        def vc(name, k=0, rows=P, n=1):
            o = VEC[name][0] + k
            return vec[0:rows, o:o + n]

        def w3(c, n=CH, k=KT):
            return wring[:, c.slot, 0:k * n].rearrange("p (k n) -> p k n", n=n)

        def bank3(b, n, rows=P):
            return PS[b][0:rows, :].rearrange("p (a n) -> p a n", n=n)

        banks = [Bank(sem, f"bank{b}") for b in range(8)]
        ring, mring = Ring(sem, "w", 6), Ring(sem, "m", 2)
        nring = Ring(sem, "n", 2)
        small_loaded = sem("small_loaded")
        ctx_loaded = sem("ctx_loaded")
        out_stored = sem("out_stored")
        dve_step = sem("dve_step")
        cs_ready, zero_ready = sem("cs_ready"), sem("zero_ready")
        ada_step, ada_used = sem("ada_step"), sem("ada_used")
        sq_ready, sd_ready, h_ready, x_ready = (
            sem("sq_ready"), sem("sd_ready"), sem("h_ready"), sem("x_ready"))
        x_ready_raw = sem("x_ready_raw")
        sin_arg, sin_done = sem("sin_arg"), sem("sin_done")
        proj_copied, stat_summed = sem("proj_copied"), sem("stat_summed")
        rh_sd, rh_ready, rope_done = sem("rh_sd"), sem("rh_ready"), sem("rope_done")
        nmax_ready, exp_done, p_ready, pv_done = sem("nmax_ready"), sem("exp_done"), sem("p_ready"), sem("pv_done")
        gate_raw, gates_ready = sem("gate_raw"), sem("gates_ready")
        windows_ready, blocks_ready, hidrep_ready = sem("windows_ready"), sem("blocks_ready"), sem("hidrep_ready")
        cshift, cexp, cp_ready = sem("cshift"), sem("cexp"), sem("cp_ready")
        ksw_ready, rows_done, vrows_ready = sem("ksw_ready"), sem("rows_done"), sem("vrows_ready")
        lam_prod = sem("lam_prod")
        down_used, silu_done, hid_done = sem("down_used"), sem("silu_done"), sem("hid_done")
        ff_upper, ff_lower, h_split = sem("ff_upper"), sem("ff_lower"), sem("h_split")
        lat_ready = sem("lat_ready")
        zconv = sem("zconv")
        hy_ready, spec_ready = sem("hy_ready"), sem("spec_ready")
        rt_exp, rt_ready, route_ready, flag_ready = sem("rt_exp"), sem("rt_ready"), sem("route_ready"), sem("flag_ready")
        over_done = sem("over_done")

        def J(b):
            return Job(banks, b)

        ada0 = loop_chunks(mring, 2, 2)
        for n, c in enumerate(ada0):
            c.freed_by = (ada_used, n + 1, 2)
        nring.last = [mring.last[0]] * 2
        tables_loaded = sem("tables_loaded")
        SP_TABLE, DF_TABLE, ML_TABLE, HY_TABLE = 16, 2 * 16, 4 * 16, 9 * 16
        ada1 = [Chunk(nring) for _ in range(16)]
        for n, c in enumerate(ada1):
            c.freed_by = (ada_used, 4 + n + 1, 0)
        adas = 4 + 16
        mod_job = [J(7)]
        norm_job = []

        def plan_norm(mean):
            norm_job.append(([J(6)] if mean else []) + [J(6)])

        def plan_proj(pairs, per_chunk):
            return [J(j % 4) for j in range(pairs)]

        def plan_rope(pairs):
            return J(7), [J(j % 2) for j in range(pairs)], [J(2 + j % 2) for j in range(pairs)]

        def plan_units(groups):
            s, t, o = [], [], []
            n = 0
            for g in groups:
                o.append(J(4 + len(o) % 2))
                for _ in range(g):
                    s.append(J(n % 2))
                    t.append(J(2 + n % 2))
                    n += 1
            return s, t, o

        def plan_out():
            cs2 = [Chunk(ring), Chunk(ring)]
            jobs = [J(j) for j in range(4)]
            cs2[0].freed_by, cs2[1].freed_by = jobs[1].when_full(), jobs[3].when_full()
            return cs2, jobs

        def plan_ffn(f, adas):
            L = {}
            L["c"] = loop_chunks(ring, 6, 2)
            L["j"] = loop_jobs(banks, [0, 1, 2, 3] * 2, 2)
            for n in range(2):
                L["c"][2 * n].freed_by = L["j"][4 * n + 2].when_full()
                L["c"][2 * n + 1].freed_by = L["j"][4 * n + 3].when_full()
                L["c"][4 + n].freed_by = (down_used, 5 * f + n + 1, 2)
            L["a"] = loop_chunks(nring, len(ADA_BODY), 2)
            for n, c in enumerate(L["a"]):
                c.freed_by = (ada_used, adas + n + 1, len(ADA_BODY))
            L["tc"] = [Chunk(ring) for _ in range(6)]
            L["tj"] = [J(b) for b in (0, 1, 2, 3, 0, 1)]
            for n, j in ((0, 2), (1, 3), (2, 4), (3, 5)):
                L["tc"][n].freed_by = L["tj"][j].when_full()
            L["ta"] = [Chunk(nring) for _ in range(24 - 2 * len(ADA_BODY))]
            for n, c in enumerate(L["ta"]):
                c.freed_by = (ada_used, adas + 2 * len(ADA_BODY) + n + 1, 0)
            L["y"] = [J(b) for b in (4, 5, 6, 7)]
            L["tc"][4].freed_by = (down_used, 5 * f + 5, 0)
            L["tc"][5].freed_by = L["y"][3].when_full()
            return L

        plan_norm(False)
        sp_w = [Chunk(ring) for _ in range(6)]
        sp_pair = plan_proj(8, 2)
        sp_tok = [J(0), J(1)]
        sp_v = [J(2), J(3)]
        for n in range(3):
            sp_w[n].freed_by = sp_pair[2 * n + 1].when_full()
        sp_w[3].freed_by = sp_w[4].freed_by = sp_tok[1].when_full()
        sp_w[5].freed_by = sp_v[1].when_full()
        sp_rope = plan_rope(8)
        sp_const, sp_more = Chunk(nring, dmas=0), Chunk(nring, dmas=0)
        sp_const.freed_by = sp_more.freed_by = sp_rope[1][7].when_full()
        cmp_w = [Chunk(ring), Chunk(ring)]
        hid_job, kvc_job, cs_job, ct_job = J(0), J(1), J(2), J(3)
        cmp_w[0].freed_by = cmp_w[1].freed_by = hid_job.when_full()
        mod_more = J(7)
        sp_units = plan_units([1] * 8 + [2] * 8)
        sp_out, sp_y = plan_out()
        plan_norm(False)
        ffn = [plan_ffn(0, adas)]
        adas += 24
        mod_job.append(J(3))
        plan_norm(False)
        df_w = [Chunk(ring) for _ in range(6)]
        df_pair = plan_proj(8, 2)
        df_v = [J(b) for b in range(4)]
        for n in range(4):
            df_w[n].freed_by = df_pair[2 * n + 1].when_full()
        df_w[4].freed_by, df_w[5].freed_by = df_v[1].when_full(), df_v[3].when_full()
        df_rope = plan_rope(8)
        df_const, df_more = Chunk(nring, dmas=0), Chunk(nring, dmas=0)
        df_const.freed_by = df_more.freed_by = df_rope[1][7].when_full()
        lam_job = J(7)
        df_units = plan_units([2] * 8)
        on_stat, on_bc = J(7), [J(j) for j in range(4)]
        df_out, df_y = plan_out()
        plan_norm(False)
        ffn.append(plan_ffn(1, adas))
        adas += 24
        mod_job.append(J(3))
        ml_const, ml_more = Chunk(nring, dmas=0), Chunk(nring, dmas=0)
        ml_w = [Chunk(ring) for _ in range(3)] + [Chunk(ring, dmas=2)]
        ml_pool = [J(0), J(1)]
        ml_lat = [J(2), J(3), J(0)]
        ml_kr = J(1)
        ml_stat = [J(2), J(3)]
        ml_d = [J(0), J(1)]
        ml_py = [J(2), J(3)]
        ml_q, ml_qr = [J(j % 2) for j in range(4)], [J(2 + j % 2) for j in range(4)]
        ml_krr = J(0)
        ml_k = [J(1 + h % 3) for h in range(8)]
        ml_v = [J(j) for j in range(4)]
        ml_w[0].freed_by, ml_w[1].freed_by = ml_pool[1].when_full(), ml_lat[2].when_full()
        ml_w[2].freed_by, ml_w[3].freed_by = ml_kr.when_full(), ml_v[3].when_full()
        ml_const.freed_by = ml_more.freed_by = (rope_done, 16 + 5, 0)
        ml_units = plan_units([2] * 8)
        ml_out, ml_y = plan_out()
        plan_norm(True)
        ffn.append(plan_ffn(2, adas))
        adas += 24
        mod_job.append(J(3))
        plan_norm(True)
        hy_const, hy_more = Chunk(nring, dmas=0), Chunk(nring, dmas=0)
        hy_f = [Chunk(ring), Chunk(ring)]
        hy_w = [Chunk(ring) for _ in range(6)]
        hy_sin = [J(0), J(1), J(2)]
        hy_taps = [(J(2 * (n % 2)), J(2 * (n % 2) + 1)) for n in range(4)]
        hy_f[0].freed_by = (hy_ready, 1, 0)
        hy_f[1].freed_by = hy_taps[3][1].when_full()
        hy_k = [J(n % 4) for n in range(8)]
        hy_n = [J(0), J(1)]
        hy_pair = [J(n % 4) for n in range(12)]
        for n in range(6):
            hy_w[n].freed_by = hy_pair[2 * n + 1].when_full()
        hy_t = [J(n) for n in range(4)]
        hy_vs = [[J(n) for n in range(4)] for _ in range(2)]
        hy_y = [[J(4), J(5)] for _ in range(2)]
        hy_out, hy_yo = plan_out()
        plan_norm(True)
        rt_job, zt_job, pos_job = J(7), [J(n) for n in range(4)], J(7)

        def plan_moe(banks, ring, used):
            M = {"used": used}
            order, names = [], []

            def j(name, b):
                order.append(b)
                names.append(name)

            for e in range(2):
                for name, b in ((("gather", e, 0), 7 - 6 * e), (("gather", e, 1), 4 - 2 * e), (("st", e), 3 * e)):
                    j(name, b)
            for name in moe_sequence():
                kind, g = name[0], name[1]
                if kind == "gu":
                    j(("g", g), g % 2), j(("u", g), 2 + g % 2)
                elif kind == "t":
                    j(("t", g), 4)
                elif kind == "d" and g % 7 == 0:
                    j(("y", g // 7, 0), 5), j(("y", g // 7, 1), 6)
                elif kind == "s":
                    j(("s", g, name[2]), 7)
            M["j"] = dict(zip(names, loop_jobs(banks, order, NE // 2)))
            cks = loop_chunks(ring, 42, NE // 2)
            M["c"] = {}
            at = 0
            for name in moe_sequence():
                if name[0] == "gu":
                    M["c"]["g", name[1]], M["c"]["u", name[1]] = cks[at], cks[at + 1]
                    cks[at].freed_by = M["j"]["g", name[1]].when_full()
                    cks[at + 1].freed_by = M["j"]["u", name[1]].when_full()
                    at += 2
                elif name[0] == "d":
                    g = name[1]
                    M["c"]["d", g] = cks[at]
                    last = g % 7 == 6
                    cks[at].freed_by = (M["j"]["y", g // 7, 1].when_full() if last
                                        else (used, g + 1 - g // 7, 12))
                    at += 1
            return M

        moe = plan_moe(banks, ring, sem("expert_down_used"))
        banks2 = [Bank(sem, f"again{b}", credit=1) for b in range(8)]
        ring2 = Ring(sem, "again_w", 6)
        moe2 = plan_moe(banks2, ring2, sem("again_down_used"))
        for M, tag in ((moe, "moe"), (moe2, "again")):
            for name in ("upper", "lower", "gathered", "sel", "wsel", "xg", "st", "silu", "hid", "ht", "ye", "acc"):
                M[name] = sem(f"{tag}_{name}")
        plan_norm(True)

        SMALL = 8 * 16

        CAUSAL_TURN = [(256, 0), (0, 128), (128, 256)]

        def causal(q, k, v0, v1, out, first, last, factor, extra=None):
            if first and last:
                values = [(v0, 0, 128, 0, True, True), (v0, 128, 256, 128, True, False), (v1, 256, 384, 128, False, True)]
            elif first:
                values = [(v0, 0, 256, 0, extra is None, False), (v1, 256, 384, 128, False, False)]
            else:
                values = [(v1, 256, 384, 128, False, False), (v0, 0, 256, 0, False, True)]
            return {"scores": [(0, q[:, P:T], k), (256, q[:, 0:P], k[:, 0:P])],
                    "turn": CAUSAL_TURN, "values": values,
                    "rows": [(0, 256, 1), (256, 384, 0)], "width": 384, "out": out, "first": first, "last": last,
                    "factor": factor, "cmp": extra, "scale": HD ** -0.5, "mask": C("mask")}

        Vt = V[:].rearrange("p (t n) -> p t n", t=2)

        def sparse_specs():
            out = []
            for h in range(8):
                p0 = (h % 2) * HD
                out.append(causal(F[p0:p0 + HD, h // 2, :], F[p0:p0 + HD, 4 + h // 2, :],
                                  Vt[:, 0, h * HD:(h + 1) * HD], Vt[:, 1, h * HD:(h + 1) * HD], h, True, True, None))
            for h in range(8):
                g, p0 = h // 4, (h % 2) * HD
                q = F[p0:p0 + HD, 8 + h // 2, :]
                for b in range(2):
                    k = F[p0:p0 + HD, 13 + b, :] if g == h % 2 else Hl[p0:p0 + HD, b * T:(b + 1) * T]
                    v = [Vt[:, t, 512 + b * P + g * HD:512 + b * P + (g + 1) * HD] for t in range(2)]
                    o = 1024 + h * HD
                    extra = (Hl[:, o:o + HD], Hl[:, 512 + g * T:512 + (g + 1) * T]) if b == 0 else None
                    out.append(causal(q, k, v[0], v[1], 8 + h, b == 0, b == 1,
                                      gates[:, :, (1 + b) * 8 + h], extra))
            return out

        def diff_specs():
            out = []
            for h in range(8):
                for c in range(2):
                    p0 = c * HD
                    out.append(causal(F[p0:p0 + HD, h, :], F[p0:p0 + HD, 8 + h, :], Vt[:, 0, h * P:(h + 1) * P],
                                      Vt[:, 1, h * P:(h + 1) * P], h, c == 0, c == 1,
                                      None if c == 0 else lamt[:, 3:4].to_broadcast([P, 2])))
            return out

        def mla_specs():
            out = []
            K8 = Fl[0:96, 2048:6144].rearrange("p (h t) -> p h t", h=8)
            V4 = V[:].rearrange("p (t n) -> p t n", t=4)
            for h in range(8):
                for qt in range(2):
                    out.append({"scores": [(0, F[0:96, h, qt * P:(qt + 1) * P], K8[:, h, :])],
                                "turn": [(n * P, n * P) for n in range(4)],
                                "values": [(V4[:, n, h * HD:(h + 1) * HD], n * P, (n + 1) * P, qt * P, n == 0, n == 3)
                                           for n in range(4)],
                                "rows": [(0, 512, 0)], "width": 512, "out": h, "first": qt == 0, "last": qt == 1,
                                "factor": None, "scale": MLA_SCALE, "mask": None})
            return out

        def heads_to(h):
            return OT[(h % 2) * HD:(h % 2 + 1) * HD, h // 2, :]

        def spectrum(h):
            a_, o = (Fl, 2048) if h == 0 else (scr, 1024)
            return tuple(a_[:, o + n * 1024:o + (n + 1) * 1024].rearrange("p (k n) -> p k n", k=2) for n in range(2))

        def gathered_upper(e):
            return OTlr[:, e * 1024:(e + 1) * 1024].rearrange("p (k n) -> p k n", k=KT)

        def weight_upper(kind, k, n=1):
            if kind == "g":
                w = scrr[:, k * CH:(k + n) * CH]
            else:
                w = Hlr[:, k * CH:(k + n) * CH] if k < 4 else aring0r[:, (k - 4) * CH:(k - 4 + n) * CH]
            return w.rearrange("p (k n) -> p k n", n=CH)

        Hupper = Vr.rearrange("p (k t) -> p k t", k=KT)
        Hlower = Hlr.rearrange("p (k t) -> p k t", k=KT)

        def ff_buffer(kind, q):
            o = (4 if kind == "u" else 0) * 512 + q * 4 * T
            return scrr[:, o:o + 4 * T].rearrange("p (k n) -> p k n", k=4)

        def ff_count(f, n, kind, q, i=None):
            at = 44 * f + 4 * n + (2 if kind == "u" else 0) + q + 1
            return at if i is None else i * 16 + at

        def ff_weights(L, n):
            if n < 8:
                n %= 4
                return L["c"][2 * (n // 2)], L["c"][2 * (n // 2) + 1], CH, (n % 2) * T
            c = 2 * ((n - 8) // 2)
            return L["tc"][c], L["tc"][c + 1], CH if c == 0 else CH // 2, (n % 2) * T

        def part_count(i, g, kind, q):
            return 56 * i + (4 * g + (2 if kind == "u" else 0) + q + 1)

        def gathered_lower(e):
            return Flr[:, e * 1024:(e + 1) * 1024].rearrange("p (k n) -> p k n", k=KT)

        yacc = F[:, 8:16, :]
        ye = Fl[:, 4096:5120]

        def sel(e):
            return Fl[:, 5120 + e * 256:5376 + e * 256].rearrange("p (t n) -> p t n", t=2)

        def wsel(e):
            return Fl[:, 5632 + e * 256:5888 + e * 256].rearrange("p (t n) -> p t n", t=2)

        spare = work[:, 2560:2816]

        def spread_sel(e):
            return tables[:, e, :]

        def window(par, g, half, v):
            src = F[g * HD:(g + 1) * HD, 15 if v else 12, :].rearrange("p (m s) -> p s m", s=16)
            dst = Hl[par * HD:(par + 1) * HD, 512 + 480 * v:992 + 480 * v].rearrange(
                "p (l g n) -> p l g n", l=16, g=2)
            return dst[:, 8 * half:8 * half + 8, g, :], src[:, par::2, half:half + NCMP]

        block = ctx.enter_context(nc.Block())

        @block.sync
        def _(sp):
            def load(c, src, i=None, dst=None):
                c.room(sp, i)
                src = src.rearrange("(k p) n -> p k n", p=P)
                k, n = src.shape[1], src.shape[2]
                dst = wring[:, c.slot, 0:k * n] if dst is None else dst
                sp.dma_start(dst.rearrange("p (k n) -> p k n", n=n), src).then_inc(c.sem, 16)

            def load_ada(c, w, col, i=None):
                load(c, w[:, bass.ds(col, CH)], i, aring[:, c.slot, :])

            def small(dst, src):
                sp.dma_start(dst, src).then_inc(small_loaded, 16)

            small(vec[:], a["vec"])
            small(con[:], a["con"])
            small(posi, a["positions"].to_broadcast([P, T]))
            small(X[:], a["x"])
            small(rw[:], a["router_w_2"][0].rearrange("(k p) e -> p k e", p=P))
            w2 = a["nsa_cmp_w2"][0].rearrange("v (k p) d -> v p k d", p=P)
            for dup in range(2):
                small(cw2[:, 0:256].rearrange("p (k u d) -> p k u d", k=2, u=2)[:, :, dup, :], w2[0])
            small(cw2[:, 256:384].rearrange("p (k d) -> p k d", k=2), w2[1])

            for n in range(2):
                load_ada(ada0[n], a["ada_w"][0], n * CH)
            with sp.Fori(1, 2) as i:
                for n in range(2):
                    load_ada(ada0[n], a["ada_w"][0], i * 2 * CH + n * CH, i)

            w = a["sp_w_in"][0]
            for c, lo, n in zip(sp_w, (0, 512, 1536, 2048, 2560, 1024), (512, 512, 512, 512, 280, 512)):
                load(c, w[:, lo:lo + n])
            sp_const.room(sp)
            sp_more.room(sp)
            sp.dma_start(aring[0:32, sp_const.slot, 0:2048], a["spread"]).then_inc(tables_loaded, 16)
            for v in range(2):
                load(cmp_w[v], a["nsa_cmp_w1"][0, v].rearrange("l d e -> (l d) e"))
            for c, h in zip(sp_out, range(2)):
                load(c, a["sp_w_out"][0][:, h * CH:(h + 1) * CH])

            def ffn_loads(L, wg, wu, wd):
                def body(i, at):
                    for n in range(2):
                        load(L["c"][2 * n], wg[:, bass.ds(at * 2 * CH + n * CH, CH)], i)
                        load(L["c"][2 * n + 1], wu[:, bass.ds(at * 2 * CH + n * CH, CH)], i)
                    for n in range(2):
                        load(L["c"][4 + n], wd[bass.ds(at * 2 * CH + n * CH, CH), :], i)

                body(None, 0)
                with sp.Fori(1, 2) as i:
                    body(i, i)
                tc = L["tc"]
                load(tc[0], wg[:, 4 * CH:5 * CH])
                load(tc[1], wu[:, 4 * CH:5 * CH])
                load(tc[2], wg[:, 5 * CH:FF])
                load(tc[3], wu[:, 5 * CH:FF])
                load(tc[4], wd[4 * CH:5 * CH, :])
                load(tc[5], wd[5 * CH:FF, :])

            ffn_loads(ffn[0], a["ffn_w_gate"][0], a["ffn_w_up"][0], a["ffn_w_down"][0])

            for n, c in enumerate(df_w):
                load(c, a["diff_w_in"][0][:, n * CH:(n + 1) * CH])
            df_const.room(sp)
            df_more.room(sp)
            sp.dma_start(aring[0:32, df_const.slot, 0:2048], a["spread"]).then_inc(tables_loaded, 16)
            for c, h in zip(df_out, range(2)):
                load(c, a["diff_w_out"][0][:, h * CH:(h + 1) * CH])
            ffn_loads(ffn[1], a["ffn_w_gate"][1], a["ffn_w_up"][1], a["ffn_w_down"][1])

            ml_const.room(sp)
            ml_more.room(sp)
            sp.dma_start(aring[:, ml_const.slot, 0:NMLAC], a["mlac"]).then_inc(tables_loaded, 16)
            sp.dma_start(aring[:, ml_const.slot, NMLAC:NMLAC + 512].rearrange("p (g d) -> p g d", g=4),
                         a["pool_w_2"][0].rearrange("g c d -> c g d")).then_inc(tables_loaded, 16)
            mod_job[2].emptied(sp)
            sp.dma_start(F[:, 16:24, :], a["ctx_2"]).then_inc(ctx_loaded, 16)
            w = a["mix_in_w_2"][0]
            load(ml_w[0], w[:, 0:512])
            load(ml_w[1], w[:, 512:1024])
            load(ml_w[2], w[:, 960:1056])
            load(ml_w[3], a["q_up_2"][0])
            src = a["kv_up_2"][0].rearrange("(k p) n -> p k n", p=P)
            sp.dma_start(wring[:, ml_w[3].slot, 1536:3584].rearrange("p (k n) -> p k n", k=2),
                         src).then_inc(ml_w[3].sem, 16)
            for c, h in zip(ml_out, range(2)):
                load(c, a["mix_out_w_2"][0][:, h * CH:(h + 1) * CH])
            ffn_loads(ffn[2], a["ffn_gate_2"][0], a["ffn_up_2"][0], a["ffn_down_2"][0])

            hy_const.room(sp)
            hy_more.room(sp)
            hc = aring[:, hy_const.slot, :]
            sp.dma_start(hc[:, 0:NHYC], a["hyc"]).then_inc(tables_loaded, 16)
            o = HYC["before"][0]
            sp.dma_start(hc[:, o:o + 320], a["routing"]).then_inc(tables_loaded, 16)
            o = HYC["fw"][0]
            sp.dma_start(hc[0:33, o:o + 64], a["hy_fw1_2"][0]).then_inc(tables_loaded, 16)
            sp.dma_start(hc[0:64, o + 64:o + 128], a["hy_fw2_2"][0]).then_inc(tables_loaded, 16)
            sp.dma_start(hc[0:64, o + 128:o + 192], a["hy_fw3_2"][0]).then_inc(tables_loaded, 16)
            hy_f[0].room(sp)
            sp.dma_start(wring[:, hy_f[0].slot, :], a["decay"]).then_inc(hy_f[0].sem, 16)
            hy_f[1].room(sp)
            sp.dma_start(wring[0:64, hy_f[1].slot, 0:2 * D], a["hy_fout_2"][0]).then_inc(hy_f[1].sem, 16)
            for n, c in enumerate(hy_w):
                load(c, a["hy_in_w_2"][0][:, n * CH:(n + 1) * CH])
            for c, h in zip(hy_out, range(2)):
                load(c, a["hy_out_w_2"][0][:, h * CH:(h + 1) * CH])

            def moe_loads(M, dst_ring):
                gate = a["moe_gate_2"][0].rearrange("e (k p) n -> p k e n", p=P)
                up = a["moe_up_2"][0].rearrange("e (k p) n -> p k e n", p=P)
                down = a["moe_down_2"][0].rearrange("e (s k p) n -> p k (e s) n", k=4, p=P)

                def body(i, at):
                    for name in moe_sequence():
                        g = name[1]
                        e, s = g // 7, g % 7
                        if name[0] == "gu":
                            for kind, src in (("g", gate), ("u", up)):
                                c = M["c"][kind, g]
                                c.room(sp, i)
                                sp.dma_start(w3(c), src[:, :, bass.ds(2 * at + e, 1), s * CH:(s + 1) * CH]
                                             .rearrange("p k e n -> p k (e n)")).then_inc(c.sem, 16)
                        elif name[0] == "d":
                            c = M["c"]["d", g]
                            c.room(sp, i)
                            sp.dma_start(w3(c, D, 4), down[:, :, bass.ds(14 * at + g, 1), :]
                                         .rearrange("p k e n -> p k (e n)")).then_inc(c.sem, 16)

                body(None, 0)
                with sp.Fori(1, NE // 2) as i:
                    body(i, i)

            moe_loads(moe, ring)
            sp.wait_ge(flag_ready, 1)
            with sp.If(sp.value_load(flag[0:1, 0:1], min_val=0, max_val=1) > 0):
                moe["j"]["y", 1, 1].filled(sp, NE // 2 - 1)
                moe_loads(moe2, ring2)
            sp.wait_ge(x_ready, 4)
            sp.dma_start(out, X[:]).then_inc(out_stored, 16)
            sp.wait_ge(out_stored, 16)

        @block.gpsimd
        def _(pool):
            def load_half(c, w, col, i=None):
                c.room(pool, i)
                pool.dma_start(ada_half(c), w[:, bass.ds(col, T)].rearrange("(k p) n -> p k n", p=P)).then_inc(c.sem, 16)

            for n, c in enumerate(ada1):
                load_half(c, a["ada_w"][0], (8 + n) * T)
            for L, w in ((ffn[0], a["ada_w"][1]), (ffn[1], a["ada_w_2"][0]), (ffn[2], a["ada_w_2"][1])):
                for c, (_, col, step, _) in zip(L["a"], ADA_BODY):
                    load_half(c, w, col)
                with pool.Fori(1, 2) as i:
                    for c, (_, col, step, _) in zip(L["a"], ADA_BODY):
                        load_half(c, w, i * step + col, i)
                for c, (_, col) in zip(L["ta"], ADA_TAIL):
                    load_half(c, w, col)

        @block.tensor
        def _(pe):
            def mm(dst, lhsT, rhs, start=True, stop=True, **kw):
                return pe.matmul(dst, lhsT, rhs, start=start, stop=stop, **kw)

            def fill(job, ins, i=None):
                ins.then_inc(job.bank.full, 1)

            def reduce_mod(layer, lo=0, hi=48):
                job = mod_job[layer]
                if lo == 0:
                    job.open(pe)
                    pe.wait_ge(ada_used, 20 + 24 * layer if layer else 4)
                for t in range(lo, hi if layer else 16):
                    last = mm(PS[job.b][:, t:t + 1], Fl[:, t * P:(t + 1) * P], C("ones")[:, 0:1])
                if hi < 48:
                    return
                if layer == 2:
                    for t in range(16):
                        last = mm(PS[job.b][:, 64 + t:65 + t], OTl[:, t * P:(t + 1) * P], C("ones")[:, 0:1])
                fill(job, last)

            def reduce_more():
                mod_more.open(pe)
                pe.wait_ge(ada_used, 20)
                for t in range(32):
                    last = mm(PS[mod_more.b][:, t:t + 1], scr[:, t * P:(t + 1) * P], C("ones")[:, 0:1])
                fill(mod_more, last)

            def sum_features(job, src, need, count):
                job.open(pe)
                pe.wait_ge(need, count)
                for k in range(KT):
                    last = mm(PS[job.b][:, 0:T], C("ones"), src[:, k, :], k == 0, k == KT - 1)
                fill(job, last)

            def norm(n, sq_count):
                jobs = norm_job[n]
                if len(jobs) == 2:
                    sum_features(jobs[0], X, x_ready_raw, n - 3)
                sum_features(jobs[-1], H, sq_ready, sq_count)

            def tile(dst, w, lo, rhs):
                rows = dst.shape[0]
                for k in range(KT):
                    last = mm(dst, w[:, k, lo:lo + rows], rhs[:, k, :], k == 0, k == KT - 1)
                return last

            def by_token(dst, w, lo, n, src, qt):
                for k in range(w.shape[1]):
                    last = mm(dst, src[:, k, qt * P:(qt + 1) * P], w[:, k, lo:lo + n], k == 0, k == w.shape[1] - 1)
                return last

            def head_sums(job, j, copied, tiles, total, full):
                pe.wait_ge(proj_copied, copied)
                for m, t in enumerate(tiles):
                    last = mm(PS[job.b][0:32, 0:T], C("half")[:, 32 - 2 * t:64 - 2 * t],
                              work[:, (j % 2) * 512 + m * T:(j % 2) * 512 + (m + 1) * T], t == 0, t == total - 1)
                if full:
                    fill(job, last)
                else:
                    last.then_inc(stat_summed, 1)

            def rope(rp, base, tiles, table):
                _, bc, ro = rp
                pe.wait_ge(rh_ready, base // 8 + 1)
                pe.wait_ge(tables_loaded, SP_TABLE if base == 0 else DF_TABLE)
                for j in range(9):
                    if j < 8:
                        bc[j].open(pe)
                        for m in range(2):
                            if 2 * j + m < tiles:
                                t = 2 * j + m
                                last = mm(PS[bc[j].b][:, m * T:(m + 1) * T],
                                          aring[0:32, table.slot, t * P:(t + 1) * P], rheads)
                        fill(bc[j], last)
                    if j >= 1:
                        n = min(2, tiles - 2 * (j - 1)) * T
                        ro[j - 1].open(pe)
                        bc[j - 1].emptied(pe)
                        fill(ro[j - 1], mm(PS[ro[j - 1].b][:, 0:n], C("rot"), Fl[:, (j - 1) * 512:(j - 1) * 512 + n]))

            def units(plan, specs, base):
                s, t, o = plan
                for i in range(len(specs) + 3):
                    if i < len(specs):
                        s[i].open(pe)
                        for dst, q, k in specs[i]["scores"]:
                            last = mm(PS[s[i].b][:, dst:dst + k.shape[-1]], q, k)
                        fill(s[i], last)
                    if 0 <= i - 2 < len(specs):
                        u = i - 2
                        t[u].open(pe)
                        pe.wait_ge(p_ready, base + u + 1)
                        pr = work[:, 1024 + (u % 2) * 512:1024 + (u % 2 + 1) * 512]
                        for src, dst in specs[u]["turn"]:
                            last = pe.transpose(PS[t[u].b][:, dst:dst + P], pr[:, src:src + P], C("ident"))
                        fill(t[u], last)
                    if i >= 3:
                        u = i - 3
                        sp_ = specs[u]
                        job = o[sp_["out"]]
                        if sp_["first"]:
                            job.open(pe)
                            if sp_.get("cmp") is not None:
                                mm(PS[job.b][0:HD, 0:T], *sp_["cmp"], True, False)
                        t[u].emptied(pe)
                        pt = work[:, 2048 + (u % 2) * 512:2048 + (u % 2 + 1) * 512]
                        for v, lo, hi, dst, start, stop in sp_["values"]:
                            last = mm(PS[job.b][0:v.shape[-1], dst:dst + hi - lo], v, pt[:, lo:hi], start, stop)
                        if sp_["last"]:
                            fill(job, last)
                        else:
                            last.then_inc(pv_done, 1)

            def project_out(cks, jobs, src):
                for j in range(4):
                    if j % 2 == 0:
                        cks[j // 2].loaded(pe)
                    jobs[j].open(pe)
                    for m in range(2):
                        last = tile(PS[jobs[j].b][:, m * T:(m + 1) * T], w3(cks[j // 2]), (j % 2) * T + m * P, src)
                    fill(jobs[j], last)

            def hidden_pair(jg, ju, f, L, n, i=None):
                cg, cu, width, lo = ff_weights(L, n)
                for kind, job, c in (("g", jg, cg), ("u", ju, cu)):
                    job.open(pe, i)
                    w = w3r(c, width)
                    for m in range(2):
                        dst = PS[job.b][:, m * T:(m + 1) * T]
                        for k in range(KT):
                            if m == 0 and k % 4 == 0:
                                pe.wait_ge(ff_upper, ff_count(f, n, kind, k // 4, i))
                            wu = ff_buffer(kind, k // 4)[:, k % 4, m * P:(m + 1) * P]
                            mm(dst, wu, Hupper[:, k, :], k == 0, False)
                        if n == 0 and m == 0 and kind == "g":
                            pe.wait_ge(h_split, 2 * f + 2)
                        for k in range(KT):
                            mm(dst, ff_buffer(kind, k // 4)[:, k % 4, m * P:(m + 1) * P], Hlower[:, k, :], False, False)
                        for k in range(KT):
                            if m == 0 and k % 4 == 0:
                                pe.wait_ge(ff_lower, ff_count(f, n, kind, k // 4, i))
                            last = mm(dst, w[:, k, lo + m * P:lo + (m + 1) * P], Hupper[:, k, :],
                                      False, k == KT - 1)
                    fill(job, last)

            def down(c, buf, tiles, i=None, full=None):
                c.loaded(pe, i)
                for kt in range(tiles):
                    for o in range(KT):
                        last = mm(PS[4 + o // 2][:, (o % 2) * T:(o % 2 + 1) * T],
                                  w3(c, D, tiles)[:, kt, o * P:(o + 1) * P],
                                  work[:, buf * 1024 + kt * T:buf * 1024 + (kt + 1) * T],
                                  False, full is not None and kt == tiles - 1 and o % 2 == 1)
                        if full is not None and kt == tiles - 1 and o % 2 == 1:
                            fill(full[o // 2], last)
                if full is None:
                    last.then_inc(down_used, 1)

            def feed_forward(f, L):
                for job in L["y"]:
                    job.open(pe)
                    mm(PS[job.b][:, :], zero[:], con[:, 0:2 * P].bitcast(BF16), True, False)
                pe.wait_ge(h_split, 2 * f + 1)
                with pe.Fori(0, 2) as i:
                    for n in range(4):
                        hidden_pair(L["j"][2 * n], L["j"][2 * n + 1], f, L, n, i)
                    for n in range(2):
                        pe.wait_ge(hid_done, 2 + 11 * f + 2 * (n + 1) + i * 4)
                        down(L["c"][4 + n], n, 4, i)
                tj, tc = L["tj"], L["tc"]
                for n in range(3):
                    hidden_pair(tj[2 * n], tj[2 * n + 1], f, L, 8 + n)
                pe.wait_ge(hid_done, 2 + 11 * f + 10)
                down(tc[4], 0, 4)
                pe.wait_ge(hid_done, 2 + 11 * f + 11)
                down(tc[5], 1, 2, full=L["y"])

            pe.wait_ge(small_loaded, SMALL)
            pe.wait_ge(zero_ready, 1)
            reduce_mod(0)
            norm(0, 1)
            pe.wait_ge(h_ready, 1)
            at = {12: (3, 0), 13: (3, 256), 14: (4, 0), 15: (3, 128)}
            for j in range(9):
                if j < 8:
                    sp_pair[j].open(pe)
                    for m in range(2):
                        t = 2 * j + m
                        c, lo = at.get(t, (t // 4, (t % 4) * P))
                        sp_w[c].loaded(pe)
                        last = tile(PS[sp_pair[j].b][:, m * T:(m + 1) * T], w3(sp_w[c], 280 if c == 4 else CH), lo, H)
                    fill(sp_pair[j], last)
                if j >= 1:
                    if j == 1:
                        sp_rope[0].open(pe)
                    head_sums(sp_rope[0], j - 1, j, [t for t in (2 * j - 2, 2 * j - 1) if t < 15], 15, j == 8)
            for qt in range(2):
                sp_tok[qt].open(pe)
                b = PS[sp_tok[qt].b]
                by_token(b[:, 0:P], w3(sp_w[3]), 384, P, H, qt)
                fill(sp_tok[qt], by_token(b[:, P:P + 152], w3(sp_w[4], 280), P, 152, H, qt))
            sp_w[5].loaded(pe)
            for qt in range(2):
                sp_v[qt].open(pe)
                fill(sp_v[qt], by_token(PS[sp_v[qt].b][:, :], w3(sp_w[5]), 0, CH, H, qt))
            rope(sp_rope, 0, 15, sp_const)

            reduce_more()
            pe.wait_ge(blocks_ready, 2)
            hid_job.open(pe)
            for v in range(2):
                cmp_w[v].loaded(pe)
                blk = Hl[:, 512 + 480 * v:992 + 480 * v].rearrange("p (l n) -> p l n", l=16)
                wv = wring[:, cmp_w[v].slot, :].rearrange("p (l e) -> p l e", l=16)
                for et in range(2):
                    for l2 in range(16):
                        o = v * 60 + et * 30
                        last = mm(PS[hid_job.b][:, o:o + 30], wv[:, l2, et * P:(et + 1) * P], blk[:, l2, :],
                                  l2 == 0, l2 == 15)
            fill(hid_job, last)
            hid_job.emptied(pe)
            kvc_job.open(pe)
            hid = Hl[:, 1792:1912].rearrange("p (v e n) -> p v e n", v=2, e=2)
            for et in range(2):
                mm(PS[kvc_job.b][:, 0:30], cw2[:, et * P:(et + 1) * P], hid[:, 0, et, :], et == 0, et == 1)
            pe.wait_ge(hidrep_ready, 1)
            rep = Hl[:, 512:1024].rearrange("p (e g m) -> p e g m", e=2, g=2)
            for g in range(2):
                for et in range(2):
                    last = mm(PS[kvc_job.b][:, 64 + 64 * g:128 + 64 * g], rep[:, et, g, :],
                              cw2[:, 256 + 64 * et:320 + 64 * et], et == 0, et == 1)
            fill(kvc_job, last)
            kvc_job.emptied(pe)
            pe.wait_ge(rope_done, 8)
            cs_job.open(pe)
            for par in range(2):
                for h, qt in ((h, qt) for h in range(par, 8, 2) for qt in range(2)):
                        g, jj = h // 4, h % 4
                        p0 = par * HD
                        o = ((g * 2 + qt) * 4 + jj) * 32
                        last = mm(PS[cs_job.b][:, o:o + NCMP], F[p0:p0 + HD, 8 + h // 2, qt * P:(qt + 1) * P],
                                  Hl[p0:p0 + HD, 1600 + g * NCMP:1600 + (g + 1) * NCMP])
                if par == 0:
                    last.then_inc(rows_done, 1)
                    pe.wait_ge(rows_done, 1)
            fill(cs_job, last)
            pe.wait_ge(cp_ready, 1)
            ct_job.open(pe)
            for g in range(2):
                for qt in range(2):
                    o = (g * 2 + qt) * P
                    last = pe.transpose(PS[ct_job.b][:, o:o + P], Hl[:, 1024 + o:1024 + o + P], C("ident"))
            fill(ct_job, last)
            ct_job.emptied(pe)
            pe.wait_ge(ksw_ready, 1)
            pe.wait_ge(vrows_ready, 1)
            sp_v[1].emptied(pe)
            units(sp_units, sparse_specs(), 0)
            sp_units[2][-1].emptied(pe)
            project_out(sp_out, sp_y, OT)
            norm(1, 2)
            feed_forward(0, ffn[0])
            reduce_mod(1, 0, 24)

            norm(2, 3)
            reduce_mod(1, 24)
            pe.wait_ge(h_ready, 3)
            for j in range(9):
                if j < 8:
                    if j % 2 == 0:
                        df_w[j // 2].loaded(pe)
                    df_pair[j].open(pe)
                    for m in range(2):
                        last = tile(PS[df_pair[j].b][:, m * T:(m + 1) * T], w3(df_w[j // 2]), (j % 2) * T + m * P, H)
                    fill(df_pair[j], last)
                if j >= 1:
                    if j == 1:
                        df_rope[0].open(pe)
                    head_sums(df_rope[0], j - 1, 8 + j, (2 * j - 2, 2 * j - 1), 16, j == 8)
            for n in range(4):
                df_w[4 + n // 2].loaded(pe)
                df_v[n].open(pe)
                fill(df_v[n], by_token(PS[df_v[n].b][:, :], w3(df_w[4 + n // 2]), 0, CH, H, n % 2))
            rope(df_rope, 8, 16, df_const)
            pe.wait_ge(lam_prod, 1)
            lam_job.open(pe)
            fill(lam_job, mm(PS[lam_job.b][:, 0:2], C("ones")[0:HD, :], lamt[0:HD, 0:2]))
            pe.wait_ge(rope_done, 16)
            df_v[3].emptied(pe)
            units(df_units, diff_specs(), 24)
            pe.wait_ge(sq_ready, 4)
            on_stat.open(pe)
            for t in range(KT):
                last = mm(PS[on_stat.b][0:32, 0:T], C("whole")[:, 32 - t:64 - t], H[:, t, :], t == 0, t == KT - 1)
            fill(on_stat, last)
            pe.wait_ge(rh_ready, 3)
            for j in range(4):
                on_bc[j].open(pe)
                for m in range(2):
                    t = 2 * j + m
                    last = mm(PS[on_bc[j].b][:, m * T:(m + 1) * T],
                              C("ident")[0:32, t:t + 1].to_broadcast([32, P]), rheads)
                fill(on_bc[j], last)
            on_bc[3].emptied(pe)
            project_out(df_out, df_y, OT)
            norm(3, 5)
            feed_forward(1, ffn[1])
            reduce_mod(2)

            pe.wait_ge(h_ready, 5)
            for qt in range(2):
                ml_w[0].loaded(pe)
                ml_pool[qt].open(pe)
                fill(ml_pool[qt], by_token(PS[ml_pool[qt].b][:, :], w3(ml_w[0]), 0, CH, H, qt))
            ml_w[1].loaded(pe)
            ml_lat[0].open(pe)
            for m in range(2):
                last = tile(PS[ml_lat[0].b][:, m * T:(m + 1) * T], w3(ml_w[1]), m * P, H)
            fill(ml_lat[0], last)
            pe.wait_ge(lat_ready, 1)
            UC = F[:, 8:16, :]
            for m in range(2):
                ml_lat[1 + m].open(pe)
                tile(PS[ml_lat[1 + m].b][:, 0:T], w3(ml_w[1]), (2 + m) * P, UC)
                fill(ml_lat[1 + m], tile(PS[ml_lat[1 + m].b][:, T:2 * T], w3(ml_w[1]), (2 + m) * P, H))
            ml_w[2].loaded(pe)
            ml_kr.open(pe)
            tile(PS[ml_kr.b][0:96, 0:T], w3(ml_w[2], 96), 0, UC)
            fill(ml_kr, tile(PS[ml_kr.b][0:96, T:2 * T], w3(ml_w[2], 96), 0, H))
            pe.wait_ge(proj_copied, 17)
            ml_stat[0].open(pe)
            for m in range(2):
                last = mm(PS[ml_stat[0].b][:, 0:T], C("ones"), work[:, m * T:(m + 1) * T], m == 0, m == 1)
            fill(ml_stat[0], last)
            pe.wait_ge(proj_copied, 19)
            ml_stat[1].open(pe)
            for m in range(2):
                last = mm(PS[ml_stat[1].b][:, :], C("ones"), work[:, 512 + m * 512:1024 + m * 512], m == 0, m == 1)
            fill(ml_stat[1], last)
            pe.wait_ge(tables_loaded, ML_TABLE)
            mc = aring[:, ml_const.slot, :]
            ml_pool[1].emptied(pe)
            pm = mc[:, 0:2048].rearrange("p (s g t) -> p s g t", s=2, g=4)
            for n in range(2):
                ml_d[n].open(pe)
                for m in range(2):
                    g = 2 * n + m
                    for s in range(2):
                        last = mm(PS[ml_d[n].b][:, m * T:(m + 1) * T],
                                  scr[:, 2048 + s * 512 + g * P:2048 + s * 512 + (g + 1) * P], pm[:, s, g, :],
                                  s == 0, s == 1)
                fill(ml_d[n], last)
            for n in range(2):
                ml_d[n].emptied(pe)
                ml_py[n].open(pe)
                for m in range(2):
                    g = 2 * n + m
                    last = mm(PS[ml_py[n].b][:, m * T:(m + 1) * T], mc[:, NMLAC + g * P:NMLAC + (g + 1) * P],
                              scr[:, 3072 + g * T:3072 + (g + 1) * T])
                fill(ml_py[n], last)
            pe.wait_ge(lat_ready, 2)
            ml_w[3].loaded(pe)
            qu = wring[:, ml_w[3].slot, 0:1536].rearrange("p (k n) -> p k n", k=2)
            ku = wring[:, ml_w[3].slot, 1536:3584].rearrange("p (k h n) -> p k h n", k=2, h=8)
            QL = scr[:, 0:512].rearrange("p (k t) -> p k t", k=2)
            KV = scr[:, 512:1536].rearrange("p (k t) -> p k t", k=2)
            for j in range(5):
                if j < 4:
                    ml_q[j].open(pe)
                    for m in range(2):
                        h = 2 * j + m
                        for k in range(2):
                            last = mm(PS[ml_q[j].b][0:96, m * T:(m + 1) * T], qu[:, k, h * 96:(h + 1) * 96],
                                      QL[:, k, :], k == 0, k == 1)
                    fill(ml_q[j], last)
                if j >= 1:
                    ml_qr[j - 1].open(pe)
                    ml_q[j - 1].emptied(pe)
                    fill(ml_qr[j - 1], mm(PS[ml_qr[j - 1].b][0:96, :], mc[0:96, 2048:2144],
                                          Fl[0:96, (j - 1) * 512:j * 512]))
            ml_krr.open(pe)
            ml_kr.emptied(pe)
            fill(ml_krr, mm(PS[ml_krr.b][0:96, 0:T], mc[0:96, 2048:2144], scr[0:96, 1792:2048]))
            for h in range(8):
                ml_k[h].open(pe)
                for k in range(2):
                    last = mm(PS[ml_k[h].b][0:HD, :], ku[:, k, h, 0:HD], KV[:, k, :], k == 0, k == 1)
                fill(ml_k[h], last)
            for n in range(4):
                ml_v[n].open(pe)
                for k in range(2):
                    last = mm(PS[ml_v[n].b][:, :], KV[:, k, n * P:(n + 1) * P], ku[:, k, :, HD:P], k == 0, k == 1)
                fill(ml_v[n], last)
            pe.wait_ge(rope_done, 16 + 6)
            ml_k[7].emptied(pe)
            ml_v[3].emptied(pe)
            units(ml_units, mla_specs(), 40)
            ml_units[2][-1].emptied(pe)
            ml_py[1].emptied(pe)
            project_out(ml_out, ml_y, OT)
            norm(4, 6)
            feed_forward(2, ffn[2])
            reduce_mod(3, 0, 20)
            sum_features(norm_job[5][0], X, x_ready_raw, 2)
            reduce_mod(3, 20, 34)
            sum_features(norm_job[5][1], H, sq_ready, 7)
            reduce_mod(3, 34)

            pe.wait_ge(tables_loaded, HY_TABLE)
            hc = aring[:, hy_const.slot, :]
            o = HYC["fw"][0]
            for n in range(3):
                if n:
                    pe.wait_ge(sin_done, 2 + n)
                rows = 33 if n == 0 else 64
                src = hc[0:33, 2560:2816] if n == 0 else work[0:64, 0:T]
                hy_sin[n].open(pe)
                fill(hy_sin[n], mm(PS[hy_sin[n].b][0:64, 0:T], hc[0:rows, o + 64 * n:o + 64 * (n + 1)], src))
            pe.wait_ge(sin_done, 5)
            hy_f[1].loaded(pe)
            fo = wring[0:64, hy_f[1].slot, 0:2 * D]
            for n in range(4):
                for d in range(2):
                    hy_taps[n][d].open(pe)
                    fill(hy_taps[n][d], mm(PS[hy_taps[n][d].b][:, :], work[0:64, (n // 2) * P:(n // 2 + 1) * P],
                                           fo[:, d * D + (n % 2) * 512:d * D + (n % 2 + 1) * 512]))

            def table(name):
                return hc[:, HYC[name][0]:HYC[name][0] + 512].rearrange("p (k n) -> p k n", k=2)

            taps = [Fl[:, 0:2048].rearrange("p (k n) -> p k n", k=2), Fl[:, 2048:4096].rearrange("p (k n) -> p k n", k=2)]
            pe.wait_ge(hy_ready, 1)
            for n in range(8):
                f, h, im = n // 4, n // 2 % 2, n % 2
                hy_k[n].open(pe)
                for k in range(2):
                    last = mm(PS[hy_k[n].b][:, :], table("fs" if im else "fr")[:, k, f * P:(f + 1) * P],
                              taps[im][:, k, h * 512:(h + 1) * 512], k == 0, k == 1)
                fill(hy_k[n], last)
            for h in range(2):
                hy_n[h].open(pe)
                for k in range(2):
                    last = mm(PS[hy_n[h].b][0:1, :], hc[:, 2816:2817], taps[0][:, k, h * 512:(h + 1) * 512], k == 0, k == 1)
                fill(hy_n[h], last)
            pe.wait_ge(h_ready, 7)
            for j in range(12):
                if j % 2 == 0:
                    hy_w[j // 2].loaded(pe)
                hy_pair[j].open(pe)
                for m in range(2):
                    last = tile(PS[hy_pair[j].b][:, m * T:(m + 1) * T], w3(hy_w[j // 2]), (j % 2) * T + m * P, H)
                fill(hy_pair[j], last)
            pe.wait_ge(hy_ready, 2)
            for n in range(4):
                hy_t[n].open(pe)
                for m in range(4):
                    ct = (n % 2) * 4 + m
                    last = pe.transpose(PS[hy_t[n].b][:, m * P:(m + 1) * P],
                                        F[:, 16 + ct, (n // 2) * P:(n // 2 + 1) * P], C("ident"))
                fill(hy_t[n], last)
            hy_t[3].emptied(pe)
            vt = Hl.rearrange("p (k n) -> p k n", k=2)
            for h in range(2):
                for n in range(4):
                    f, im = n // 2, n % 2
                    job = hy_vs[h][n]
                    job.open(pe)
                    for k in range(2):
                        last = mm(PS[job.b][:, :], table("fi" if im else "fr")[:, k, f * P:(f + 1) * P],
                                  vt[:, k, h * 512:(h + 1) * 512], k == 0, k == 1)
                    fill(job, last)
            for h in range(2):
                pe.wait_ge(spec_ready, h + 1)
                re, im = spectrum(h)
                for n in range(2):
                    job = hy_y[h][n]
                    job.open(pe)
                    for m in range(2):
                        lo = (2 * n + m) * P
                        parts = [(s, g, f) for f in range(2) for s, g in ((re, "gr"), (im, "gi"))]
                        for q, (s, g, f) in enumerate(parts):
                            last = mm(PS[job.b][:, m * T:(m + 1) * T], s[:, f, lo:lo + P], table(g)[:, f, :], q == 0, q == 3)
                    fill(job, last)
            pe.wait_ge(hy_ready, 3)
            project_out(hy_out, hy_yo, F)
            norm(6, 8)

            pe.wait_ge(h_ready, 8)
            rt_job.open(pe)
            for qt in range(2):
                for k in range(KT):
                    last = mm(PS[7][:, qt * 8:qt * 8 + 8], H[:, k, qt * P:(qt + 1) * P], rw[:, k, :], k == 0, k == KT - 1)
            fill(rt_job, last)
            for n in range(4):
                zt_job[n].open(pe)
                for m in range(4):
                    k = (n % 2) * 4 + m
                    last = pe.transpose(PS[zt_job[n].b][:, m * P:(m + 1) * P], H[:, k, (n // 2) * P:(n // 2 + 1) * P], C("ident"))
                fill(zt_job[n], last)
            pe.wait_ge(route_ready, 1)
            pos_job.open(pe)
            mm(PS[7][:, 0:8], R("before"), ch8[:, 0, :])
            for o, lhs in ((8, R("before")), (16, C("ones"))):
                mm(PS[7][:, o:o + 8], C("ones"), ch8[:, 0, :], True, False)
                last = mm(PS[7][:, o:o + 8], lhs, ch8[:, 1, :], False, True)
            fill(pos_job, last)
            zt_job[3].emptied(pe)

            def experts(M):
                J_, K_ = M["j"], M["c"]
                ztok = V[:].rearrange("p (t n) -> p t n", t=2)
                with pe.Fori(0, NE // 2) as i:
                    for e in range(2):
                        pe.wait_ge(M["sel"], 2 * i + e + 1)
                        for q in range(2):
                            job = J_["gather", e, q]
                            job.open(pe, i)
                            for m in range(4):
                                for t in range(2):
                                    last = mm(PS[job.b][:, m * P:(m + 1) * P], ztok[:, t, (4 * q + m) * P:(4 * q + m + 1) * P],
                                              sel(e)[:, t, :], t == 0, t == 1)
                            fill(job, last)
                        job = J_["st", e]
                        job.open(pe, i)
                        pe.wait_ge(M["wsel"], 2 * i + e + 1)
                        for t in range(2):
                            last = pe.transpose(PS[job.b][:, t * P:(t + 1) * P], wsel(e)[:, t, :], C("ident"))
                        fill(job, last)
                    for name in moe_sequence():
                        kind, g = name[0], name[1]
                        if kind == "gu":
                            if g % 7 == 0:
                                J_["gather", g // 7, 1].emptied(pe, i)
                            for w in ("g", "u"):
                                J_[w, g].open(pe, i)
                                dst, e = PS[J_[w, g].b][:, :], g // 7
                                for k in range(KT):
                                    if k % 4 == 0:
                                        pe.wait_ge(M["upper"], part_count(i, g, w, k // 4))
                                    wu = weight_upper(w, k)[:, 0, :]
                                    mm(dst, gathered_upper(e)[:, k, :], wu, k == 0, False)
                                    mm(dst, gathered_lower(e)[:, k, :], wu, False, False)
                                for k in range(KT):
                                    if k % 4 == 0:
                                        pe.wait_ge(M["lower"], part_count(i, g, w, k // 4))
                                    last = mm(dst, gathered_upper(e)[:, k, :], w3r(K_[w, g])[:, k, :],
                                              False, k == KT - 1)
                                fill(J_[w, g], last)
                        elif kind == "t":
                            J_["t", g].open(pe, i)
                            pe.wait_ge(M["hid"], 14 * i + g + 1)
                            for m in range(4):
                                last = pe.transpose(PS[4][:, m * P:(m + 1) * P],
                                                    work[:, (g % 2) * 512 + m * P:(g % 2) * 512 + (m + 1) * P], C("ident"))
                            fill(J_["t", g], last)
                        elif kind == "d":
                            e = g // 7
                            y = J_["y", e, 0], J_["y", e, 1]
                            if g % 7 == 0:
                                y[0].open(pe, i)
                                y[1].open(pe, i)
                            K_["d", g].loaded(pe, i)
                            J_["t", g].emptied(pe, i)
                            ht = work[:, 1024 + (g % 2) * 512:1536 + (g % 2) * 512].rearrange("p (k n) -> p k n", k=4)
                            for k in range(4):
                                for h in range(2):
                                    last = mm(PS[5 + h][:, :], ht[:, k, :], w3(K_["d", g], D, 4)[:, k, h * 512:(h + 1) * 512],
                                              g % 7 == 0 and k == 0, g % 7 == 6 and k == 3)
                                    if g % 7 == 6 and k == 3:
                                        fill(y[h], last)
                            if g % 7 != 6:
                                last.then_inc(M["used"], 1)
                        else:
                            e, q = name[1], name[2]
                            job = J_["s", e, q]
                            job.open(pe, i)
                            if q == 0:
                                J_["y", e, 1].emptied(pe, i)
                                J_["st", e].emptied(pe, i)
                            for m in range(2):
                                k = 2 * q + m
                                last = mm(PS[7][:, m * T:(m + 1) * T], ye[:, k * P:(k + 1) * P], spread_sel(e))
                            fill(job, last)

            experts(moe)
            pe.wait_ge(flag_ready, 1)
            with pe.If(pe.value_load(flag[0:1, 0:1], min_val=0, max_val=1) > 0):
                for job in (moe["j"]["s", 1, 3], moe["j"]["y", 1, 1], moe["j"]["t", 13], moe["j"]["u", 13], moe["j"]["u", 12]):
                    job.emptied(pe, NE // 2 - 1)
                experts(moe2)
            norm(7, 9)

        @block.scalar
        def _(act):
            def copy(dst, src, **kw):
                return act.activation(dst, src, ACT.Copy, **kw)

            def root(dst, src, n, eps):
                return act.activation(dst, src, ACT.Sqrt, bias=eps, scale=1.0 / n)

            def norm(n, eps="rms_eps"):
                norm_job[n][-1].filled(act)
                root(rstd[:], PS[6][:, 0:T], D, C(eps)).then_inc(norm_job[n][-1].bank.free, 1)

            def project(jobs, base, tiles):
                for j, job in enumerate(jobs):
                    job.filled(act)
                    if j >= 2:
                        act.wait_ge(stat_summed, (7 if base else 0) + j - 1)
                    n = min(2, tiles - 2 * j) * T
                    sq = act.activation(work[:, (j % 2) * 512:(j % 2) * 512 + n], PS[job.b][:, 0:n], ACT.Square)
                    sq.then_inc(proj_copied, 1)
                    copy(Fl[:, j * 512:(j + 1) * 512], PS[job.b][:, :]).then_inc(job.bank.free, 1)

            def head_root(job, n, rows=32):
                job.filled(act)
                root(rheads[0:rows, :], PS[job.b][0:rows, 0:T], n, C("rms_eps", rows)).then_inc(job.bank.free, 1)

            def units(plan, specs, base, place, pv_base):
                s, t, o = plan
                pv = pv_base
                for i in range(len(specs) + 3):
                    if 0 <= i - 2 < len(specs):
                        u = i - 2
                        t[u].filled(act)
                        if u >= 2:
                            sp_ = specs[u - 2]
                            if sp_["last"]:
                                o[sp_["out"]].filled(act)
                            else:
                                pv += 1
                                act.wait_ge(pv_done, pv)
                        w = specs[u]["width"]
                        copy(work[:, 2048 + (u % 2) * 512:2048 + (u % 2) * 512 + w],
                             PS[t[u].b][:, 0:w]).then_inc(t[u].bank.free, 1)
                    if i < len(specs):
                        sp_ = specs[i]
                        b = i % 2
                        act.wait_ge(nmax_ready, base + i + 1)
                        for n, (lo, hi, r) in enumerate(sp_["rows"]):
                            last = act.activation(work[:, 1024 + b * 512 + lo:1024 + b * 512 + hi],
                                                  work[:, b * 512 + lo:b * 512 + hi], ACT.Exp,
                                                  bias=nmax[:, b, r:r + 1], accum_out=ssum[:, b, r:r + 1])
                        last.then_inc(exp_done, 1)
                    if i >= 3 and specs[i - 3]["last"]:
                        h = specs[i - 3]["out"]
                        o[h].filled(act)
                        dst = place(h)
                        copy(dst, PS[o[h].b][0:dst.shape[0], 0:T]).then_inc(o[h].bank.free, 1)

            def feed_forward(f, L):
                def silu(job, n, i=None):
                    job.filled(act, i)
                    act.wait_ge(hid_done, 11 * f + n + 1 if i is None else i * 4 + (11 * f + n + 1))
                    act.activation(work[:, 2048 + (n % 2) * 512:2560 + (n % 2) * 512], PS[job.b][:, :],
                                   ACT.Silu).then_inc(job.bank.free, 1)

                with act.Fori(0, 2) as i:
                    for n in range(4):
                        silu(L["j"][2 * n], n, i)
                        ff_split(L, n + 1, L["j"][2 * n:2 * n + 2], i)
                for n in range(3):
                    silu(L["tj"][2 * n], 8 + n)
                    if n < 2:
                        ff_split(L, 9 + n, L["tj"][2 * n:2 * n + 2])

            def ff_split(L, n, before=(None, None), i=None):
                cg, cu, width, lo = ff_weights(L, n)
                for kind, c, job in zip("gu", (cg, cu), before):
                    if n == 4:
                        act.wait_ge(c.sem, i * c.stride + (c.value + c.stride))
                    else:
                        c.loaded(act, i)
                    if job is not None:
                        job.filled(act, i)
                    for q in range(2):
                        copy(ff_buffer(kind, q), w3(c, width)[:, 4 * q:4 * q + 4, lo:lo + T]).then_inc(ff_upper, 1)

            act.wait_ge(small_loaded, SMALL)
            act.activation(cs[:], vec[:, 0:24], ACT.Silu).then_inc(cs_ready, 1)
            for n in range(2):
                act.wait_ge(sin_arg, n + 1)
                if n == 0:
                    act.activation(sinT, work[:, 0:T], ACT.Sin).then_inc(sin_done, 1)
                else:
                    act.activation(cosT, work[:, T:2 * T], ACT.Sin, bias=C("half_pi"), scale=-1.0).then_inc(sin_done, 1)
            norm(0)
            project(sp_pair, 0, 15)
            head_root(sp_rope[0], HD)
            act.wait_ge(gate_raw, 2)
            act.activation(gates[:], gates[:], ACT.Sigmoid).then_inc(gates_ready, 1)
            sp_v[1].filled(act)
            sp_pair[7].emptied(act)
            for par in range(2):
                for g in range(2):
                    for half in range(2):
                        last = copy(*window(par, g, half, 1))
            last.then_inc(windows_ready, 1)
            hid_job.filled(act)
            act.activation(Hl[:, 1792:1912], PS[hid_job.b][:, 0:120], ACT.Silu).then_inc(hid_job.bank.free, 1)
            kvc_job.filled(act)
            copy(Hl[:, 1600:1630], PS[kvc_job.b][:, 0:30])
            copy(Hl[:, 1632:1760], PS[kvc_job.b][:, 64:192]).then_inc(kvc_job.bank.free, 1)
            act.wait_ge(cshift, 1)
            cexp_view = Hl[:, 1024:1536].rearrange("p (a n) -> p a n", a=16)[:, :, 0:NCMP]
            act.activation(cexp_view, cexp_view, ACT.Exp).then_inc(cexp, 1)
            ct_job.filled(act)
            copy(Hl[:, 512:1024], PS[ct_job.b][:, :]).then_inc(ct_job.bank.free, 1)
            units(sp_units, sparse_specs(), 0, heads_to, 0)
            ff_split(ffn[0], 0)
            norm(1)
            feed_forward(0, ffn[0])

            norm(2)
            project(df_pair, 8, 16)
            head_root(df_rope[0], HD)
            lam_job.filled(act)
            act.activation(lamt[:, 0:2], PS[lam_job.b][:, 0:2], ACT.Exp).then_inc(lam_job.bank.free, 1)
            units(df_units, diff_specs(), 24, lambda h: OT[:, h, :], 8)
            head_root(on_stat, P)
            ff_split(ffn[1], 0)
            norm(3)
            feed_forward(1, ffn[1])

            for qt in range(2):
                ml_pool[qt].filled(act)
                copy(scr[:, 2048 + qt * 512:2560 + qt * 512], PS[ml_pool[qt].b][:, :]).then_inc(ml_pool[qt].bank.free, 1)
            for n, dst in ((0, 0), (1, 512), (2, 1024)):
                job = ml_lat[n]
                job.filled(act)
                act.activation(work[:, dst:dst + 512], PS[job.b][:, :], ACT.Square).then_inc(proj_copied, 1)
                copy(scr[:, dst:dst + 512], PS[job.b][:, :]).then_inc(job.bank.free, 1)
            ml_kr.filled(act)
            copy(scr[0:96, 1536:2048], PS[ml_kr.b][0:96, :]).then_inc(ml_kr.bank.free, 1)
            for n, (lo, w) in enumerate(((1536, T), (1792, 512))):
                ml_stat[n].filled(act)
                root(work[:, lo:lo + w], PS[ml_stat[n].b][:, 0:w], 256, C("rms_eps")).then_inc(ml_stat[n].bank.free, 1)
            for n in range(2):
                ml_d[n].filled(act)
                copy(scr[:, 3072 + n * 512:3584 + n * 512], PS[ml_d[n].b][:, :]).then_inc(ml_d[n].bank.free, 1)
            for j in range(4):
                ml_q[j].filled(act)
                copy(Fl[0:96, j * 512:(j + 1) * 512], PS[ml_q[j].b][0:96, :]).then_inc(ml_q[j].bank.free, 1)
            for h in range(8):
                ml_k[h].filled(act)
                copy(Fl[0:HD, 2048 + h * 512:2560 + h * 512], PS[ml_k[h].b][0:HD, :]).then_inc(ml_k[h].bank.free, 1)
            for n in range(4):
                ml_v[n].filled(act)
                copy(V[:, n * 512:(n + 1) * 512], PS[ml_v[n].b][:, :]).then_inc(ml_v[n].bank.free, 1)
            units(ml_units, mla_specs(), 40, lambda h: heads_to(8 + h), 16)
            ff_split(ffn[2], 0)
            norm(4, "ln_eps")
            feed_forward(2, ffn[2])
            norm(5, "ln_eps")

            for n in range(3):
                act.wait_ge(sin_arg, 3 + n)
                act.activation(work[0:64, 0:T], work[0:64, T:2 * T], ACT.Sin).then_inc(sin_done, 1)
            for n in range(8):
                hy_k[n].filled(act)
                f, h, im = n // 4, n // 2 % 2, n % 2
                dst = (V if im else OTl)[:, f * 1024 + h * 512:f * 1024 + (h + 1) * 512]
                copy(dst, PS[hy_k[n].b][:, :]).then_inc(hy_k[n].bank.free, 1)
            for h in range(2):
                hy_n[h].filled(act)
                copy(scr[0:1, h * 512:(h + 1) * 512], PS[hy_n[h].b][0:1, :]).then_inc(hy_n[h].bank.free, 1)
            for j in range(12):
                hy_pair[j].filled(act)
                for m in range(2):
                    t = 2 * j + m
                    last = act.activation(F[:, t, :], PS[hy_pair[j].b][:, m * T:(m + 1) * T], ACT.Identity,
                                          bias=vc("conv_b", t), scale=vc("conv_w", 24 + t))
                last.then_inc(zconv, 1)
            for n in range(4):
                hy_t[n].filled(act)
                copy(Hl[:, n * 512:(n + 1) * 512], PS[hy_t[n].b][:, :]).then_inc(hy_t[n].bank.free, 1)
            for h in range(2):
                for n in range(4):
                    hy_vs[h][n].filled(act)
                    copy(spectrum(h)[n % 2][:, n // 2, :], PS[hy_vs[h][n].b][:, :]).then_inc(hy_vs[h][n].bank.free, 1)
            norm(6, "ln_eps")

            act.wait_ge(rt_ready, 1)
            act.activation(pw[:], pw[:], ACT.Exp).then_inc(rt_exp, 1)
            for n in range(4):
                zt_job[n].filled(act)
                copy(V[:, n * 512:(n + 1) * 512], PS[zt_job[n].b][:, :]).then_inc(zt_job[n].bank.free, 1)

            def experts(M):
                J_ = M["j"]


                def upper(kind, g, i):
                    c = M["c"][kind, g]
                    c.loaded(act, i)
                    if g >= 1:
                        J_[kind, g - 1].filled(act, i)
                    for q in range(2):
                        copy(weight_upper(kind, 4 * q, 4), w3(c)[:, 4 * q:4 * q + 4, :]).then_inc(M["upper"], 1)

                with act.Fori(0, NE // 2) as i:
                    upper("g", 0, i)
                    for e in range(2):
                        for q in range(2):
                            job = J_["gather", e, q]
                            job.filled(act, i)
                            copy(gathered_upper(e)[:, 4 * q:4 * q + 4, :].rearrange("p k n -> p (k n)"),
                                 PS[job.b][:, :]).then_inc(M["gathered"], 1)
                        job = J_["st", e]
                        job.filled(act, i)
                        copy(spread_sel(e), PS[job.b][:, 0:T]).then_inc(job.bank.free, 1)
                    upper("u", 0, i)
                    for g in range(15):
                        if g < 14:
                            J_["g", g].filled(act, i)
                            act.wait_ge(M["hid"], 14 * i + g - 1) if g >= 2 else None
                            act.activation(work[:, 2048 + (g % 2) * 512:2560 + (g % 2) * 512], PS[g % 2][:, :],
                                           ACT.Silu).then_inc(J_["g", g].bank.free, 1)
                        if g < 13:
                            upper("g", g + 1, i)
                            upper("u", g + 1, i)
                        if g >= 1:
                            J_["t", g - 1].filled(act, i)
                            copy(work[:, 1024 + ((g - 1) % 2) * 512:1536 + ((g - 1) % 2) * 512],
                                 PS[4][:, :]).then_inc(J_["t", g - 1].bank.free, 1)
                        if g in (8, 14):
                            e = 0 if g == 8 else 1
                            for h in range(2):
                                J_["y", e, h].filled(act, i)
                                copy(ye[:, h * 512:(h + 1) * 512], PS[5 + h][:, :]).then_inc(J_["y", e, h].bank.free, 1)

            experts(moe)
            act.wait_ge(flag_ready, 1)
            with act.If(act.value_load(flag[0:1, 0:1], min_val=0, max_val=1) > 0):
                experts(moe2)
            norm(7, "ln_eps")

        @block.vector
        def _(ve):
            turned = [0]
            step = Steps(ve, dve_step)

            def tell(signal, n=1):
                ve.tensor_copy(mx8[:, 0, 0:1], mx8[:, 0, 0:1]).then_inc(signal, n)

            def tt(dst, x, y, op):
                return ve.tensor_tensor(dst, x, y, op)

            def ts(dst, x, s1, op0, s2=None, op1=None):
                return ve.tensor_scalar(dst, x, s1, s2, op0, op1) if op1 is not None else ve.tensor_scalar(
                    dst, x, s1, None, op0)

            def stt(dst, x, s, y, op0, op1):
                return ve.scalar_tensor_tensor(out=dst, in0=x, scalar=s, in1=y, op0=op0, op1=op1)

            def reduced(dst, src, out, rows=P):
                step(ts(dst, src, 1.0 / TWO_PI, ALU.mult, MAGIC, ALU.add))
                step(ts(dst, dst, -MAGIC, ALU.add))
                turns = spare[0:rows, :]
                step(ve.tensor_copy(turns, dst))
                step(stt(dst, turns, -PI_A, src, ALU.mult, ALU.add))
                step(stt(dst, turns, -PI_B, dst, ALU.mult, ALU.add))
                step(stt(dst, turns, -PI_C, dst, ALU.mult, ALU.add))
                ts(dst, dst, PI_CLAMP, ALU.min, -PI_CLAMP, ALU.max).then_inc(out, 1)

            def add_chunk(w, dst, cvec, counts, final, i=None):
                at, stride = counts
                for k in range(KT):
                    if k:
                        ve.wait_ge(ada_step, at + k if i is None else i * stride + (at + k))
                    ins = (ts(dst, w[:, k, :], cvec[:, k:k + 1], ALU.mult) if k == 0 else
                           stt(dst, w[:, k, :], cvec[:, k:k + 1], dst, ALU.mult, ALU.add))
                    ins.then_inc(ada_step if k < KT - 1 else final, 1)

            def add_shared(w, context, tokens, counts, i):
                at, stride = counts
                for n in range(2 * KT):
                    k, dst, o = n // 2, (context, tokens)[n % 2], (16, 8)[n % 2]
                    if k:
                        ve.wait_ge(ada_step, i * stride + (at + n - 1))
                    ins = (ts(dst, w[:, k, :], cs[:, o:o + 1], ALU.mult) if k == 0 else
                           stt(dst, w[:, k, :], cs[:, o + k:o + k + 1], dst, ALU.mult, ALU.add))
                    ins.then_inc(ada_step if n < 2 * KT - 1 else ada_used, 1)

            def take_mod(layer):
                job = mod_job[layer]
                job.filled(ve)
                b = vec[:, VEC["ada_b"][0] + 48 * layer:VEC["ada_b"][0] + 48 * (layer + 1)]
                if layer == 2:
                    step(tt(modc[:], PS[job.b][:, 64:80], b[:, 0:16], ALU.add))
                n = 48 if layer else 16
                tt(mod[:, layer, 0:n], PS[job.b][:, 0:n], b[:, 0:n], ALU.add).then_inc(job.bank.free, 1)
                job.emptied(ve)

            def scale_of(layer, sc, gain):
                step(stt(gsc[:], mod[:, layer, sc:sc + 8], 1.0, gain, ALU.add, ALU.mult))

            def rms(n, layer, sc, gain, sh, sq, take=None):
                tt(H[:], X[:], X[:], ALU.mult).then_inc(sq_ready, 1)
                if take is None:
                    scale_of(layer, sc, gain)
                norm_job[n][-1].emptied(ve)
                ve.wait_ge(sq_ready, sq)
                step(ve.reciprocal(rstd[:], rstd[:]))
                step(tt(H[:], X[:], rstd[:].unsqueeze(1).to_broadcast([P, KT, T]), ALU.mult))
                if take is not None:
                    take_mod(take)
                    scale_of(layer, sc, gain)
                for k in range(KT):
                    last = ts(H[:, k, :], H[:, k, :], gsc[:, k:k + 1], ALU.mult, mod[:, layer, sh + k:sh + k + 1], ALU.add)
                last.then_inc(h_ready, 1)

            def layer_norm(n, ln, sq):
                mean, var = norm_job[n]
                mean.filled(ve)
                stt(X[:], PS[mean.b][:, 0:T].unsqueeze(1).to_broadcast([P, KT, T]), -1.0 / D, X[:],
                    ALU.mult, ALU.add).then_inc(mean.bank.free, 1)
                mean.emptied(ve)
                tt(H[:], X[:], X[:], ALU.mult).then_inc(sq_ready, 1)
                var.emptied(ve)
                step(ve.reciprocal(rstd[:], rstd[:]))
                step(tt(X[:], X[:], rstd[:].unsqueeze(1).to_broadcast([P, KT, T]), ALU.mult))
                for k in range(KT):
                    o = ln * 8 + k
                    last = ts(X[:, k, :], X[:, k, :], vc("ln_g", o), ALU.mult, vc("ln_b", o), ALU.add)
                last.then_inc(x_ready, 1)

            def modulate(dst, src, m, sc, sh, signal, count):
                step(ts(gsc[:], m[:, sc:sc + 8], 1.0, ALU.add))
                for k in range(KT):
                    last = ts(dst[:, k, :], src[:, k, :], gsc[:, k:k + 1], ALU.mult, m[:, sh + k:sh + k + 1], ALU.add)
                last.then_inc(signal, 1)
                ve.wait_ge(signal, count)

            def residual(jobs, layer, g, signal):
                for j, job in enumerate(jobs):
                    job.filled(ve)
                    for m in range(2):
                        k = 2 * j + m
                        last = stt(X[:, k, :], PS[job.b][:, m * T:(m + 1) * T], mod[:, layer, g + k:g + k + 1],
                                   X[:, k, :], ALU.mult, ALU.add)
                    last.then_inc(job.bank.free, 1)
                jobs[-1].emptied(ve)
                if signal is not None:
                    tell(signal)

            def rope(rp, pairs, gains, base, tiles):
                stat, bc, ro = rp
                stat.emptied(ve)
                step(ve.reciprocal(rheads, rheads))
                tell(rh_ready)
                pairs[-1].emptied(ve)
                for j in range(9):
                    if j < 8:
                        bc[j].filled(ve)
                        for m in range(2):
                            t = 2 * j + m
                            if t < tiles:
                                last = stt(F[:, t, :], F[:, t, :], gains(t), PS[bc[j].b][:, m * T:(m + 1) * T],
                                           ALU.mult, ALU.mult)
                        last.then_inc(bc[j].bank.free, 1)
                    if j >= 1:
                        n = min(2, tiles - 2 * (j - 1))
                        turn(F[:, 2 * j - 2:2 * j - 2 + n, :], ro[j - 1], cosT, sinT, n, P)

            def turn(x, job, cos, sin, n, rows):
                t1 = work[0:rows, 2048:2048 + n * T].rearrange("p (a t) -> p a t", a=n)
                t2 = work[0:rows, 2560:2560 + n * T].rearrange("p (a t) -> p a t", a=n)
                job.filled(ve)
                if turned[0]:
                    ve.wait_ge(rope_done, turned[0])
                turned[0] += 1
                tt(t1, x, cos.unsqueeze(1).to_broadcast([rows, n, T]), ALU.mult)
                ps = PS[job.b][0:rows, 0:n * T].rearrange("p (a t) -> p a t", a=n)
                tt(t2, ps, sin.unsqueeze(1).to_broadcast([rows, n, T]), ALU.mult).then_inc(job.bank.free, 1)
                job.emptied(ve)
                tt(x, t1, t2, ALU.add).then_inc(rope_done, 1)

            def units(plan, specs, base):
                s, _, _ = plan
                for i in range(len(specs) + 1):
                    if i < len(specs):
                        sp_, b = specs[i], i % 2
                        w = sp_["width"]
                        dst = work[:, b * 512:b * 512 + w]
                        s[i].filled(ve)
                        if sp_["mask"] is not None:
                            stt(dst, PS[s[i].b][:, 0:w], sp_["scale"], sp_["mask"], ALU.mult, ALU.add).then_inc(s[i].bank.free, 1)
                        else:
                            ts(dst, PS[s[i].b][:, 0:w], sp_["scale"], ALU.mult).then_inc(s[i].bank.free, 1)
                        s[i].emptied(ve)
                        for lo, hi, r in sp_["rows"]:
                            last = ve.tensor_reduce(nmax[:, b, r:r + 1], work[:, b * 512 + lo:b * 512 + hi], AX.X,
                                                    ALU.max, negate=True)
                        last.then_inc(nmax_ready, 1)
                    if i >= 1:
                        u = i - 1
                        sp_, b = specs[u], u % 2
                        ve.wait_ge(exp_done, base + u + 1)
                        n = len(sp_["rows"])
                        step(ve.reciprocal(fac[:, b, 0:n], ssum[:, b, 0:n]))
                        if sp_["factor"] is not None:
                            step(tt(fac[:, b, 0:n], fac[:, b, 0:n], sp_["factor"], ALU.mult))
                        for lo, hi, r in sp_["rows"]:
                            x = work[:, 1024 + b * 512 + lo:1024 + b * 512 + hi]
                            last = ts(x, x, fac[:, b, r:r + 1], ALU.mult)
                        last.then_inc(p_ready, 1)

            def ff_lower_parts(f, L, n, kind, i=None):
                cg, cu, width, lo = ff_weights(L, n)
                for q in range(2):
                    w, rest = (part(cg if kind == "g" else cu, width)[:, 4 * q:4 * q + 4, lo:lo + T]
                               for part in (w3, w3r))
                    ve.wait_ge(ff_upper, ff_count(f, n, kind, q, i))
                    tt(rest, w, ff_buffer(kind, q).bitcast(F32), ALU.subtract).then_inc(ff_lower, 1)

            def feed_forward(f, L, layer):
                two = f == 1
                cvec = cs[:, 0:8] if f == 0 else cs[:, 8:16]
                s0 = 140 + f * 168 + (64 if f == 2 else 0)

                def product(n, job, dst, i=None):
                    job.filled(ve, i)
                    gate = L_gate[n]
                    gate.emptied(ve, i)
                    tt(work[:, dst:dst + 512], work[:, 2048 + (n % 2) * 512:2560 + (n % 2) * 512], PS[job.b][:, :],
                       ALU.mult).then_inc(job.bank.free, 1)
                    job.emptied(ve, i)
                    tell(hid_done)

                L_gate = {n: L["j"][2 * n] for n in range(4)} | {8 + n: L["tj"][2 * n] for n in range(3)}
                ve.wait_ge(h_ready, [2, 4, 6][f])
                ve.tensor_copy(Hupper, H[:]).then_inc(h_split, 1)
                ve.wait_ge(h_split, 2 * f + 1)
                tt(Hlower, H[:], Hupper.bitcast(F32), ALU.subtract).then_inc(h_split, 1)
                per = 7 * len(ADA_BODY) + (8 * 4 if two else 0)
                at = s0
                with ve.Fori(0, 2) as i:
                    for n in range(4):
                        ff_lower_parts(f, L, n + 1, "g", i)
                        product(n, L["j"][2 * n + 1], (n // 2) * 1024 + (n % 2) * 512, i)
                        ff_lower_parts(f, L, n + 1, "u", i)
                        for m, (pair, col, far, shared) in enumerate(ADA_BODY):
                            if pair != n:
                                continue
                            c = L["a"][m]
                            c.loaded(ve, i)
                            if shared and two:
                                add_shared(ada_half(c), OTl[:, bass.ds(i * far + col, T)],
                                           Fl[:, bass.ds(i * far + col, T)], (at, per), i)
                                at += 15
                                continue
                            add_chunk(ada_half(c), Fl[:, bass.ds(i * far + col, T)], cvec, (at, per), ada_used, i)
                            at += 7
                at += per
                for n in range(3):
                    if n < 2:
                        ff_lower_parts(f, L, 9 + n, "g")
                    product(8 + n, L["tj"][2 * n + 1], (n // 2) * 1024 + (n % 2) * 512)
                    if n < 2:
                        ff_lower_parts(f, L, 9 + n, "u")
                    for c, (pair, col) in zip(L["ta"], ADA_TAIL):
                        if pair == n:
                            c.loaded(ve)
                            add_chunk(ada_half(c), Fl[:, col:col + T], cvec, (at, 0), ada_used)
                            at += 7

            ve.memset(zero[:], 0.0).then_inc(zero_ready, 1)
            ve.memset(mx8[:], 0.0)
            for _ in range(2):
                ve.sem_inc(hid_done, 1)
            for b in banks2:
                ve.sem_inc(b.free, 1)
            ve.wait_ge(small_loaded, SMALL)
            step(ve.tensor_copy(rstd[:], posi))
            step(ts(rstd[:], rstd[:], C("invf"), ALU.mult))
            reduced(work[:, 0:T], rstd[:], sin_arg)
            ve.wait_ge(sin_arg, 1)
            stt(work[:, T:2 * T], work[:, 0:T], -1.0, work[:, 0:T], ALU.mult, ALU.max).then_inc(sin_arg, 1)
            tt(lamt[0:HD, 0:1], vc("lam", 0, HD), vc("lam", 1, HD), ALU.mult)
            tt(lamt[0:HD, 1:2], vc("lam", 2, HD), vc("lam", 3, HD), ALU.mult).then_inc(lam_prod, 1)
            step(ts(ogain[:], vc("out_norm"), 1.0 - LAM_INIT, ALU.mult))
            ve.wait_ge(cs_ready, 1)
            with ve.Fori(0, 2) as i:
                for n in range(2):
                    ada0[n].loaded(ve, i)
                    add_chunk(aring[:, ada0[n].slot, :].rearrange("p (k n) -> p k n", k=KT), Fl[:, bass.ds(i * 2 * CH + n * CH, CH)], cs[:, 0:8], (7 * n, 14), ada_used, i)

            take_mod(0)
            rms(0, 0, 8, vec[:, VEC["attn_norm"][0]:VEC["attn_norm"][0] + 8], 0, 1)
            for n, c in enumerate(ada1):
                c.loaded(ve)
                add_chunk(ada_half(c), scr[:, n * T:(n + 1) * T], cs[:, 0:8], (28 + 7 * n, 0), ada_used)
            ve.wait_ge(sin_done, 2)
            for qt in range(2):
                sp_tok[qt].filled(ve)
                ve.tensor_copy(V[:, qt * 1024 + 512:qt * 1024 + 768], PS[sp_tok[qt].b][:, 0:256])
                ve.tensor_copy(gates[:, qt, :], PS[sp_tok[qt].b][:, 256:280]).then_inc(sp_tok[qt].bank.free, 1)
            sp_tok[1].emptied(ve)
            tell(gate_raw, 2)
            for qt in range(2):
                sp_v[qt].filled(ve)
                ve.tensor_copy(V[:, qt * 1024:qt * 1024 + 512], PS[sp_v[qt].b][:, :]).then_inc(sp_v[qt].bank.free, 1)
            sp_gain = ["moba_q"] * 4 + ["moba_k"] * 4 + ["nsa_q"] * 4
            rope(sp_rope, sp_pair, lambda t: vc(sp_gain[t]) if t < 12 else vc("nsa_k", t - 12), 0, 15)
            ve.wait_ge(rope_done, 8)
            for par in range(2):
                for g in range(2):
                    for half in range(2):
                        last = ve.tensor_copy(*window(par, g, half, 0))
            step(last)
            ve.wait_ge(windows_ready, 1)
            for v in range(2):
                blk = Hl[:, 512 + 480 * v:992 + 480 * v].rearrange("p (l n) -> p l n", l=16)
                pos = vc("pos_v" if v else "pos_k", n=16).unsqueeze(2).to_broadcast([P, 16, 30])
                tt(blk, blk, pos, ALU.add).then_inc(blocks_ready, 1)
            for b in range(2):
                ve.tensor_copy(Hl[0:HD, b * T:(b + 1) * T], F[HD:P, 13 + b, :])
                last = ve.tensor_copy(Hl[HD:P, b * T:(b + 1) * T], F[0:HD, 13 + b, :])
            last.then_inc(ksw_ready, 1)
            hid_job.emptied(ve)
            rep = Hl[:, 512:1024].rearrange("p (e g j n) -> p e g j n", e=2, g=2, j=4)
            hid = Hl[:, 1792:1912].rearrange("p (v e g n) -> p v e g n", v=2, e=2, g=2)
            step(ve.memset(Hl[:, 512:1536], 0.0))
            for et in range(2):
                for g in range(2):
                    last = ve.tensor_copy(rep[:, et, g, :, 0:NCMP], hid[:, 1, et, g, :].unsqueeze(1).to_broadcast([P, 4, NCMP]))
            last.then_inc(hidrep_ready, 1)
            cs_job.filled(ve)
            pc5 = Hl[:, 1024:1536].rearrange("p (g t j n) -> p g t j n", g=2, t=2, j=4)
            ps5 = PS[cs_job.b][:, :].rearrange("p (g t j n) -> p g t j n", g=2, t=2, j=4)
            pc3 = Hl[:, 1024:1536].rearrange("p (a n) -> p a n", n=32)[:, :, 0:NCMP]

            def by_block(name, t):
                return C(name)[:, t * NCMP:(t + 1) * NCMP].unsqueeze(1).to_broadcast([P, 4, NCMP])

            for g in range(2):
                for t in range(2):
                    last = stt(pc5[:, g, t, :, 0:NCMP], ps5[:, g, t, :, 0:NCMP], HD ** -0.5, by_block("cmask", t), ALU.mult, ALU.add)
            last.then_inc(cs_job.bank.free, 1)
            cs_job.emptied(ve)
            step(ve.tensor_reduce(cst[:, 0, :], pc3, AX.X, ALU.max, negate=True))
            tt(pc3, pc3, cst[:, 0, :].unsqueeze(2).to_broadcast([P, 16, NCMP]), ALU.add).then_inc(cshift, 1)
            ve.wait_ge(cexp, 1)
            step(ve.tensor_reduce(cst[:, 0, :], pc3, AX.X, ALU.add))
            step(ve.reciprocal(cst[:, 0, :], cst[:, 0, :]))
            ve.wait_ge(gates_ready, 1)
            cst4 = cst[:, 0, :].rearrange("p (g t j) -> p g t j", g=2, t=2)
            gv = gates[:, :, 0:8].rearrange("p t (g j) -> p g t j", g=2)
            step(tt(cst4, cst4, gv, ALU.mult))
            step(tt(pc3, pc3, cst[:, 0, :].unsqueeze(2).to_broadcast([P, 16, NCMP]), ALU.mult))
            for g in range(2):
                for t in range(2):
                    last = tt(pc5[:, g, t, :, 0:NCMP], pc5[:, g, t, :, 0:NCMP], by_block("cvalid", t), ALU.mult)
            last.then_inc(cp_ready, 1)
            ct_job.filled(ve)
            step(ve.memset(Hl[:, 1024:1536], 0.0))
            vrows = Hl[:, 1024:1536].rearrange("p (g j d) -> p g j d", g=2, j=4)
            for jj in range(4):
                r = 32 * jj
                last = ve.tensor_copy(vrows[r:r + 32, :, jj, :],
                                      Hl[r:r + 32, 1632:1760].rearrange("p (g d) -> p g d", g=2))
            last.then_inc(vrows_ready, 1)
            mod_more.filled(ve)
            o = VEC["ada_b"][0]
            tt(mod[:, 0, 16:48], PS[mod_more.b][:, 0:32], vec[:, o + 16:o + 48], ALU.add).then_inc(mod_more.bank.free, 1)
            mod_more.emptied(ve)
            units(sp_units, sparse_specs(), 0)
            for kind in "gu":
                ff_lower_parts(0, ffn[0], 0, kind)
            residual(sp_y, 0, 16, None)
            rms(1, 0, 32, vec[:, VEC["ffn_norm"][0]:VEC["ffn_norm"][0] + 8], 24, 2)
            feed_forward(0, ffn[0], 0)
            residual(ffn[0]["y"], 0, 40, None)

            rms(2, 1, 8, vec[:, VEC["attn_norm"][0] + 8:VEC["attn_norm"][0] + 16], 0, 3, take=1)
            for n in range(4):
                df_v[n].filled(ve)
                o = (n % 2) * 1024 + (n // 2) * 512
                ve.tensor_copy(V[:, o:o + 512], PS[df_v[n].b][:, :]).then_inc(df_v[n].bank.free, 1)
            rope(df_rope, df_pair, lambda t: vc("diff_q" if t < 8 else "diff_k"), 8, 16)
            lam_job.emptied(ve)
            step(tt(lamt[:, 2:3], lamt[:, 1:2], lamt[:, 0:1], ALU.subtract))
            step(ts(lamt[:, 3:4], lamt[:, 2:3], -LAM_INIT, ALU.add))
            units(df_units, diff_specs(), 24)
            df_units[2][-1].emptied(ve)
            tt(H[:], OT[:], OT[:], ALU.mult).then_inc(sq_ready, 1)
            on_stat.emptied(ve)
            step(ve.reciprocal(rheads, rheads))
            tell(rh_ready)
            for j in range(4):
                on_bc[j].filled(ve)
                for m in range(2):
                    t = 2 * j + m
                    last = stt(OT[:, t, :], OT[:, t, :], ogain[:], PS[on_bc[j].b][:, m * T:(m + 1) * T], ALU.mult, ALU.mult)
                last.then_inc(on_bc[j].bank.free, 1)
            for kind in "gu":
                ff_lower_parts(1, ffn[1], 0, kind)
            residual(df_y, 1, 16, None)
            rms(3, 1, 32, vec[:, VEC["ffn_norm"][0] + 8:VEC["ffn_norm"][0] + 16], 24, 5)
            feed_forward(1, ffn[1], 1)
            residual(ffn[1]["y"], 1, 40, None)
            take_mod(2)

            modulate(H, X, mod[:, 2, :], 8, 0, h_ready, 5)
            ve.wait_ge(ctx_loaded, 16)
            modulate(F[:, 8:16, :], F[:, 16:24, :], modc[:], 8, 0, lat_ready, 1)
            step(ts(X[:], X[:], ALPHA, ALU.mult))
            ml_stat[1].emptied(ve)
            step(ve.reciprocal(work[:, 1536:2304], work[:, 1536:2304]))
            ml_lat[2].emptied(ve)
            for m in range(2):
                stt(scr[:, m * T:(m + 1) * T], scr[:, m * T:(m + 1) * T], vc("q_norm", m), work[:, 1536:1792], ALU.mult, ALU.mult)
                x = scr[:, 512 + m * 512:1024 + m * 512]
                last = stt(x, x, vc("kv_norm", m), work[:, 1792:2304], ALU.mult, ALU.mult)
            last.then_inc(lat_ready, 1)
            for n in range(2):
                ml_py[n].filled(ve)
                for m in range(2):
                    g = 2 * n + m
                    last = ts(OT[:, g, :], PS[ml_py[n].b][:, m * T:(m + 1) * T], vc("pool_scale", g), ALU.mult)
                last.then_inc(ml_py[n].bank.free, 1)
            mc = aring[:, ml_const.slot, :]
            ve.wait_ge(tables_loaded, ML_TABLE)
            for j in range(4):
                turn(F[0:96, 2 * j:2 * j + 2, :], ml_qr[j], mc[0:96, 2144:2400], mc[0:96, 2400:2656], 2, 96)
            turn(scr[0:96, 1792:2048].unsqueeze(1), ml_krr, mc[0:96, 2144:2400], mc[0:96, 2400:2656], 1, 96)
            ve.wait_ge(rope_done, 21)
            ve.tensor_copy(Fl[64:96, 2048:6144].rearrange("p (h t) -> p h t", h=8),
                           scr[64:96, 1536:2048].unsqueeze(1).to_broadcast([32, 8, 512])).then_inc(rope_done, 1)
            units(ml_units, mla_specs(), 40)
            for kind in "gu":
                ff_lower_parts(2, ffn[2], 0, kind)
            residual(ml_y, 2, 16, x_ready_raw)
            layer_norm(4, 0, 6)
            ve.wait_ge(x_ready, 1)
            modulate(H, X, mod[:, 2, :], 32, 24, h_ready, 6)
            step(ts(X[:], X[:], ALPHA, ALU.mult))
            feed_forward(2, ffn[2], 2)
            residual(ffn[2]["y"], 2, 40, x_ready_raw)
            layer_norm(5, 1, 7)
            take_mod(3)
            ve.wait_ge(x_ready, 2)

            modulate(H, X, mod[:, 3, :], 8, 0, h_ready, 7)
            step(ts(X[:], X[:], ALPHA, ALU.mult))
            for n in range(3):
                hy_sin[n].filled(ve)
                x = work[0:64, 2 * T:3 * T]
                ts(x, PS[hy_sin[n].b][0:64, 0:T], vc("fb", n, HD), ALU.add, vc("freq", 0, HD), ALU.mult).then_inc(
                    hy_sin[n].bank.free, 1)
                hy_sin[n].emptied(ve)
                reduced(work[0:64, T:2 * T], x, sin_arg, 64)
            hy_f[0].loaded(ve)
            dec = wring[:, hy_f[0].slot, :].rearrange("p (d t n) -> p d t n", d=2, t=2)
            for n in range(4):
                t, h = n // 2, n % 2
                o = t * 1024 + h * 512
                fwd, bwd = work[:, 1024:1536], work[:, 1536:2048]
                for d, dst in ((0, fwd), (1, bwd)):
                    hy_taps[n][d].filled(ve)
                    tt(dst, PS[hy_taps[n][d].b][:, :], dec[:, d, t, h * 512:(h + 1) * 512], ALU.mult).then_inc(
                        hy_taps[n][d].bank.free, 1)
                hy_taps[n][1].emptied(ve)
                tt(Fl[:, o:o + 512], fwd, bwd, ALU.add)
                step(tt(Fl[:, 2048 + o:2560 + o], fwd, bwd, ALU.subtract))
            tell(hy_ready)
            for j in range(12):
                ve.wait_ge(zconv, j + 1)
                hy_pair[j].filled(ve)
                for m in range(2):
                    t = 2 * j + m
                    z = PS[hy_pair[j].b][:, m * T:(m + 1) * T]
                    step(stt(F[:, t, 1:T], z[:, 0:T - 1], vc("conv_w", t), F[:, t, 1:T], ALU.mult, ALU.add))
                    last = stt(F[:, t, 0:T - 1], z[:, 1:T], vc("conv_w", 48 + t), F[:, t, 0:T - 1], ALU.mult, ALU.add)
                last.then_inc(hy_pair[j].bank.free, 1)
            hy_pair[11].emptied(ve)
            tt(F[:, 16:24, :], F[:, 16:24, :], F[:, 8:16, :], ALU.mult).then_inc(hy_ready, 1)
            KR = OTl.rearrange("p (f n) -> p f n", f=2)
            KI = V[:].rearrange("p (f n) -> p f n", f=2)
            t1, t2, t3 = (work[:, q * 1024:(q + 1) * 1024].rearrange("p (f n) -> p f n", f=2) for q in range(3))
            hy_n[1].emptied(ve)
            for h in range(2):
                hy_vs[h][3].emptied(ve)
                re, im = spectrum(h)
                kr, ki = KR[:, :, h * 512:(h + 1) * 512], KI[:, :, h * 512:(h + 1) * 512]
                tt(t1, re, kr, ALU.mult)
                tt(t2, im, ki, ALU.mult)
                step(tt(t3, re, ki, ALU.mult))
                step(tt(re, t1, t2, ALU.subtract))
                step(tt(t1, im, kr, ALU.mult))
                step(tt(t1[0:1, 0, :], im[0:1, 0, :], scr[0:1, h * 512:(h + 1) * 512], ALU.mult))
                tt(im, t1, t3, ALU.add).then_inc(spec_ready, 1)
                ve.wait_ge(spec_ready, h + 1)
            for h in range(2):
                for n in range(2):
                    job = hy_y[h][n]
                    job.filled(ve)
                    for m in range(2):
                        ct = 4 * h + 2 * n + m
                        last = stt(F[:, 16 + ct, :], F[:, 16 + ct, :], vc("skip", ct), PS[job.b][:, m * T:(m + 1) * T],
                                   ALU.mult, ALU.add)
                    last.then_inc(job.bank.free, 1)
            hy_y[1][1].emptied(ve)
            tt(F[:, 0:8, :], F[:, 0:8, :], F[:, 16:24, :], ALU.mult).then_inc(hy_ready, 1)
            residual(hy_yo, 3, 16, x_ready_raw)
            layer_norm(6, 2, 8)
            ve.wait_ge(x_ready, 3)
            modulate(H, X, mod[:, 3, :], 32, 24, h_ready, 8)
            step(ts(X[:], X[:], ALPHA, ALU.mult))

            rt_job.filled(ve)
            ve.tensor_copy(lg[:], PS[7][:, 0:16].rearrange("p (t e) -> p t e", t=2)).then_inc(rt_job.bank.free, 1)
            rt_job.emptied(ve)
            for t in range(2):
                step(ve.max(out=mx8[:, t, :], in_=lg[:, t, :]))
                last = ts(pw[:, t, :], lg[:, t, :], mx8[:, t, 0:1], ALU.subtract)
            last.then_inc(rt_ready, 1)
            big = cmp8[:, 0, :].rearrange("p (e j) -> p e j", e=8)
            same = cmp8[:, 1, :].rearrange("p (e j) -> p e j", e=8)
            for t in range(2):
                mine = lg[:, t, :].unsqueeze(2).to_broadcast([P, 8, 8])
                other = lg[:, t, :].unsqueeze(1).to_broadcast([P, 8, 8])
                tt(big, other, mine, ALU.is_gt)
                step(tt(same, other, mine, ALU.is_equal))
                step(tt(same, same, R("tie").rearrange("p (e j) -> p e j", e=8), ALU.mult))
                step(tt(big, big, same, ALU.add))
                step(ve.tensor_reduce(ch8[:, t, :], big, AX.X, ALU.add))
            ts(ch8[:], ch8[:], 1.5, ALU.is_lt).then_inc(route_ready, 1)
            ve.wait_ge(route_ready, 1)
            ve.wait_ge(rt_exp, 1)
            step(tt(pw[:], pw[:], ch8[:], ALU.mult))
            step(ve.tensor_reduce(psum8[:], pw[:], AX.X, ALU.add))
            step(ve.reciprocal(psum8[:], psum8[:]))
            step(tt(pw[:], pw[:], psum8[:].unsqueeze(2).to_broadcast([P, 2, 8]), ALU.mult))
            pos_job.filled(ve)
            step(stt(posm[:], PS[7][:, 0:16].rearrange("p (t e) -> p t e", t=2), 1.0, ch8[:], ALU.add, ALU.mult))
            step(ts(posm[:], posm[:], -1.0, ALU.add))
            ve.tensor_reduce(over[:], PS[7][:, 16:24], AX.X, ALU.max).then_inc(pos_job.bank.free, 1)
            pos_job.emptied(ve)
            ts(flag[:], over[:], SLOTS + 0.5, ALU.is_gt).then_inc(flag_ready, 1)
            step(ve.memset(yacc, 0.0))

            def experts(M):
                J_ = M["j"]
                with ve.Fori(0, NE // 2) as i:
                    for e in range(2):
                        for t in range(2):
                            last = ts(sel(e)[:, t, :], R("slot"), posm[:, t, bass.ds(2 * i + e, 1)], ALU.is_equal)
                        last.then_inc(M["sel"], 1)
                        ve.wait_ge(M["sel"], 2 * i + e + 1)
                        for t in range(2):
                            last = ts(wsel(e)[:, t, :], sel(e)[:, t, :], pw[:, t, bass.ds(2 * i + e, 1)], ALU.mult)
                        last.then_inc(M["wsel"], 1)

                    def lower(kind, g):
                        for q in range(2):
                            w, rest = (f(M["c"][kind, g])[:, 4 * q:4 * q + 4, :] for f in (w3, w3r))
                            ve.wait_ge(M["upper"], part_count(i, g, kind, q))
                            tt(rest, w, weight_upper(kind, 4 * q, 4).bitcast(F32), ALU.subtract).then_inc(M["lower"], 1)

                    lower("g", 0)
                    for e in range(2):
                        for q in range(2):
                            job = J_["gather", e, q]
                            ve.wait_ge(M["gathered"], 4 * i + 2 * e + q + 1)
                            tt(gathered_lower(e)[:, 4 * q:4 * q + 4, :].rearrange("p k n -> p (k n)"), PS[job.b][:, :],
                               gathered_upper(e)[:, 4 * q:4 * q + 4, :].bitcast(F32).rearrange("p k n -> p (k n)"),
                               ALU.subtract).then_inc(job.bank.free, 1)
                    lower("u", 0)

                    def scatter(e, q):
                        job = J_["s", e, q]
                        job.filled(ve, i)
                        x = yacc[:, 2 * q:2 * q + 2, :]
                        tt(x, x, PS[7][:, :].rearrange("p (a t) -> p a t", a=2), ALU.add).then_inc(job.bank.free, 1)

                    for g in range(14):
                        if g < 13:
                            lower("g", g + 1)
                        J_["u", g].filled(ve, i)
                        J_["g", g].emptied(ve, i)
                        tt(work[:, (g % 2) * 512:(g % 2) * 512 + 512], work[:, 2048 + (g % 2) * 512:2560 + (g % 2) * 512],
                           PS[2 + g % 2][:, :], ALU.mult).then_inc(J_["u", g].bank.free, 1)
                        J_["u", g].emptied(ve, i)
                        tell(M["hid"])
                        if g < 13:
                            lower("u", g + 1)
                        if g >= 10:
                            scatter(0, g - 10)
                    for q in range(4):
                        scatter(1, q)
                    J_["s", 1, 3].emptied(ve, i)

            experts(moe)
            with ve.If(ve.value_load(flag[0:1, 0:1], min_val=0, max_val=1) > 0):
                ts(posm[:], posm[:], -float(SLOTS), ALU.add).then_inc(over_done, 1)
                ve.wait_ge(over_done, 1)
                experts(moe2)
            for k in range(KT):
                last = stt(X[:, k, :], yacc[:, k, :], mod[:, 3, 40 + k:41 + k], X[:, k, :], ALU.mult, ALU.add)
            last.then_inc(x_ready_raw, 1)
            layer_norm(7, 3, 9)


_WEIGHTS = ["ada_w", "ffn_w_gate", "ffn_w_up", "ffn_w_down", "sp_w_in", "sp_w_out", "nsa_cmp_w1", "nsa_cmp_w2",
            "diff_w_in", "diff_w_out", "ada_w_2", "mix_in_w_2", "pool_w_2", "q_up_2", "kv_up_2", "mix_out_w_2",
            "ffn_gate_2", "ffn_up_2", "ffn_down_2", "hy_in_w_2", "hy_fw1_2", "hy_fw2_2", "hy_fw3_2", "hy_fout_2",
            "hy_out_w_2", "router_w_2", "moe_gate_2", "moe_up_2", "moe_down_2"]


def kernel(**inputs):
    import concourse.bacc as bacc
    from concourse.bass_utils import run_bass_kernel_spmd as run

    x = {k: np.asarray(v) for k, v in inputs.items()}

    def columns(v):
        return np.ascontiguousarray(v).reshape(-1, P).T

    def twice(v):
        v = np.ascontiguousarray(v).reshape(-1, 64).T
        return np.concatenate([v, v], 0)

    def upper(v):
        v = np.ascontiguousarray(v).reshape(-1, 64).T
        return np.concatenate([v, np.zeros_like(v)], 0)

    def feature_major(v):
        return np.ascontiguousarray(v.reshape(T, KT, P).transpose(2, 1, 0))

    vec = np.concatenate([
        columns(x["c"]), columns(x["c_2"]), columns(x["c_ctx_2"]), columns(x["attn_norm"]), columns(x["ffn_norm"]),
        columns(x["ada_b"]), columns(x["ada_b_2"]), columns(x["ln_g_2"]), columns(x["ln_b_2"]),
        columns(x["pool_scale_2"]), columns(x["q_norm_2"]), columns(x["kv_norm_2"]), columns(x["hy_conv_w_2"]),
        columns(x["hy_conv_b_2"]), columns(x["hy_skip_2"]), twice(x["moba_q_norm"]), twice(x["moba_k_norm"]),
        twice(x["nsa_q_norm"]), twice(x["nsa_k_norm"]), twice(x["diff_q_norm"]), twice(x["diff_k_norm"]),
        columns(x["diff_out_norm"]), upper(x["diff_lambda"]), upper(x["hy_fb1_2"]), upper(x["hy_fb2_2"]),
        upper(x["hy_fb3_2"]), upper(x["hy_freq_2"]), columns(x["nsa_cmp_pos"])], 1)
    con, mlac, hyc, routing, spread, decay = shape_constants()
    arrays = {"vec": np.ascontiguousarray(vec), "con": con, "mlac": mlac, "hyc": hyc, "routing": routing, "spread": spread, "decay": decay,
              "positions": x["positions"], "x": feature_major(x["x"]), "ctx_2": feature_major(x["ctx_2"])}
    arrays |= {n: np.ascontiguousarray(x[n]) for n in _WEIGHTS}

    nc = bacc.Bacc("TRN2", target_bir_lowering=False, num_devices=1)
    args = {n: nc.dram_tensor(f"in_{n}", v.shape, mybir.dt.from_np(v.dtype), kind="ExternalInput").ap()
            for n, v in arrays.items()}
    out = nc.dram_tensor("out", (P, KT, T), F32, kind="ExternalOutput").ap()
    build(nc, args, out)
    got = run(nc, [{f"in_{n}": v for n, v in arrays.items()}], core_ids=[0]).results[0]["out"]
    return np.ascontiguousarray(got.transpose(2, 1, 0)).reshape(1, T, D)
```
